# Optimizing a Trainium2 kernel written in Bass

```python
import math
import jax, jax.numpy as jnp
from jax import lax
import numpy as np

D_MODEL = 1024
BATCH = 1
SEQ = 512
DEPTH = 1

N_MEM = 256
EPS = 1e-6
GLA_HEADS = 4
GLA_DK = D_MODEL // (2 * GLA_HEADS)
GLA_DV = D_MODEL // GLA_HEADS
GLA_RANK = 16
GLA_GATE_NORM = 16.0
GLA_CHUNK = 64
DSA_HEADS = 8
DSA_KV_HEADS = 2
DSA_HD = D_MODEL // DSA_HEADS
IDX_HEADS = 8
IDX_DIM = 64
TOPK_MAX = 256
Q_BLOCK = 128
REL_BUCKETS = 32
REL_MAX_DIST = 128
X_HEADS = 4
X_HD = D_MODEL // X_HEADS
N_BRANCH = 3

SPLIT_SIZES = (
    GLA_HEADS * GLA_DK,
    GLA_HEADS * GLA_DK,
    GLA_HEADS * GLA_DV,
    GLA_RANK,
    GLA_HEADS * GLA_DV,
    DSA_HEADS * DSA_HD,
    DSA_KV_HEADS * DSA_HD,
    DSA_KV_HEADS * DSA_HD,
    IDX_HEADS * IDX_DIM,
    IDX_DIM,
    IDX_HEADS,
    DSA_HEADS * DSA_HD,
    X_HEADS * X_HD,
    X_HEADS * X_HD,
    N_BRANCH * D_MODEL,
)
W_IN_COLS = 11352


def rmsnorm(x, g):
    xf = x.astype(jnp.float32)
    y = xf * lax.rsqrt(jnp.mean(xf * xf, axis=-1, keepdims=True) + EPS)
    return (y * g.astype(jnp.float32)).astype(x.dtype)

def split_cols(u):
    offsets = np.cumsum(np.array(SPLIT_SIZES))[:-1].tolist()
    return jnp.split(u, offsets, axis=-1)

def t5_bucket(dist):
    max_exact = REL_BUCKETS // 2
    d = jnp.maximum(dist, 1).astype(jnp.float32)
    large = max_exact + (jnp.log(d / max_exact) / math.log(REL_MAX_DIST / max_exact)
                         * (REL_BUCKETS - max_exact)).astype(jnp.int32)
    large = jnp.minimum(large, REL_BUCKETS - 1)
    return jnp.where(dist < max_exact, dist, large)

def gla_mixer(q, k, v, a_low, z, w_a_up, b_a, g_head):
    B, L, _ = q.shape
    H, dk, dv, C = GLA_HEADS, GLA_DK, GLA_DV, GLA_CHUNK
    nc = L // C
    q = q.reshape(B, nc, C, H, dk) * (dk ** -0.5)
    k = k.reshape(B, nc, C, H, dk)
    v = v.reshape(B, nc, C, H, dv)
    log_a = jax.nn.log_sigmoid((a_low @ w_a_up + b_a).astype(jnp.float32)) / GLA_GATE_NORM
    b = jnp.cumsum(log_a.reshape(B, nc, C, H, dk), axis=2)
    b_last = b[:, :, -1:]
    q_d = q * jnp.exp(b).astype(q.dtype)
    k_d = k * jnp.exp(-b).astype(k.dtype)
    k_t = k * jnp.exp(b_last - b).astype(k.dtype)
    decay = jnp.exp(b_last[:, :, 0]).astype(q.dtype)
    causal = jnp.tril(jnp.ones((C, C), dtype=bool))
    att = jnp.einsum('bnthd,bnshd->bnhts', q_d, k_d)
    att = jnp.where(causal, att, jnp.zeros_like(att))
    o_intra = jnp.einsum('bnhts,bnshv->bnthv', att, v)

    def step(state, inp):
        qc, kc, vc, dc = inp
        o = jnp.einsum('bthd,bhdv->bthv', qc, state)
        state = dc[..., None] * state + jnp.einsum('bthd,bthv->bhdv', kc, vc)
        return state, o

    s0 = jnp.zeros((B, H, dk, dv), q.dtype)
    xs = (q_d.transpose(1, 0, 2, 3, 4), k_t.transpose(1, 0, 2, 3, 4),
          v.transpose(1, 0, 2, 3, 4), decay.transpose(1, 0, 2, 3))
    _, o_inter = lax.scan(step, s0, xs)
    o = o_intra + o_inter.transpose(1, 0, 2, 3, 4)
    o = rmsnorm(o.reshape(B, L, H, dv), g_head)
    return o.reshape(B, L, H * dv) * jax.nn.silu(z)

def dsa_mixer(q, k, v, iq, ik, iw, z, rel_bias):
    B, L, _ = q.shape
    topk = min(TOPK_MAX, L // 4)
    nb = L // Q_BLOCK
    KV = DSA_KV_HEADS
    G = DSA_HEADS // KV
    q = q.reshape(B, nb, Q_BLOCK, KV, G, DSA_HD) * (DSA_HD ** -0.5)
    k = k.reshape(B, L, KV, DSA_HD)
    v = v.reshape(B, L, KV, DSA_HD)
    iq = iq.reshape(B, nb, Q_BLOCK, IDX_HEADS, IDX_DIM)
    iw = iw.reshape(B, nb, Q_BLOCK, IDX_HEADS) * (IDX_HEADS ** -0.5) * (IDX_DIM ** -0.5)
    ik_f = ik.astype(jnp.float32)
    key_pos = jnp.arange(L, dtype=jnp.int32)

    def block(inp):
        qb, iqb, iwb, start = inp
        q_pos = start + jnp.arange(Q_BLOCK, dtype=jnp.int32)
        s = jax.nn.relu(jnp.einsum('bqhd,bsd->bqhs', iqb.astype(jnp.float32), ik_f))
        score = jnp.einsum('bqhs,bqh->bqs', s, iwb.astype(jnp.float32))
        visible = key_pos[None, :] <= q_pos[:, None]
        score = jnp.where(visible[None], score, -jnp.inf)
        _, idx = lax.top_k(score, topk)
        valid = idx <= q_pos[None, :, None]
        k_sel = jax.vmap(lambda kb, ib: kb[ib])(k, idx)
        v_sel = jax.vmap(lambda vb, ib: vb[ib])(v, idx)
        logits = jnp.einsum('bqcgd,bqncd->bqcgn', qb, k_sel).astype(jnp.float32)
        bucket = t5_bucket(jnp.maximum(q_pos[None, :, None] - idx, 0))
        bias = rel_bias[bucket].reshape(B, Q_BLOCK, topk, KV, G).transpose(0, 1, 3, 4, 2)
        logits = logits + bias.astype(jnp.float32)
        logits = jnp.where(valid[:, :, None, None, :], logits, -1e30)
        p = jax.nn.softmax(logits, axis=-1).astype(v.dtype)
        o = jnp.einsum('bqcgn,bqncd->bqcgd', p, v_sel)
        return o.reshape(B, Q_BLOCK, DSA_HEADS * DSA_HD)

    starts = jnp.arange(nb, dtype=jnp.int32) * Q_BLOCK
    xs = (q.transpose(1, 0, 2, 3, 4, 5), iq.transpose(1, 0, 2, 3, 4),
          iw.transpose(1, 0, 2, 3), starts)
    o = lax.map(block, xs)
    o = o.transpose(1, 0, 2, 3).reshape(B, L, DSA_HEADS * DSA_HD)
    return o * jax.nn.silu(z)

def cross_mixer(q, z, mem_n, w_mem_kv):
    B, L, _ = q.shape
    M = mem_n.shape[1]
    mk, mv = jnp.split(mem_n @ w_mem_kv, 2, axis=-1)
    mk = mk.reshape(B, M, X_HEADS, X_HD)
    mv = mv.reshape(B, M, X_HEADS, X_HD)
    q = q.reshape(B, L, X_HEADS, X_HD) * (X_HD ** -0.5)
    logits = jnp.einsum('bthd,bmhd->bhtm', q, mk).astype(jnp.float32)
    p = jax.nn.softmax(logits, axis=-1).astype(mv.dtype)
    o = jnp.einsum('bhtm,bmhd->bthd', p, mv).reshape(B, L, X_HEADS * X_HD)
    return o * jax.nn.silu(z)

def first_inputs(seed: int = 0) -> dict:
    key = jax.random.key(seed)
    ks = jax.random.split(key, 16)
    D = D_MODEL

    def w(k, shape, fan_in):
        return jax.random.normal(k, shape, jnp.float32) * (fan_in ** -0.5)

    def gain(k, shape):
        return 1.0 + 0.05 * jax.random.normal(k, shape, jnp.float32)

    return {
        "x": jax.random.normal(ks[0], (BATCH, SEQ, D), jnp.float32),
        "mem": jax.random.normal(ks[1], (BATCH, N_MEM, D), jnp.float32),
        "g_pre": gain(ks[2], (DEPTH, D)),
        "g_post": gain(ks[3], (DEPTH, D)),
        "g_mem": gain(ks[4], (DEPTH, D)),
        "w_in": w(ks[5], (DEPTH, D, W_IN_COLS), D),
        "w_gla_a_up": w(ks[6], (DEPTH, GLA_RANK, GLA_HEADS * GLA_DK), GLA_RANK),
        "b_gla_a": 0.1 * jax.random.normal(ks[7], (DEPTH, GLA_HEADS * GLA_DK), jnp.float32),
        "g_gla": gain(ks[8], (DEPTH, GLA_DV)),
        "rel_bias": 0.5 * jax.random.normal(ks[9], (REL_BUCKETS, DSA_HEADS), jnp.float32),
        "w_mem_kv": w(ks[10], (DEPTH, D, 2 * X_HEADS * X_HD), D),
        "w_gla_out": w(ks[11], (DEPTH, GLA_HEADS * GLA_DV, D), GLA_HEADS * GLA_DV),
        "w_dsa_out": w(ks[12], (DEPTH, DSA_HEADS * DSA_HD, D), DSA_HEADS * DSA_HD),
        "w_x_out": w(ks[13], (DEPTH, X_HEADS * X_HD, D), X_HEADS * X_HD),
        "w_o": w(ks[14], (DEPTH, D, D), D),
    }

def first_block(x, mem, g_pre, g_post, g_mem, w_in, w_gla_a_up, b_gla_a, g_gla,
              rel_bias, w_mem_kv, w_gla_out, w_dsa_out, w_x_out, w_o):
    for i in range(DEPTH):
        h = rmsnorm(x, g_pre[i])
        (gq, gk, gv, ga, gz, dq, dk, dv, iq, ik, iw, dz, xq, xz, gates) = split_cols(h @ w_in[i])
        y_gla = gla_mixer(gq, gk, gv, ga, gz, w_gla_a_up[i], b_gla_a[i], g_gla[i])
        y_dsa = dsa_mixer(dq, dk, dv, iq, ik, iw, dz, rel_bias)
        y_mem = cross_mixer(xq, xz, rmsnorm(mem, g_mem[i]), w_mem_kv[i])
        s_gla, s_dsa, s_mem = jnp.split(jax.nn.sigmoid(gates), N_BRANCH, axis=-1)
        merged = (s_gla * (y_gla @ w_gla_out[i]) + s_dsa * (y_dsa @ w_dsa_out[i])
                  + s_mem * (y_mem @ w_x_out[i]))
        x = x + rmsnorm(merged @ w_o[i], g_post[i])
    return x


DEPTH_2 = 2

N_A_LAYERS = DEPTH_2 // 2
N_B_LAYERS = DEPTH_2 - N_A_LAYERS

HEAD_DIM = 64
ROPE_THETA = 10000.0

MLSTM_HEADS = 4
MLSTM_DV = (3 * D_MODEL // 4) // MLSTM_HEADS
MLSTM_DQK = MLSTM_DV // 2
MLSTM_QK_W = MLSTM_HEADS * MLSTM_DQK
MLSTM_V_W = MLSTM_HEADS * MLSTM_DV
MLSTM_CHUNK = 64
GATE_SOFTCAP = 15.0
M_INIT = -1e30

SWA_Q_HEADS = (3 * D_MODEL // 4) // HEAD_DIM
SWA_KV_HEADS = 4
SWA_Q_W = SWA_Q_HEADS * HEAD_DIM
SWA_KV_W = SWA_KV_HEADS * HEAD_DIM
SWA_WINDOW = 128

MEM_TOKENS = 256
MEM_HEADS = 4
MEM_HEAD_DIM = (D_MODEL // 4) // MEM_HEADS
MEM_W = MEM_HEADS * MEM_HEAD_DIM

A_IN_W = 2 * MLSTM_QK_W + 2 * MLSTM_V_W + 2 * MLSTM_HEADS + MEM_W
B_IN_W = SWA_Q_W + MEM_W
MIX_W = MLSTM_V_W + MEM_W

D_FF = ((8 * D_MODEL // 3 + 255) // 256) * 256


def rmsnorm_2(x, g):
    xf = x.astype(jnp.float32)
    y = xf * lax.rsqrt(jnp.mean(xf * xf, axis=-1, keepdims=True) + EPS)
    return (y * g.astype(jnp.float32)).astype(x.dtype)

def rope_tables(positions):
    inv = 1.0 / (ROPE_THETA ** (jnp.arange(0, HEAD_DIM, 2, dtype=jnp.float32) / HEAD_DIM))
    ang = positions.astype(jnp.float32)[..., None] * inv
    return jnp.cos(ang), jnp.sin(ang)

def apply_rope(t, cos, sin):
    t1, t2 = jnp.split(t.astype(jnp.float32), 2, axis=-1)
    c = cos[:, :, None, :]
    s = sin[:, :, None, :]
    return jnp.concatenate([t1 * c - t2 * s, t2 * c + t1 * s], axis=-1).astype(t.dtype)

def mlstm_chunkwise(q, k, v, i_pre, f_pre):
    f32 = jnp.float32
    B_, S_, H, dqk = q.shape
    L = MLSTM_CHUNK
    NC = S_ // L

    def chunks(t):
        return t.astype(f32).reshape(B_, NC, L, H, -1).transpose(0, 3, 1, 2, 4)

    qc = chunks(q)
    kc = chunks(k) * (dqk ** -0.5)
    vc = chunks(v)
    ig = i_pre.astype(f32).reshape(B_, NC, L, H).transpose(0, 3, 1, 2)
    logf = jax.nn.log_sigmoid(f_pre.astype(f32)).reshape(B_, NC, L, H).transpose(0, 3, 1, 2)
    b = jnp.cumsum(logf, axis=-1)
    g = b[..., -1]
    a = g[..., None] - b + ig

    def step(carry, inp):
        C, n, m = carry
        g_c, a_c, k_c, v_c = inp
        m_new = jnp.maximum(g_c + m, jnp.max(a_c, axis=-1))
        decay = jnp.exp(g_c + m - m_new)
        w = jnp.exp(a_c - m_new[..., None])
        C_new = decay[..., None, None] * C + jnp.einsum('bhl,bhlv,bhlk->bhvk', w, v_c, k_c)
        n_new = decay[..., None] * n + jnp.einsum('bhl,bhlk->bhk', w, k_c)
        return (C_new, n_new, m_new), (C, n, m)

    dv = v.shape[-1]
    init = (jnp.zeros((B_, H, dv, dqk), f32), jnp.zeros((B_, H, dqk), f32), jnp.full((B_, H), M_INIT, f32))
    xs = (g.transpose(2, 0, 1), a.transpose(2, 0, 1, 3), kc.transpose(2, 0, 1, 3, 4), vc.transpose(2, 0, 1, 3, 4))
    _, (C_st, n_st, m_st) = lax.scan(step, init, xs)
    C_st = C_st.transpose(1, 2, 0, 3, 4)
    n_st = n_st.transpose(1, 2, 0, 3)
    m_st = m_st.transpose(1, 2, 0)

    causal = jnp.tril(jnp.ones((L, L), dtype=bool))
    dmat = jnp.where(causal, b[..., :, None] - b[..., None, :] + ig[..., None, :], -jnp.inf)
    inter_log = b + m_st[..., None]
    m_row = jnp.maximum(inter_log, jnp.max(dmat, axis=-1))
    scores = jnp.einsum('bhcjd,bhcsd->bhcjs', qc, kc) * jnp.exp(dmat - m_row[..., None])
    inter_w = jnp.exp(inter_log - m_row)
    num = (jnp.einsum('bhcjs,bhcsv->bhcjv', scores, vc)
           + inter_w[..., None] * jnp.einsum('bhcjk,bhcvk->bhcjv', qc, C_st))
    den = jnp.sum(scores, axis=-1) + inter_w * jnp.einsum('bhcjk,bhck->bhcj', qc, n_st)
    h = num / jnp.maximum(jnp.abs(den), jnp.exp(-m_row))[..., None]
    return h.transpose(0, 2, 3, 1, 4).reshape(B_, S_, H, dv)

def mlstm_mixer(h, w_in, b_gates, g_out):
    B_, S_, _ = h.shape
    p = h @ w_in
    q, k, v, o, gates, mq = jnp.split(
        p, [MLSTM_QK_W, 2 * MLSTM_QK_W, 2 * MLSTM_QK_W + MLSTM_V_W, 2 * MLSTM_QK_W + 2 * MLSTM_V_W,
            2 * MLSTM_QK_W + 2 * MLSTM_V_W + 2 * MLSTM_HEADS], axis=-1)
    gates = gates.astype(jnp.float32) + b_gates.astype(jnp.float32)
    gates = GATE_SOFTCAP * jnp.tanh(gates / GATE_SOFTCAP)
    i_pre, f_pre = jnp.split(gates, 2, axis=-1)
    hm = mlstm_chunkwise(q.reshape(B_, S_, MLSTM_HEADS, MLSTM_DQK), k.reshape(B_, S_, MLSTM_HEADS, MLSTM_DQK),
                         v.reshape(B_, S_, MLSTM_HEADS, MLSTM_DV), i_pre, f_pre)
    hm = hm * lax.rsqrt(jnp.mean(hm * hm, axis=-1, keepdims=True) + EPS)
    hm = hm * g_out.astype(jnp.float32).reshape(MLSTM_HEADS, MLSTM_DV)
    hm = jax.nn.sigmoid(o.astype(jnp.float32)) * hm.reshape(B_, S_, MLSTM_V_W)
    return hm.astype(h.dtype), mq.reshape(B_, S_, MEM_HEADS, MEM_HEAD_DIM)

def swa_sink_attention(q, k, v, sinks):
    B_, S_, Hq, dh = q.shape
    Hkv = k.shape[2]
    G = Hq // Hkv
    W = SWA_WINDOW
    NB = S_ // W
    qb = q.reshape(B_, NB, W, Hkv, G, dh)

    def band(t):
        tb = jnp.pad(t, ((0, 0), (W, 0), (0, 0), (0, 0))).reshape(B_, NB + 1, W, Hkv, dh)
        return jnp.concatenate([tb[:, :-1], tb[:, 1:]], axis=2)

    kband = band(k)
    vband = band(v)
    s = jnp.einsum('bnqhgd,bnkhd->bnhgqk', qb, kband).astype(jnp.float32) * (dh ** -0.5)
    qpos = jnp.arange(W)[:, None] + W
    kpos = jnp.arange(2 * W)[None, :]
    diff = qpos - kpos
    in_band = (diff >= 0) & (diff < W)
    blk = jnp.arange(NB)[:, None, None]
    valid = in_band[None] & (blk * W + kpos[None] - W >= 0)
    s = jnp.where(valid[None, :, None, None, :, :], s, -jnp.inf)
    sink = sinks.astype(jnp.float32).reshape(Hkv, G)[None, None, :, :, None, None]
    m = jnp.maximum(jnp.max(s, axis=-1, keepdims=True), sink)
    p = jnp.exp(s - m)
    p = p / (jnp.sum(p, axis=-1, keepdims=True) + jnp.exp(sink - m))
    o = jnp.einsum('bnhgqk,bnkhd->bnqhgd', p.astype(v.dtype), vband)
    return o.reshape(B_, S_, Hq * dh)

def swa_mixer(h, w_in, sinks, k_sh, v_sh, cos, sin):
    B_, S_, _ = h.shape
    p = h @ w_in
    q, mq = jnp.split(p, [SWA_Q_W], axis=-1)
    q = apply_rope(q.reshape(B_, S_, SWA_Q_HEADS, HEAD_DIM), cos, sin)
    o = swa_sink_attention(q, k_sh, v_sh, sinks)
    return o, mq.reshape(B_, S_, MEM_HEADS, MEM_HEAD_DIM)

def memory_attention(mq, mk, mv):
    B_, S_, Hm, dh = mq.shape
    s = jnp.einsum('bqhd,bmhd->bhqm', mq, mk).astype(jnp.float32) * (dh ** -0.5)
    p = jax.nn.softmax(s, axis=-1)
    o = jnp.einsum('bhqm,bmhd->bqhd', p.astype(mv.dtype), mv)
    return o.reshape(B_, S_, Hm * dh)

def shared_kv(x, g_kv, w_kv, cos, sin):
    B_, S_, _ = x.shape
    kv = rmsnorm_2(x, g_kv) @ w_kv
    k, v = jnp.split(kv, 2, axis=-1)
    k = apply_rope(k.reshape(B_, S_, SWA_KV_HEADS, HEAD_DIM), cos, sin)
    return k, v.reshape(B_, S_, SWA_KV_HEADS, HEAD_DIM)

def swiglu(h, w_in, w_out):
    gate, up = jnp.split(h @ w_in, 2, axis=-1)
    return (jax.nn.silu(gate) * up) @ w_out

def second_inputs(seed: int = 0) -> dict:
    key = jax.random.key(seed)
    ks = jax.random.split(key, 24)
    f32 = jnp.float32

    def w(k, shape, fan_in):
        return jax.random.normal(k, shape, f32) * (fan_in ** -0.5)

    def gain(k, shape):
        return 1.0 + 0.05 * jax.random.normal(k, shape, f32)

    x = jax.random.normal(ks[0], (BATCH, SEQ, D_MODEL), f32)
    mem = jax.random.normal(ks[1], (BATCH, MEM_TOKENS, D_MODEL), f32)
    offset = jax.random.randint(ks[2], (BATCH,), 0, 1024, dtype=jnp.int32)
    positions = (offset[:, None] + jnp.arange(SEQ, dtype=jnp.int32)[None, :]).astype(jnp.int32)

    i_bias = 0.1 * jax.random.normal(ks[3], (N_A_LAYERS, MLSTM_HEADS), f32)
    f_bias = 3.0 + 3.0 * jax.random.uniform(ks[4], (N_A_LAYERS, MLSTM_HEADS), f32)
    return {
        "x": x,
        "mem": mem,
        "positions": positions,
        "g_mix_pre": gain(ks[5], (DEPTH_2, D_MODEL)),
        "g_mix_post": gain(ks[6], (DEPTH_2, D_MODEL)),
        "g_ffn_pre": gain(ks[7], (DEPTH_2, D_MODEL)),
        "g_ffn_post": gain(ks[8], (DEPTH_2, D_MODEL)),
        "g_mem": gain(ks[9], (DEPTH_2, D_MODEL)),
        "w_mem_kv": w(ks[10], (DEPTH_2, D_MODEL, 2 * MEM_W), D_MODEL),
        "w_out": w(ks[11], (DEPTH_2, MIX_W, D_MODEL), MIX_W),
        "w_ffn_in": w(ks[12], (DEPTH_2, D_MODEL, 2 * D_FF), D_MODEL),
        "w_ffn_out": w(ks[13], (DEPTH_2, D_FF, D_MODEL), D_FF),
        "w_in_a": w(ks[14], (N_A_LAYERS, D_MODEL, A_IN_W), D_MODEL),
        "b_gates_a": jnp.concatenate([i_bias, f_bias], axis=-1),
        "g_mlstm_out": gain(ks[15], (N_A_LAYERS, MLSTM_V_W)),
        "g_kv": gain(ks[16], (D_MODEL,)),
        "w_kv": w(ks[17], (D_MODEL, 2 * SWA_KV_W), D_MODEL),
        "w_in_b": w(ks[18], (N_B_LAYERS, D_MODEL, B_IN_W), D_MODEL),
        "sinks_b": 0.5 * jax.random.normal(ks[19], (N_B_LAYERS, SWA_Q_HEADS), f32),
    }

def second_block(x, mem, positions, g_mix_pre, g_mix_post, g_ffn_pre, g_ffn_post, g_mem, w_mem_kv, w_out,
              w_ffn_in, w_ffn_out, w_in_a, b_gates_a, g_mlstm_out, g_kv, w_kv, w_in_b, sinks_b):
    B_ = x.shape[0]
    cos, sin = rope_tables(positions)
    k_sh = None
    v_sh = None
    for l in range(DEPTH_2):
        h = rmsnorm_2(x, g_mix_pre[l])
        mk, mv = jnp.split(rmsnorm_2(mem, g_mem[l]) @ w_mem_kv[l], 2, axis=-1)
        mk = mk.reshape(B_, MEM_TOKENS, MEM_HEADS, MEM_HEAD_DIM)
        mv = mv.reshape(B_, MEM_TOKENS, MEM_HEADS, MEM_HEAD_DIM)
        if l < N_A_LAYERS:
            main, mq = mlstm_mixer(h, w_in_a[l], b_gates_a[l], g_mlstm_out[l])
        else:
            j = l - N_A_LAYERS
            main, mq = swa_mixer(h, w_in_b[j], sinks_b[j], k_sh, v_sh, cos, sin)
        mo = memory_attention(mq, mk, mv)
        mix = jnp.concatenate([main, mo], axis=-1) @ w_out[l]
        x = x + rmsnorm_2(mix, g_mix_post[l])
        x = x + rmsnorm_2(swiglu(rmsnorm_2(x, g_ffn_pre[l]), w_ffn_in[l], w_ffn_out[l]), g_ffn_post[l])
        if l == N_A_LAYERS - 1:
            k_sh, v_sh = shared_kv(x, g_kv, w_kv, cos, sin)
    return x


def setup_inputs(seed=0):
    out = dict(first_inputs(seed))
    for name, value in second_inputs(seed + 1).items():
        if name != "x":
            out[name + "_2"] = value
    return out


def reference(
    x, mem, g_pre, g_post, g_mem, w_in, w_gla_a_up, b_gla_a, g_gla, rel_bias, w_mem_kv,
    w_gla_out, w_dsa_out, w_x_out, w_o, mem_2, positions_2, g_mix_pre_2, g_mix_post_2,
    g_ffn_pre_2, g_ffn_post_2, g_mem_2, w_mem_kv_2, w_out_2, w_ffn_in_2, w_ffn_out_2, w_in_a_2,
    b_gates_a_2, g_mlstm_out_2, g_kv_2, w_kv_2, w_in_b_2, sinks_b_2,
):
    x = first_block(
        x, mem, g_pre, g_post, g_mem, w_in, w_gla_a_up, b_gla_a, g_gla, rel_bias, w_mem_kv,
        w_gla_out, w_dsa_out, w_x_out, w_o,
    )
    return second_block(
        x, mem_2, positions_2, g_mix_pre_2, g_mix_post_2, g_ffn_pre_2, g_ffn_post_2, g_mem_2,
        w_mem_kv_2, w_out_2, w_ffn_in_2, w_ffn_out_2, w_in_a_2, b_gates_a_2, g_mlstm_out_2,
        g_kv_2, w_kv_2, w_in_b_2, sinks_b_2,
    )


_drawn_inputs = setup_inputs


def setup_inputs(seed=0):
    import zlib

    import numpy as np

    out = dict(_drawn_inputs(seed))
    spreads = {}
    factors = {'g_mem': 5.444,
     'g_mem_2': 3.64,
     'sinks_b_2': 27.334,
     'b_gla_a': 3.147,
     'g_gla': 2.872,
     'g_mlstm_out_2': 3.06,
     'g_kv_2': 8.0}
    for name, (base, spread) in spreads.items():
        noise = np.random.default_rng([zlib.crc32(name.encode()), seed]).standard_normal(out[name].shape)
        drawn = base * np.exp(spread * noise) if base else spread * noise
        out[name] = __import__('jax').numpy.asarray(drawn.astype(out[name].dtype))
    for name, factor in factors.items():
        out[name] = (out[name] * factor).astype(out[name].dtype)
    return out
```

```python
import math
from contextlib import ExitStack

import numpy as np

import concourse.bass as bass
from concourse import mybir

F32 = mybir.dt.float32
F32R = mybir.dt.float32r
I32 = mybir.dt.int32
U32 = mybir.dt.uint32
ALU = mybir.AluOpType
ACT = mybir.ActivationFunctionType
AX = mybir.AxisListType

P = 128
D = 1024
T = 512
NT = T // P
KT = D // P
C = 256
M = 256
EPS = 1e-6
NEG = -1e30

GLA_H, GLA_DK, GLA_DV, GLA_RANK, GLA_NORM = 4, 128, 256, 16, 16.0
DSA_H, DSA_KV, DSA_HD = 8, 2, 128
IDX_H, IDX_D, TOPK = 8, 64, 128
BUCKETS, MAX_DIST = 32, 128
X_H, X_HD = 4, 256
ML_H, ML_DK, ML_DV = 4, 96, 192
SOFTCAP = 15.0
SW_H, SW_KV, SW_HD = 12, 4, 64
MEM_H, MEM_HD = 4, 64
FF = 2816
FFT = FF // P

TAKEN = -3.4e38
HIDDEN = -3.3e38

O_GQ, O_GK, O_GV, O_GA, O_GZ = 0, 512, 1024, 2048, 2064
O_DQ, O_DK, O_DV, O_IQ, O_IK, O_IW, O_DZ = 3088, 4112, 4368, 4624, 5136, 5200, 5208
O_XQ, O_XZ, O_GATES = 6232, 7256, 8280

K_ID, K_U64, K_U128, K_ONE, K_SWA, K_DCM, K_LCM, K_HOT, K_INV, K_EPS = (
    0, 128, 256, 384, 512, 768, 896, 1024, 1408, 1440)
K_ALL = 1441

V_PRE, V_MEM, V_GLA, V_MIX0, V_FFN0, V_KV, V_MIX1, V_FFN1, V_MEM0, V_MEM1 = (
    0, 8, 16, 18, 26, 34, 42, 50, 58, 66)
V_RB31, V_BG, V_SINK = 74, 82, 90
V_ALL = 102
V_COLS = V_ALL + DSA_H

LINE = 512
LINE_HEAD = (LINE + 1) * P

TURN = (6.28125, 0.0019350051879882812, 3.0199159795074593e-07)
PI_IN = 3.1415925


def swa_columns():
    order = []
    for block in range(SW_H // 2):
        for half in range(2):
            order.append(6 * (block // 3) + 3 * half + block % 3)
    return order


SWA_ORDER = swa_columns()


def slots():
    out = []

    def full(w, col, r0=0, rt=KT, n=C):
        out.append([(w, r0, rt, col, n, 0)])

    def run(w, col, n, **k):
        for c in range(0, n, C):
            full(w, col + c, **k)

    out.append([("w_in", 0, KT, O_IK, 64, 0), ("w_in", 0, KT, O_IK, 64, 64),
                ("w_in", 0, KT, O_GA, 16, 128), ("w_in", 0, KT, O_IW, 8, 144)])
    run("w_in", O_GQ, 512)
    run("w_in", O_GK, 512)
    run("w_in", O_GV, 1024)
    run("w_in", O_GZ, 1024)
    for c in range(4):
        full("w_in", O_GATES + C * c)
        full("w_gla_out", C * c)
    run("w_in", O_DQ, 1024)
    run("w_in", O_DK, 256)
    run("w_in", O_DV, 256)
    run("w_in", O_IQ, 512)
    run("w_in", O_DZ, 1024)
    for c in range(4):
        full("w_in", O_GATES + D + C * c)
        full("w_dsa_out", C * c)
    run("w_mem_kv", 0, 2048)
    run("w_in", O_XQ, 1024)
    run("w_in", O_XZ, 1024)
    for c in range(4):
        full("w_in", O_GATES + 2 * D + C * c)
        full("w_x_out", C * c)
    run("w_o", 0, 1024)
    for layer in range(2):
        if layer == 0:
            for c in range(8):
                full("w_in_a", 192 * c, n=192)
            run("w_in_a", 1536, 768)
            full("w_in_a", 2304, n=8)
            full("w_in_a", 2312)
        else:
            full("w_kv", 0)
            full("w_kv", 256)
            for c in range(3):
                out.append([("w_in_b", 0, KT, 64 * SWA_ORDER[4 * c + i], 64, 64 * i) for i in range(4)])
            full("w_in_b", 768)
        for c in range(2):
            full(f"w_mem_kv_{layer}", C * c)
        run(f"w_out_{layer}", 0, 1024)
        for c in range(FF // C):
            full(f"w_ffn_in_{layer}", C * c)
            full(f"w_ffn_in_{layer}", FF + C * c)
        for c in range(4):
            for r in range(0, FFT, KT):
                full(f"w_ffn_out_{layer}", C * c, r0=r, rt=min(KT, FFT - r))
    return out


NS = len(slots())


class Waits:

    def __init__(self, eng, chain):
        self.eng, self.chain, self.at, self.links = eng, chain, {}, 0

    def next(self, sem, by=1):
        self.at[sem.name] = self.at.get(sem.name, 0) + by
        self.eng.wait_ge(sem, self.at[sem.name])

    def link(self, instruction):
        self.links += 1
        instruction.then_inc(self.chain, 1)
        self.eng.wait_ge(self.chain, self.links)


def build(nc, stream, x_in, mem_in, mem2_in, consts, cols, gposts, wup, gmlb, pos_in, line, out):
    ctx = ExitStack()
    with ctx:
        def sb(name, shape, dt=F32):
            return ctx.enter_context(nc.sbuf_tensor(name, shape, dt))

        def region(name, kbytes):
            base = ctx.enter_context(ExitStack())

            def place(tensor, at, shape, dt=F32):
                with ExitStack() as inner:
                    if at:
                        inner.enter_context(nc.sbuf_tensor(f"before_{tensor}", [P, int(at * 256)], F32))
                    return inner.enter_context(nc.sbuf_tensor(tensor, shape, dt))

            def close():
                base.enter_context(nc.sbuf_tensor(name, [P, kbytes * 256], F32))
            return place, close

        raw = sb("raw", [P, 2, KT, C])
        whi = sb("whi", [P, 2, KT, C], F32R)
        wlo = sb("wlo", [P, 2, KT, C], F32R)
        X = sb("X", [P, NT, D])
        K = sb("K", [P, K_ALL])
        V = sb("V", [P, V_COLS])
        gpost = sb("gpost", [P, D])
        small = sb("small", [P, 512])

        place, close = region("H", 32)
        hhi = place("hhi", 0, [P, KT, T], F32R)
        hlo = place("hlo", 16, [P, KT, T], F32R)
        o_ffn = place("o_ffn", 0, [P, NT, D])
        hm = place("hm", 0, [P, NT, ML_H, ML_DV])
        xp2 = place("xp2", 16, [P, NT, M])
        xpt2 = place("xpt2", 20, [P, 2, T])
        mo = place("mo", 24, [P, 2, T])
        close()

        place, close = region("R", 99)
        yhi = place("yhi", 0, [P, KT, T], F32R)
        ylo = place("ylo", 16, [P, KT, T], F32R)
        merged = place("merged", 32, [P, KT, T])
        xn = place("xn", 64, [P, NT, D])
        o_mix = place("o_mix", 48, [P, NT, D])
        ztmp = place("ztmp", 48, [P, 2, T])
        gsig = place("gsig", 52, [P, 2, T])
        gprod = place("gprod", 56, [P, 2, T])
        ikT = place("ikT", 96, [P, T])
        gq = place("gq", 48, [P, GLA_H, T])
        gk = place("gk", 56, [P, GLA_H, T])
        gv = place("gv", 64, [P, NT, D])
        go = place("go", 80, [P, KT, T])
        spT = place("spT", 80, [P, T])
        la = place("la", 0, [P, NT, 512])
        gkt = place("gkt", 8, [P, GLA_H, T])
        S_t = place("S_t", 0, [P, 4, GLA_H, GLA_DV])
        gktok = place("gktok", 16, [P, NT, 512])
        attm = place("attm", 24, [P, GLA_H, P])
        lscr = place("lscr", 16, [P, NT, 512])
        gsq = place("gsq", 48, [P, KT, T])
        ge = place("ge", 26, [P, 3, T])
        wup_s = place("wup_s", 26, [GLA_RANK, 512])
        ba_s = place("ba_s", 28, [1, 512])
        dq = place("dq", 48, [P, DSA_H, T])
        dk = place("dk", 64, [P, DSA_KV, T])
        dv = place("dv", 68, [P, NT, C])
        iq = place("iq", 72, [P, 4, T])
        do = place("do", 80, [P, DSA_H, T])
        tbias = place("tbias", 0, [P, DSA_H, C])
        score = place("score", 8, [P, T])
        maskt = place("maskt", 10, [P, T])
        relu = place("relu", 12, [P, 4, T])
        pt = place("pt", 12, [P, 4, 4, P])
        lg = place("lg", 20, [P, 4, T])
        linet = place("linet", 28, [DSA_H, 384])
        xq = place("xq", 48, [P, 8, T])
        mk = place("mk", 64, [P, 8, M])
        mv = place("mv", 72, [P, 2, D])
        xo = place("xo", 80, [P, 8, T])
        memx = place("memx", 0, [P, 2, D])
        mhi = place("mhi", 8, [P, KT, M], F32R)
        mlo = place("mlo", 16, [P, KT, M], F32R)
        memn = place("memn", 24, [P, 2, D])
        xp = place("xp", 0, [P, NT, M])
        xpt = place("xpt", 4, [P, 2, T])
        mk2 = place("mk2", 77, [P, 2, M])
        mv2 = place("mv2", 79, [P, 2, M])
        lq = place("lq", 32, [P, ML_H, T])
        lk = place("lk", 40, [P, ML_H, T])
        lv = place("lv", 48, [P, NT, ML_H, ML_DV + 1])
        lo = place("lo", 61, [P, NT, 768])
        mq = place("mq", 73, [P, 2, T])
        gT = place("gT", 81, [P, T])
        lw = place("lw", 81, [P, T])
        Lb = place("Lb", 83, [P, ML_H, T])
        at = place("at", 16, [P, NT, T])
        ljunk = place("ljunk", 94, [P, ML_DV])
        gmb = place("gmb", 91, [P, 768])
        sk = place("sk", 32, [P, NT, C])
        sv = place("sv", 36, [P, NT, C])
        sq = place("sq", 40, [P, NT, 768])
        qrT = place("qrT", 40, [P, 6, T])
        mqb = place("mqb", 52, [P, 2, T])
        ra = place("ra", 56, [P, 768])
        rb = place("rb", 59, [P, 768])
        sqr = place("sqr", 62, [P, NT, 768])
        so = place("so", 62, [P, 6, T])
        skr = place("skr", 81, [P, NT, C])
        krT = place("krT", 85, [P, 2, T])
        slg = place("slg", 89, [P, NT, C])
        spt = place("spt", 93, [P, 7, P])
        cs = place("cs", 97, [P, 2, NT, 32])
        ahi = place("ahi", 0, [P, FFT, T], F32R)
        alo = place("alo", 44, [P, FFT, T], F32R)
        fa = place("fa", 88, [P, 2, T])
        fs = place("fs", 92, [P, 2, T])
        close()

        PS = ctx.enter_context(nc.psum_tensor("PS", [P, 8, 512], F32))

        def col(tensor, a, n=1):
            return tensor[:, a:a + n]

        ident = K[:, K_ID:K_ID + P]
        u64 = K[:, K_U64:K_U64 + P]
        u128 = K[:, K_U128:K_U128 + P]
        ones = K[:, K_ONE:K_ONE + P]
        swa = K[:, K_SWA:K_SWA + C]
        dcm = K[:, K_DCM:K_DCM + P]
        lcm = K[:, K_LCM:K_LCM + P]
        hot = K[0:BUCKETS, K_HOT:K_HOT + 384]
        inv = K[:, K_INV:K_INV + 32]
        relb_v = V[0:BUCKETS, V_ALL:V_COLS]
        epsc = K[:, K_EPS:K_EPS + 1]

        ss = small[:, 0:16]
        root = small[:, 16:32]
        rstd = small[:, 32:48]
        iwt = small[:, 48:80].rearrange("p (t h) -> p t h", t=NT)
        nmax = small[:, 80:84]
        psum_ = small[:, 84:88]
        prec = small[:, 88:92]
        top8 = small[:, 96:104]
        dec = small[:, 104:136].rearrange("p (h c) -> p h c", h=GLA_H)
        lgt = small[:, 136:168].rearrange("p (t g) -> p t g", t=NT)
        lex = small[:, 184:200].rearrange("p (t h) -> p t h", t=NT)
        lgf = small[:, 200:216].rearrange("p (t h) -> p t h", t=NT)
        bi = small[:, 216:280].rearrange("p (s j h) -> p s j h", s=4, j=4)
        rstd16 = small[:, 280:296]
        nsink = small[:, 296:308]
        esink = small[:, 308:312]
        posf = small[:, 312:316]
        posi = small[:, 316:320].bitcast(I32)
        lden = small[:, 320:324]
        blast = small[:, 324:332]

        S = {}

        def sem(name):
            S[name] = ctx.enter_context(nc.semaphore(name))
            return S[name]

        raw_ready = [sem(f"raw_ready{p}") for p in range(2)]
        hi_ready = [sem(f"hi_ready{p}") for p in range(2)]
        lo_ready = [sem(f"lo_ready{p}") for p in range(2)]
        slot_used = [sem(f"slot_used{p}") for p in range(2)]
        pair_free = [sem(f"pair_free{p}") for p in range(2)]
        for name in """x_loaded const_loaded gate_w_loaded gpost_loaded gpost_used gml_loaded
                out_stored norm_root xn_ready norm_turned hhi_ready hlo_ready act_chain dve_chain
                pool_chain z_silu z_prod y_hi y_lo g_sig merged_hi merged_ready
                special_ready iw_turned la_abs la_psum la_exp la_ready b_psum eb_ready ediff_ready ekt_ready
                gk_ready gkt_ready kt_turned kt_copied att_psum att_ready gla_upd S_ready
                go_psum go_copied sq_ready ssq_psum gla_root gla_rstd rs_psum go_ready
                store_act store_dve mem_loaded
                rel_loaded line_psum line_ready line_stored tbias_loaded idx_psum relu_ready relu_used
                score_ready score_masked dsa_mask lg_psum lg_ready p_exp p_norm p_turned pt_ready
                pv_psum o_copied o_sq o_root x_new
                gt_ready gt_turned gate_soft gate_abs gate_exp logf_ready cl_psum bi_ready lb_psum lb_ready
                lsc_psum lw_arg lw_exp at_ready num_psum hm_ready hm_sq hm_root hm_done hm_turned
                mem_first rope_arg rope_sin rope_done rope_turned rot_copied ffn_silu ffn_a ffn_hi ffn_lo
                ffo_full ffo_free sink_exp ones_ready final pos_loaded""".split():
            sem(name)

        block = ctx.enter_context(nc.Block())

        @block.tensor
        def _(pe):
            w = Waits(pe, S["pool_chain"])
            n = m = 0

            def three(out, k, n_k, lhs, rhs):
                (lh, ll), (rh, rl) = lhs, rhs
                nc.tensor.matmul(out, lh, rh, start=(k == 0), stop=False)
                nc.tensor.matmul(out, lh, rl, start=False, stop=False)
                return nc.tensor.matmul(out, ll, rh, start=False, stop=(k == n_k - 1))

            def slot_begin():
                pe.wait_ge(lo_ready[n % 2], n // 2 + 1)
                if m >= 2:
                    pe.wait_ge(pair_free[m % 2], m // 2)

            def gemm_features(hi, lo, groups=(0, P), tokens=T):
                nonlocal n, m
                slot_begin()
                p = n % 2
                for g, c in enumerate(groups):
                    for k in range(KT):
                        last = three(PS[:, 2 * (m % 2) + g, 0:tokens], k, KT,
                                     (whi[:, p, k, c:c + P], wlo[:, p, k, c:c + P]), (hi[:, k, :], lo[:, k, :]))
                last.then_inc(slot_used[p], 1)
                n, m = n + 1, m + 1

            def gemm_tokens(hi, lo, width=C, tiles=NT):
                nonlocal n, m
                slot_begin()
                p = n % 2
                for t in range(tiles):
                    out_ = PS[:, 2 * (m % 2) + t // 2, (t % 2) * C:(t % 2) * C + width]
                    for k in range(KT):
                        last = three(out_, k, KT, (hi[:, k, t * P:t * P + P], lo[:, k, t * P:t * P + P]),
                                     (whi[:, p, k, 0:width], wlo[:, p, k, 0:width]))
                last.then_inc(slot_used[p], 1)
                n, m = n + 1, m + 1

            def stored():
                for b in range(2):
                    pe.wait_ge(pair_free[b], (m + 1 - b) // 2)

            def turn_normed(src, tiles, again=False):
                for k in range(KT):
                    if k >= 4:
                        w.next(S["hlo_ready"])
                    for t in range(tiles):
                        if k == 0 and not again:
                            w.next(S["xn_ready"])
                        last = nc.tensor.transpose(PS[:, 4 + k % 4, t * P:t * P + P],
                                                   src[:, t, k * P:k * P + P], ident)
                    last.then_inc(S["norm_turned"], 1)
                w.next(S["hlo_ready"], 4)

            def memory_attention(heads, parts, values, cross):
                for h in range(heads):
                    if h:
                        w.next(S["o_copied"])
                    ps_ = parts(h)
                    for t in range(NT):
                        for i, (q_, k_, (rows, kt)) in enumerate(ps_):
                            last = nc.tensor.matmul(PS[:, 4 + t // 2, (t % 2) * C:(t % 2) * C + M],
                                                    q_[rows, kt, t * P:t * P + P], k_[rows, kt, :],
                                                    start=(i == 0), stop=(i == len(ps_) - 1))
                    last.then_inc(S["lg_psum"], 1)
                    w.next(S["p_norm"])
                    p_ = xp if cross else xp2
                    for j in range(2):
                        for t in range(NT):
                            last = nc.tensor.transpose(PS[:, 6 + j, t * P:t * P + P], p_[:, t, j * P:j * P + P], ident)
                    last.then_inc(S["p_turned"], 1)
                    w.next(S["pt_ready"])
                    pt_ = xpt if cross else xpt2
                    for v in range(2 if cross else 1):
                        for j in range(2):
                            if cross:
                                last = nc.tensor.matmul(PS[:, 4 + v, :], values[:, j, h * X_HD + v * P:h * X_HD + v * P + P],
                                                        pt_[:, j, :], start=(j == 0), stop=(j == 1))
                            else:
                                r = MEM_HD * (h % 2)
                                last = nc.tensor.matmul(PS[r:r + MEM_HD, 4, :], values[:, j, h * MEM_HD:h * MEM_HD + MEM_HD],
                                                        pt_[:, j, :], start=(j == 0), stop=(j == 1))
                    last.then_inc(S["pv_psum"], 1)
                w.next(S["o_copied"])

            def z_and_merge():
                for c in range(4):
                    gemm_features(hhi, hlo)
                w.next(S["y_lo"], 4)
                for c in range(4):
                    gemm_features(hhi, hlo)
                    gemm_features(yhi, ylo)

            pe.wait_ge(S["const_loaded"], 32)
            turn_normed(xn, NT)
            gemm_features(hhi, hlo)
            for c in range(4):
                gemm_features(hhi, hlo)
            for c in range(4):
                gemm_tokens(hhi, hlo)

            stored()
            for t in range(NT):
                last = nc.tensor.transpose(PS[:, 4, t * 32:t * 32 + 32], spT[0:32, t * P:t * P + P], ident[0:32, 0:32])
            last.then_inc(S["iw_turned"], 1)
            w.next(S["special_ready"])
            pe.wait_ge(S["gate_w_loaded"], 32)
            for t in range(NT):
                nc.tensor.matmul(PS[:, 4 + t, :], spT[0:GLA_RANK, t * P:t * P + P], wup_s[:, :], start=True, stop=False)
                last = nc.tensor.matmul(PS[:, 4 + t, :], ones[0:1, :], ba_s[:, :], start=False, stop=True)
            last.then_inc(S["la_psum"], 1)
            w.next(S["la_ready"])
            for h in range(GLA_H):
                for t in range(NT):
                    last = nc.tensor.matmul(PS[:, 4 + h, t * P:t * P + P], la[:, t, h * P:h * P + P], u64, start=True, stop=True)
                last.then_inc(S["b_psum"], 1)
            for h in range(GLA_H):
                w.next(S["gk_ready"])
                for t in range(NT):
                    last = nc.tensor.transpose(PS[:, 4 + h, t * P:t * P + P], gkt[:, h, t * P:t * P + P], ident)
                last.then_inc(S["kt_turned"], 1)
            w.next(S["kt_copied"], GLA_H)
            for t in range(NT):
                tk = slice(t * P, t * P + P)
                if t:
                    w.next(S["go_copied"])
                for h in range(GLA_H):
                    last = nc.tensor.matmul(PS[:, 4, h * P:h * P + P], gk[:, h, tk], gq[:, h, tk], start=True, stop=True)
                last.then_inc(S["att_psum"], 1)
                for j in range(2):
                    c = 2 * t + j
                    if c == 2 * NT - 1:
                        break
                    if c:
                        w.next(S["S_ready"])
                    r = slice(64 * j, 64 * j + 64)
                    for h in range(GLA_H):
                        last = nc.tensor.matmul(PS[:, 5 + h // 2, (h % 2) * C:(h % 2) * C + GLA_DV],
                                                gktok[r, t, h * P:h * P + P], gv[r, t, h * GLA_DV:(h + 1) * GLA_DV],
                                                start=True, stop=True)
                    last.then_inc(S["gla_upd"], 1)
                w.next(S["att_ready"])
                if t == NT - 1:
                    w.next(S["S_ready"])
                for h in range(GLA_H):
                    for v in range(2):
                        i = (h % 2) * 2 + v
                        vc = slice(h * GLA_DV + v * P, h * GLA_DV + v * P + P)
                        bank = 4 if h < 2 else 7
                        nc.tensor.matmul(PS[:, bank, i * P:i * P + P], gv[:, t, vc], attm[:, h, :], start=True, stop=False)
                        if t:
                            nc.tensor.matmul(PS[:, bank, i * P:i * P + 64], S_t[:, (2 * t) % 4, h, v * P:v * P + P],
                                             gq[:, h, t * P:t * P + 64], start=False, stop=False)
                        last = nc.tensor.matmul(PS[:, bank, i * P + 64:i * P + P], S_t[:, (2 * t + 1) % 4, h, v * P:v * P + P],
                                                gq[:, h, t * P + 64:t * P + P], start=False, stop=True)
                last.then_inc(S["go_psum"], 1)
            w.next(S["go_copied"])
            w.next(S["sq_ready"])
            for t in range(NT):
                for h in range(GLA_H):
                    for v in range(2):
                        last = nc.tensor.matmul(PS[:, 4, 4 * t + h:4 * t + h + 1], gsq[:, 2 * h + v, t * P:t * P + P],
                                                ones[:, 0:1], start=(v == 0), stop=(v == 1))
            last.then_inc(S["ssq_psum"], 1)
            w.next(S["gla_rstd"])
            for h in range(GLA_H):
                for t in range(NT):
                    last = nc.tensor.matmul(PS[:, 4 + h, t * P:t * P + P],
                                            rstd16[:, 4 * t + h:4 * t + h + 1].broadcast_to([P, P]), ident, start=True, stop=True)
            last.then_inc(S["rs_psum"], 1)
            z_and_merge()

            for c in range(5):
                gemm_features(hhi, hlo)
            gemm_tokens(hhi, hlo)
            for c in range(2):
                gemm_features(hhi, hlo)
            nc.tensor.matmul(PS[0:DSA_H, 4, 0:384], relb_v, hot, start=True, stop=True).then_inc(S["line_psum"], 1)
            stored()
            w.next(S["line_ready"])
            for qt in range(NT):
                L = (qt + 1) * P
                tq = slice(qt * P, L)
                if qt:
                    for h in range(IDX_H):
                        if h >= 4:
                            w.next(S["relu_ready"])
                        r = slice(IDX_D * (h % 2), IDX_D * (h % 2) + IDX_D)
                        nc.tensor.matmul(PS[:, 4 + h % 4, 0:L], iq[r, h // 2, tq], ikT[r, 0:L],
                                         start=True, stop=True).then_inc(S["idx_psum"], 1)
                    w.next(S["relu_ready"], 4)
                for half in range(2):
                    for i in range(4):
                        last = nc.tensor.matmul(PS[:, 4 + i, 0:L], dq[:, 4 * half + i, tq], dk[:, half, 0:L], start=True, stop=True)
                    last.then_inc(S["lg_psum"], 1)
                    w.next(S["p_norm"])
                    for i in range(4):
                        for b in range(qt + 1):
                            last = nc.tensor.transpose(PS[:, 4 + i, b * P:b * P + P], lg[:, i, b * P:b * P + P], ident)
                    last.then_inc(S["p_turned"], 1)
                    w.next(S["pt_ready"])
                    for i in range(4):
                        for b in range(qt + 1):
                            last = nc.tensor.matmul(PS[:, 4, i * P:i * P + P], dv[:, b, half * P:half * P + P], pt[:, i, b, :],
                                                    start=(b == 0), stop=(b == qt))
                    last.then_inc(S["pv_psum"], 1)
                    w.next(S["o_copied"])
            z_and_merge()

            turn_normed(memn, 2)
            for c in range(4):
                gemm_features(mhi, mlo, tokens=M)
            for c in range(4):
                gemm_tokens(mhi, mlo, tiles=2)
            for c in range(4):
                gemm_features(hhi, hlo)
            stored()
            memory_attention(X_H, lambda h: [(xq, mk, (slice(0, P), 2 * h + i)) for i in range(2)], mv, True)
            z_and_merge()
            w.next(S["y_lo"], 4)
            for c in range(4):
                gemm_tokens(yhi, ylo)

            def feed_forward():
                nonlocal n, m
                turn_normed(xn, NT)
                k0, m0 = n // 2, m // 2
                a, b = n % 2, (n + 1) % 2
                ga, gb = m % 2, (m + 1) % 2
                ka, kb = n // 2, (n + 1) // 2
                ma, mb = m // 2, (m + 1) // 2
                with pe.Fori(0, FFT // 2) as i:
                    for p, g, kk, mm in ((a, ga, ka, ma), (b, gb, kb, mb)):
                        pe.wait_ge(lo_ready[p], i + (kk + 1))
                        pe.wait_ge(pair_free[g], i + mm)
                        for j in range(2):
                            for k in range(KT):
                                last = three(PS[:, 2 * g + j, :], k, KT,
                                             (whi[:, p, k, j * P:j * P + P], wlo[:, p, k, j * P:j * P + P]),
                                             (hhi[:, k, :], hlo[:, k, :]))
                        last.then_inc(slot_used[p], 1)
                n, m = n + FFT, m + FFT
                w.next(S["ffn_lo"], FFT // 2)
                stored()
                for c in range(4):
                    if c >= 2:
                        w.next(S["ffo_free"])
                    for r in range(0, FFT, KT):
                        pe.wait_ge(lo_ready[n % 2], n // 2 + 1)
                        p = n % 2
                        rows = min(KT, FFT - r)
                        for t in range(NT):
                            for k in range(rows):
                                last = three(PS[:, 4 * (c % 2) + t, 0:C], r + k, FFT,
                                             (ahi[:, r + k, t * P:t * P + P], alo[:, r + k, t * P:t * P + P]),
                                             (whi[:, p, k, :], wlo[:, p, k, :]))
                        last.then_inc(slot_used[p], 1)
                        n += 1
                w.next(S["ffo_free"], 2)

            def memory_parts(q_):
                return lambda h: [(q_, mk2, (slice(MEM_HD * (h % 2), MEM_HD * (h % 2) + MEM_HD), h // 2))]

            turn_normed(xn, NT)
            for c in range(4):
                gemm_features(hhi, hlo, groups=(0, ML_DK))
            for c in range(4):
                gemm_tokens(hhi, hlo, width=ML_DV)
            for c in range(3):
                gemm_tokens(hhi, hlo)
            gemm_features(hhi, hlo, groups=(0,))
            gemm_features(hhi, hlo)
            turn_normed(memn, 2)
            gemm_features(mhi, mlo, tokens=M)
            gemm_tokens(mhi, mlo, tiles=2)
            stored()
            for t in range(NT):
                last = nc.tensor.transpose(PS[:, 4, t * 8:t * 8 + 8], gT[0:8, t * P:t * P + P], ident[0:8, 0:8])
            last.then_inc(S["gt_turned"], 1)
            w.next(S["logf_ready"])
            nc.tensor.matmul(PS[:, 4, 0:16], u128, small[:, 200:216], start=True, stop=True).then_inc(S["cl_psum"], 1)
            w.next(S["bi_ready"])
            for h in range(ML_H):
                for t in range(NT):
                    last = nc.tensor.matmul(PS[:, 4 + h, t * P:t * P + P], lgf[:, t, h:h + 1].broadcast_to([P, P]), u128,
                                            start=True, stop=True)
            last.then_inc(S["lb_psum"], 1)
            w.next(S["lb_ready"])
            for h in range(ML_H):
                if h:
                    w.next(S["hm_ready"])
                for s in range(NT):
                    last = nc.tensor.matmul(PS[:, 4 + s, s * P:T], lk[0:ML_DK, h, s * P:s * P + P], lq[0:ML_DK, h, s * P:T],
                                            start=True, stop=True)
                last.then_inc(S["lsc_psum"], 1)
                w.next(S["at_ready"])
                for t in range(NT):
                    for s in range(t + 1):
                        last = nc.tensor.matmul(PS[:, 4 + t // 2, (t % 2) * C:(t % 2) * C + ML_DV + 1],
                                                at[:, s, t * P:t * P + P], lv[:, s, h, :], start=(s == 0), stop=(s == t))
                last.then_inc(S["num_psum"], 1)
            w.next(S["hm_ready"])
            memory_attention(MEM_H, memory_parts(mq), mv2, False)
            for k in range(6):
                if k >= 4:
                    w.next(S["y_lo"])
                for t in range(NT):
                    if k == 0:
                        w.next(S["hm_done"])
                    last = nc.tensor.transpose(PS[:, 4 + k % 4, t * P:t * P + P],
                                               hm[:, t].rearrange("p h d -> p (h d)")[:, k * P:k * P + P], ident)
                last.then_inc(S["hm_turned"], 1)
            w.next(S["y_lo"], 5)
            for c in range(4):
                gemm_tokens(yhi, ylo)
            feed_forward()

            turn_normed(xn, NT)
            gemm_tokens(hhi, hlo)
            gemm_tokens(hhi, hlo)
            turn_normed(xn, NT, again=True)
            for c in range(3):
                gemm_tokens(hhi, hlo)
            gemm_features(hhi, hlo)
            turn_normed(memn, 2)
            gemm_features(mhi, mlo, tokens=M)
            gemm_tokens(mhi, mlo, tiles=2)
            stored()
            for b in range(8):
                if b >= 4:
                    w.next(S["rot_copied"])
                for t in range(NT):
                    if b == 0:
                        w.next(S["rope_done"])
                    src = skr[:, t, b * P:b * P + P] if b < 2 else sqr[:, t, (b - 2) * P:(b - 1) * P]
                    last = nc.tensor.transpose(PS[:, 4 + b % 4, t * P:t * P + P], src, ident)
                last.then_inc(S["rope_turned"], 1)
            w.next(S["rot_copied"], 4)
            for h in range(SW_H):
                if h:
                    w.next(S["o_copied"])
                place_, kv = SWA_ORDER.index(h), h // 3
                r = slice(SW_HD * (kv % 2), SW_HD * (kv % 2) + SW_HD)
                for t in range(NT):
                    k0 = max(t - 1, 0) * P
                    o0 = 0 if t else P
                    last = nc.tensor.matmul(PS[:, 4 + t // 2, (t % 2) * C + o0:(t % 2) * C + C],
                                            qrT[r, place_ // 2, t * P:t * P + P], krT[r, kv // 2, k0:t * P + P], start=True, stop=True)
                last.then_inc(S["lg_psum"], 1)
                w.next(S["p_norm"])
                for j in range(7):
                    t, b = (j + 1) // 2, (j + 1) % 2
                    last = nc.tensor.transpose(PS[:, 6 + j // 4, (j % 4) * P:(j % 4) * P + P], slg[:, t, b * P:b * P + P], ident)
                last.then_inc(S["p_turned"], 1)
                w.next(S["pt_ready"])
                ro = slice(SW_HD * (h % 2), SW_HD * (h % 2) + SW_HD)
                for t in range(NT):
                    for b in range(0 if t else 1, 2):
                        j = 2 * t + b - 1
                        last = nc.tensor.matmul(PS[ro, 4, t * P:t * P + P], sv[:, t + b - 1, kv * SW_HD:(kv + 1) * SW_HD],
                                                spt[:, j, :], start=(b == (0 if t else 1)), stop=(b == 1))
                last.then_inc(S["pv_psum"], 1)
            w.next(S["o_copied"])
            memory_attention(MEM_H, memory_parts(mqb), mv2, False)
            w.next(S["y_lo"], 4)
            for c in range(4):
                gemm_tokens(yhi, ylo)
            feed_forward()
            assert n == NS

        @block.scalar
        def _(act):
            w = Waits(act, S["act_chain"])
            n = m = 0

            def copy(out_, in_, scale=1.0, func=ACT.Copy):
                return nc.scalar.activation(out_, in_, func, scale=scale)

            def split(s):
                if s < NS:
                    act.wait_ge(raw_ready[s % 2], 16 * (s // 2 + 1))
                    if s >= 2:
                        act.wait_ge(slot_used[s % 2], s // 2)
                    copy(whi[:, s % 2], raw[:, s % 2]).then_inc(hi_ready[s % 2], 1)

            def pair():
                return PS[:, 2 * (m % 2):2 * (m % 2) + 2, :]

            def pair_tokens():
                return pair().rearrange("p b (u c) -> p (b u) c", u=2)

            def taken(instruction):
                nonlocal n, m
                instruction.then_inc(pair_free[m % 2], 1)
                split(n + 2)
                n, m = n + 1, m + 1

            def computed():
                act.wait_ge(slot_used[n % 2], n // 2 + 1)

            def store_features(dst, c, scale=1.0, tokens=T):
                computed()
                taken(copy(dst[:, 2 * c:2 * c + 2, :], pair()[:, :, 0:tokens], scale))

            def store_tokens(dst, c, scale=1.0, tiles=NT, func=ACT.Copy):
                computed()
                taken(copy(dst[:, :, c * C:(c + 1) * C], pair_tokens()[:, 0:tiles, :], scale, func))

            def passed():
                nonlocal n, m
                split(n + 2)
                n, m = n + 1, m + 1

            def square_sums(src, tiles, sources=None):
                for t in range(tiles):
                    if sources is not None:
                        w.next(sources)
                    last = nc.scalar.activation(PS[:, 6:8, :].rearrange("p b c -> p (b c)"), src[:, t], ACT.Square,
                                                accum_out=ss[:, t:t + 1])
                    w.link(last)

            def roots(signal, tiles=NT):
                nc.scalar.activation(root[:, 0:tiles], ss[:, 0:tiles], ACT.Sqrt, bias=epsc, scale=1.0 / D)\
                    .then_inc(S[signal], 1)

            def norm(src, tiles, gain, hi, source=None, again=False):
                if not again:
                    square_sums(src, tiles, source)
                    roots("norm_root", tiles)
                for k in range(KT):
                    w.next(S["norm_turned"])
                    copy(hi[:, k, :], PS[:, 4 + k % 4, 0:tiles * P], V[:, gain + k:gain + k + 1]).then_inc(S["hhi_ready"], 1)

            def split_output(src, count, at=0):
                for c in range(count):
                    copy(yhi[:, at + 2 * c:at + 2 * c + 2, :], src[:, 2 * c:2 * c + 2, :]).then_inc(S["y_hi"], 1)

            def z_and_merge():
                for c in range(4):
                    computed()
                    taken(copy(ztmp[:, :, :], pair(), func=ACT.Silu))
                    w.next(S["z_prod"])
                    copy(yhi[:, 2 * c:2 * c + 2, :], ZO[0][:, 2 * c:2 * c + 2, :]).then_inc(S["y_hi"], 1)
                for c in range(4):
                    computed()
                    if c:
                        act.wait_ge(pair_free[(m + 1) % 2], (m + 1) // 2)
                    taken(copy(gsig[:, :, :], pair(), func=ACT.Sigmoid))
                    passed()

            ZO = [None]

            def memory_attention(heads, cross, dst):
                p_, pt_ = (xp, xpt) if cross else (xp2, xpt2)
                for h in range(heads):
                    w.next(S["lg_ready"])
                    for t in range(NT):
                        last = nc.scalar.activation(p_[:, t, :], PS[:, 4 + t // 2, (t % 2) * C:(t % 2) * C + C], ACT.Exp,
                                                    bias=nmax[:, t:t + 1], accum_out=psum_[:, t:t + 1])
                    last.then_inc(S["p_exp"], 1)
                    w.next(S["p_turned"])
                    copy(pt_[:, :, :], PS[:, 6:8, :]).then_inc(S["pt_ready"], 1)
                    w.next(S["pv_psum"])
                    if cross:
                        last = copy(dst[:, 2 * h:2 * h + 2, :], PS[:, 4:6, :])
                    else:
                        r = slice(MEM_HD * (h % 2), MEM_HD * (h % 2) + MEM_HD)
                        last = copy(dst[r, h // 2, :], PS[r, 4, :])
                    last.then_inc(S["o_copied"], 1)
                w.next(S["o_copied"], heads)

            act.wait_ge(S["x_loaded"], 16)
            act.wait_ge(S["const_loaded"], 32)
            norm(X, NT, V_PRE, hhi)
            split(0)
            split(1)
            computed()
            copy(ikT[:, :], PS[:, 0, :])
            taken(copy(spT[0:32, :], PS[0:32, 1, :]))
            for c in range(2):
                store_features(gq, c, GLA_DK ** -0.5)
            for c in range(2):
                store_features(gk, c)
            for c in range(4):
                store_tokens(gv, c)

            w.next(S["la_psum"])
            w.link(copy(lscr[:, :, :], PS[:, 4:8, :], func=ACT.Abs))
            w.link(copy(lscr[:, :, :], lscr[:, :, :], -1.0, ACT.Exp))
            nc.scalar.activation(lscr[:, :, :], lscr[:, :, :], ACT.Ln, bias=1.0).then_inc(S["la_exp"], 1)
            for h in range(GLA_H):
                w.next(S["b_psum"])
                if h:
                    w.next(S["gk_ready"])
                copy(ge[:, 0, :], PS[:, 4 + h, :], 1.0 / GLA_NORM, ACT.Exp)
                copy(ge[:, 1, :], PS[:, 4 + h, :], -1.0 / GLA_NORM, ACT.Exp).then_inc(S["eb_ready"], 1)
                w.next(S["ediff_ready"])
                copy(ge[:, 2, :], ge[:, 2, :], 1.0 / GLA_NORM, ACT.Exp).then_inc(S["ekt_ready"], 1)
            for h in range(GLA_H):
                w.next(S["kt_turned"])
                copy(gktok[:, :, h * P:h * P + P], PS[:, 4 + h, :].rearrange("p (t d) -> p t d", t=NT))\
                    .then_inc(S["kt_copied"], 1)
            for t in range(NT):
                w.next(S["go_psum"])
                copy(go[:, 0:4, t * P:t * P + P], PS[:, 4, :].rearrange("p (v t) -> p v t", v=4))
                copy(go[:, 4:8, t * P:t * P + P], PS[:, 7, :].rearrange("p (v t) -> p v t", v=4)).then_inc(S["go_copied"], 1)
            w.next(S["go_copied"], NT)
            copy(gsq[:, :, :], go[:, :, :], func=ACT.Square).then_inc(S["sq_ready"], 1)
            w.next(S["ssq_psum"])
            nc.scalar.activation(root[:, 0:16], PS[:, 4, 0:16], ACT.Sqrt, bias=epsc, scale=1.0 / GLA_DV)\
                .then_inc(S["gla_root"], 1)
            ZO[0] = go
            z_and_merge()

            for c in range(4):
                store_features(dq, c, DSA_HD ** -0.5)
            store_features(dk, 0)
            store_tokens(dv, 0)
            for c in range(2):
                store_features(iq, c)
            w.next(S["line_psum"])
            copy(linet[:, :], PS[0:DSA_H, 4, 0:384]).then_inc(S["line_ready"], 1)
            for qt in range(NT):
                L = (qt + 1) * P
                if qt:
                    for h in range(IDX_H):
                        if h >= 4 or qt > 1:
                            w.next(S["relu_used"])
                        w.next(S["idx_psum"])
                        copy(relu[:, h % 4, 0:L], PS[:, 4 + h % 4, 0:L], func=ACT.Relu).then_inc(S["relu_ready"], 1)
                for half in range(2):
                    w.next(S["lg_ready"])
                    for i in range(4):
                        last = nc.scalar.activation(lg[:, i, 0:L], lg[:, i, 0:L], ACT.Exp,
                                                    bias=nmax[:, i:i + 1], accum_out=psum_[:, i:i + 1])
                    last.then_inc(S["p_exp"], 1)
                    w.next(S["p_turned"])
                    copy(pt[:, :, 0:qt + 1, :], PS[:, 4:8, 0:L].rearrange("p i (b q) -> p i b q", q=P)).then_inc(S["pt_ready"], 1)
                    w.next(S["pv_psum"])
                    copy(do[:, 4 * half:4 * half + 4, qt * P:L], PS[:, 4, :].rearrange("p (i q) -> p i q", i=4))\
                        .then_inc(S["o_copied"], 1)
            w.next(S["o_copied"], 2 * NT)
            ZO[0] = do
            z_and_merge()

            act.wait_ge(S["mem_loaded"], 16)
            norm(memx, 2, V_MEM, mhi)
            for c in range(4):
                store_features(mk, c, tokens=M)
            for c in range(4):
                store_tokens(mv, c, tiles=2)
            for c in range(4):
                store_features(xq, c, X_HD ** -0.5)
            memory_attention(X_H, True, xo)
            ZO[0] = xo
            z_and_merge()
            w.next(S["merged_ready"], 3)
            split_output(merged, 4)
            for c in range(4):
                store_tokens(o_mix, c)

            def after(o):
                if o is o_ffn:
                    w.next(S["ffo_free"], 4)
                else:
                    for b in range(2):
                        act.wait_ge(pair_free[b], (m + 1 - b) // 2)
                square_sums(o, NT)
                roots("o_root")

            def feed_forward(gain):
                nonlocal n, m
                norm(X, NT, gain, hhi, S["x_new"])
                sg, su = n % 2, (n + 1) % 2
                kg, ku = n // 2, (n + 1) // 2
                pg = m % 2
                r0 = w.at.get(S["ffn_a"].name, 0)
                with act.Fori(0, FFT // 2) as i:
                    act.wait_ge(slot_used[sg], i + (kg + 1))
                    copy(fs[:, :, :], PS[:, 2 * pg:2 * pg + 2, :], func=ACT.Silu).then_inc(pair_free[pg], 1)
                    act.wait_ge(raw_ready[sg], i * 16 + 16 * (kg + 2))
                    copy(whi[:, sg], raw[:, sg]).then_inc(hi_ready[sg], 1)
                    act.wait_ge(S["ffn_a"], i + (r0 + 1))
                    copy(ahi[:, bass.ds(i * 2, 2), :], fa[:, :, :]).then_inc(S["ffn_hi"], 1)
                    act.wait_ge(slot_used[su], i + (ku + 1))
                    act.wait_ge(raw_ready[su], i * 16 + 16 * (ku + 2))
                    copy(whi[:, su], raw[:, su]).then_inc(hi_ready[su], 1)
                w.at[S["ffn_a"].name] = r0 + FFT // 2
                n, m = n + FFT, m + FFT
                for c in range(4):
                    for r in range(0, FFT, KT):
                        act.wait_ge(slot_used[n % 2], n // 2 + 1)
                        if r + KT >= FFT:
                            copy(o_ffn[:, :, c * C:(c + 1) * C], PS[:, 4 * (c % 2):4 * (c % 2) + 4, 0:C])\
                                .then_inc(S["ffo_free"], 1)
                        split(n + 2)
                        n += 1
                after(o_ffn)

            after(o_mix)

            norm(X, NT, V_MIX0, hhi, S["x_new"])
            for c in range(4):
                computed()
                dst = (lq if c < 2 else lk)[0:ML_DK, 2 * (c % 2):2 * (c % 2) + 2, :]
                taken(copy(dst, pair()[0:ML_DK], 1.0 if c < 2 else ML_DK ** -0.5))
            for h in range(ML_H):
                computed()
                taken(copy(lv[:, :, h, 0:ML_DV], pair_tokens()[:, :, 0:ML_DV]))
            for c in range(3):
                store_tokens(lo, c, func=ACT.Sigmoid)
            computed()
            taken(copy(gT[0:8, :], pair()[0:8, 0, :]))
            store_features(mq, 0, MEM_HD ** -0.5)
            act.wait_ge(S["mem_loaded"], 32)
            norm(memx, 2, V_MEM0, mhi)
            store_features(mk2, 0, tokens=M)
            store_tokens(mv2, 0, tiles=2)
            w.next(S["gate_soft"])
            copy(lgt[:, :, :], lgt[:, :, :], 1.0 / SOFTCAP, ACT.Tanh).then_inc(S["gate_abs"], 1)
            w.next(S["gate_exp"])
            w.link(copy(lex[:, :, :], lgt[:, :, 4:8], func=ACT.Abs))
            w.link(copy(lex[:, :, :], lex[:, :, :], -1.0, ACT.Exp))
            nc.scalar.activation(lex[:, :, :], lex[:, :, :], ACT.Ln, bias=1.0).then_inc(S["la_exp"], 1)
            w.next(S["lb_psum"])
            copy(Lb[:, :, :], PS[:, 4:8, :]).then_inc(S["lb_ready"], 1)
            for h in range(ML_H):
                w.next(S["lw_arg"])
                for s in range(NT):
                    for j in range(s, NT):
                        js = slice(j * P, j * P + P)
                        src, b = (at[:, s, js], 0.0) if j == s else (Lb[:, h, js], bi[:, s, j, h:h + 1])
                        last = nc.scalar.activation(at[:, s, js], src, ACT.Exp, bias=b)
                last.then_inc(S["lw_exp"], 1)
                w.next(S["hm_ready"])
                for t in range(NT):
                    w.link(nc.scalar.activation(ljunk[:, :], hm[:, t, h, :], ACT.Square,
                                                accum_out=ss[:, 4 * t + h:4 * t + h + 1]))
            nc.scalar.activation(root[:, 0:16], ss[:, 0:16], ACT.Sqrt, bias=epsc, scale=1.0 / ML_DV).then_inc(S["hm_root"], 1)
            memory_attention(MEM_H, False, mo)
            for k in range(6):
                w.next(S["hm_turned"])
                copy(yhi[:, k, :], PS[:, 4 + k % 4, :]).then_inc(S["y_hi"], 1)
            split_output(mo, 1, at=6)
            for c in range(4):
                store_tokens(o_mix, c)
            after(o_mix)
            feed_forward(V_FFN0)

            norm(X, NT, V_KV, hhi, S["x_new"])
            store_tokens(sk, 0)
            store_tokens(sv, 0)
            norm(X, NT, V_MIX1, hhi, again=True)
            for c in range(3):
                store_tokens(sq, c, SW_HD ** -0.5)
            store_features(mqb, 0, MEM_HD ** -0.5)
            act.wait_ge(S["mem_loaded"], 48)
            norm(memx, 2, V_MEM1, mhi)
            store_features(mk2, 0, tokens=M)
            store_tokens(mv2, 0, tiles=2)
            for j in range(2):
                w.next(S["rope_arg"])
                copy(cs[:, j], cs[:, j], func=ACT.Sin).then_inc(S["rope_sin"], 1)
            for b in range(8):
                w.next(S["rope_turned"])
                copy(krT[:, b, :] if b < 2 else qrT[:, b - 2, :], PS[:, 4 + b % 4, :]).then_inc(S["rot_copied"], 1)
            for h in range(SW_H):
                w.next(S["lg_ready"])
                for t in range(NT):
                    nc.scalar.activation(slg[:, t, :], slg[:, t, :], ACT.Exp, bias=nmax[:, t:t + 1],
                                         accum_out=psum_[:, t:t + 1])
                nc.scalar.activation(esink, nmax, ACT.Exp, bias=V[:, V_SINK + h:V_SINK + h + 1]).then_inc(S["p_exp"], 1)
                w.next(S["p_turned"])
                copy(spt[:, :, :], PS[:, 6:8, :].rearrange("p b (j q) -> p (b j) q", q=P)[:, 0:7, :]).then_inc(S["pt_ready"], 1)
                w.next(S["pv_psum"])
                r = slice(SW_HD * (h % 2), SW_HD * (h % 2) + SW_HD)
                copy(so[r, h // 2, :], PS[r, 4, :]).then_inc(S["o_copied"], 1)
            w.next(S["o_copied"], SW_H)
            memory_attention(MEM_H, False, mo)
            split_output(so, 3)
            split_output(mo, 1, at=6)
            for c in range(4):
                store_tokens(o_mix, c)
            after(o_mix)
            feed_forward(V_FFN1)

        @block.vector
        def _(dve):
            w = Waits(dve, S["dve_chain"])
            V_ = nc.vector
            n = m = 0

            def split(s):
                if s < NS:
                    dve.wait_ge(hi_ready[s % 2], s // 2 + 1)
                    V_.tensor_tensor(wlo[:, s % 2], raw[:, s % 2], whi[:, s % 2], ALU.subtract).then_inc(lo_ready[s % 2], 1)

            def pair():
                return PS[:, 2 * (m % 2):2 * (m % 2) + 2, :]

            def passed(count=1):
                nonlocal n, m
                for _ in range(count):
                    split(n + 2)
                    n, m = n + 1, m + 1

            def stored():
                for b in range(2):
                    dve.wait_ge(pair_free[b], (m + 1 - b) // 2)

            def norm(src, dst, tiles, gain, hi, lo, again=False):
                if not again:
                    w.next(S["norm_root"])
                    w.link(V_.reciprocal(rstd[:, 0:tiles], root[:, 0:tiles]))
                    for t in range(tiles):
                        V_.tensor_scalar(dst[:, t], src[:, t], rstd[:, t:t + 1], None, ALU.mult).then_inc(S["xn_ready"], 1)
                for k in range(KT):
                    w.next(S["hhi_ready"])
                    V_.scalar_tensor_tensor(lo[:, k, :], PS[:, 4 + k % 4, 0:tiles * P], V[:, gain + k:gain + k + 1],
                                            hi[:, k, :], ALU.mult, ALU.subtract).then_inc(S["hlo_ready"], 1)

            def split_output(src, count, at_=0):
                for c in range(count):
                    w.next(S["y_hi"])
                    V_.tensor_tensor(ylo[:, at_ + 2 * c:at_ + 2 * c + 2, :], src[:, 2 * c:2 * c + 2, :],
                                     yhi[:, at_ + 2 * c:at_ + 2 * c + 2, :], ALU.subtract).then_inc(S["y_lo"], 1)

            def z_and_merge(o, branch):
                nonlocal n, m
                for c in range(4):
                    oc = o[:, 2 * c:2 * c + 2, :]
                    dve.wait_ge(pair_free[m % 2], m // 2 + 1)
                    V_.tensor_tensor(oc, oc, ztmp[:, :, :], ALU.mult).then_inc(S["z_prod"], 1)
                    passed()
                    w.next(S["y_hi"])
                    V_.tensor_tensor(ylo[:, 2 * c:2 * c + 2, :], oc, yhi[:, 2 * c:2 * c + 2, :], ALU.subtract)\
                        .then_inc(S["y_lo"], 1)
                for c in range(4):
                    mc = merged[:, 2 * c:2 * c + 2, :]
                    dve.wait_ge(pair_free[m % 2], m // 2 + 1)
                    passed()
                    dve.wait_ge(slot_used[n % 2], n // 2 + 1)
                    if branch == 0:
                        last = V_.tensor_tensor(mc, pair(), gsig[:, :, :], ALU.mult)
                        last.then_inc(pair_free[m % 2], 1)
                    else:
                        V_.tensor_tensor(gprod[:, :, :], pair(), gsig[:, :, :], ALU.mult).then_inc(pair_free[m % 2], 1)
                        dve.wait_ge(pair_free[m % 2], m // 2 + 1)
                        last = V_.tensor_tensor(mc, mc, gprod[:, :, :], ALU.add)
                        if c < 3:
                            w.link(last)
                    if c == 3 and branch:
                        last.then_inc(S["merged_ready"], 1)
                    passed()
                if not branch:
                    V_.tensor_copy(nmax[:, 0:1], ones[:, 0:1]).then_inc(S["merged_ready"], 1)

            def softmax_scale(p_, width):
                w.next(S["p_exp"])
                w.link(V_.reciprocal(prec, psum_))
                V_.tensor_tensor(p_, p_, prec.unsqueeze(2).broadcast_to([P, 4, width]), ALU.mult).then_inc(S["p_norm"], 1)

            def memory_attention(heads, cross):
                for h in range(heads):
                    w.next(S["lg_psum"])
                    V_.tensor_reduce(nmax, PS[:, 4:6, :].rearrange("p b (u c) -> p (b u) c", u=2), AX.X, ALU.max, negate=True)\
                        .then_inc(S["lg_ready"], 1)
                    softmax_scale((xp if cross else xp2)[:, :, :], M)

            dve.wait_ge(S["const_loaded"], 32)
            norm(X, xn, NT, V_PRE, hhi, hlo)
            split(0)
            split(1)
            passed(9)

            V_.memset(attm[:, :, :], 0.0)
            V_.tensor_scalar(nsink, V[:, V_SINK:V_SINK + SW_H], -1.0, None, ALU.mult)
            w.next(S["iw_turned"])
            V_.tensor_scalar(iwt, PS[:, 4, 0:128].rearrange("p (t c) -> p t c", t=NT)[:, :, 16:24],
                             IDX_H ** -0.5, IDX_D ** -0.5, ALU.mult, ALU.mult).then_inc(S["special_ready"], 1)
            w.next(S["la_exp"])
            V_.scalar_tensor_tensor(la[:, :, :], PS[:, 4:8, :], 0.0, lscr[:, :, :], ALU.min, ALU.subtract)\
                .then_inc(S["la_ready"], 1)
            for h in range(GLA_H):
                w.next(S["eb_ready"])
                b_ = PS[:, 4 + h, :].rearrange("p (c t) -> p c t", t=64)
                w.link(V_.tensor_copy(blast, b_[:, :, 63]))
                V_.tensor_tensor(ge[:, 2, :].rearrange("p (c t) -> p c t", t=64), blast.unsqueeze(2).broadcast_to([P, 8, 64]), b_,
                                 ALU.subtract).then_inc(S["ediff_ready"], 1)
                V_.tensor_copy(dec[:, h, :], ge[:, 0, :].rearrange("p (c t) -> p c t", t=64)[:, :, 63])
                V_.tensor_tensor(gq[:, h, :], gq[:, h, :], ge[:, 0, :], ALU.mult)
                w.next(S["ekt_ready"])
                w.link(V_.tensor_tensor(gkt[:, h, :], gk[:, h, :], ge[:, 2, :], ALU.mult))
                V_.tensor_tensor(gk[:, h, :], gk[:, h, :], ge[:, 1, :], ALU.mult).then_inc(S["gk_ready"], 1)
            w.next(S["kt_copied"], GLA_H)
            for t in range(NT):
                w.next(S["att_psum"])
                V_.copy_predicated(attm[:, :, :], u64.bitcast(U32).unsqueeze(1).broadcast_to([P, GLA_H, P]),
                                   PS[:, 4, :].rearrange("p (h t) -> p h t", h=GLA_H)).then_inc(S["att_ready"], 1)
                for c in (2 * t, 2 * t + 1):
                    if c == 2 * NT - 1:
                        break
                    w.next(S["gla_upd"])
                    for h in range(GLA_H):
                        new, upd = S_t[:, (c + 1) % 4, h, :], PS[:, 5 + h // 2, (h % 2) * C:(h % 2) * C + C]
                        if c:
                            last = V_.scalar_tensor_tensor(new, S_t[:, c % 4, h, :], dec[:, h, c:c + 1], upd, ALU.mult, ALU.add)
                        else:
                            last = V_.tensor_copy(new, upd)
                    last.then_inc(S["S_ready"], 1)
                    w.next(S["S_ready"])
            w.next(S["gla_root"])
            V_.reciprocal(rstd16, root[:, 0:16]).then_inc(S["gla_rstd"], 1)
            w.next(S["rs_psum"])
            for h in range(GLA_H):
                for v in range(2):
                    i = 2 * h + v
                    last = V_.scalar_tensor_tensor(go[:, i, :], go[:, i, :], V[:, V_GLA + v:V_GLA + v + 1], PS[:, 4 + h, :],
                                                   ALU.mult, ALU.mult)
            w.link(last)
            z_and_merge(go, 0)

            passed(8)
            dve.wait_ge(S["tbias_loaded"], 16)
            for qt in range(NT):
                L = (qt + 1) * P
                if qt:
                    for h in range(IDX_H):
                        w.next(S["relu_ready"])
                        iw = iwt[:, qt, h:h + 1]
                        if h == 0:
                            last = V_.tensor_scalar(score[:, 0:L], relu[:, 0, 0:L], iw, None, ALU.mult)
                        else:
                            last = V_.scalar_tensor_tensor(score[:, 0:L], relu[:, h % 4, 0:L], iw, score[:, 0:L], ALU.mult, ALU.add)
                        last.then_inc(S["relu_used"], 1)
                        w.next(S["relu_used"])
                    V_.tensor_copy(top8[:, 0:1], score[:, 0:1]).then_inc(S["score_ready"], 1)
                    w.next(S["score_masked"])
                    for r in range(TOPK // 8):
                        w.link(V_.max(top8, score[:, 0:L]))
                        w.link(V_.match_replace(score[:, 0:L], top8, score[:, 0:L], TAKEN))
                    w.link(V_.tensor_scalar(maskt[:, 0:L], score[:, 0:L], TAKEN, NEG, ALU.not_equal, ALU.mult))
                mask = maskt[:, 0:L] if qt else dcm
                near = min(L, C)
                for half in range(2):
                    w.next(S["lg_psum"])
                    l_ = lg[:, :, 0:L]
                    w.link(V_.tensor_tensor(l_, PS[:, 4:8, 0:L], mask.unsqueeze(1).broadcast_to([P, 4, L]), ALU.add))
                    w.link(V_.tensor_tensor(lg[:, :, L - near:L], lg[:, :, L - near:L],
                                            tbias[:, 4 * half:4 * half + 4, C - near:C], ALU.add))
                    V_.tensor_reduce(nmax, l_, AX.X, ALU.max, negate=True).then_inc(S["lg_ready"], 1)
                    softmax_scale(l_, L)
            stored()
            w.next(S["o_copied"], 8)
            z_and_merge(do, 1)

            norm(memx, memn, 2, V_MEM, mhi, mlo)
            passed(12)
            memory_attention(X_H, True)
            w.next(S["o_copied"], X_H)
            z_and_merge(xo, 2)
            split_output(merged, 4)
            passed(4)

            def residual(o, loads):
                w.next(S["o_root"])
                w.link(V_.reciprocal(rstd[:, 0:NT], root[:, 0:NT]))
                dve.wait_ge(S["gpost_loaded"], 16 * loads)
                for t in range(NT):
                    w.link(V_.scalar_tensor_tensor(o[:, t], o[:, t], rstd[:, t:t + 1], gpost[:, :], ALU.mult, ALU.mult))
                    V_.tensor_tensor(X[:, t], X[:, t], o[:, t], ALU.add).then_inc(S["x_new"], 1)

            def feed_forward(gain, loads):
                nonlocal n, m
                norm(X, xn, NT, gain, hhi, hlo)
                sg, su = n % 2, (n + 1) % 2
                kg, ku = n // 2, (n + 1) // 2
                pg, pu, mg = m % 2, (m + 1) % 2, m // 2
                r0 = w.at.get(S["ffn_hi"].name, 0)
                with dve.Fori(0, FFT // 2) as i:
                    dve.wait_ge(hi_ready[sg], i + (kg + 2))
                    V_.tensor_tensor(wlo[:, sg], raw[:, sg], whi[:, sg], ALU.subtract).then_inc(lo_ready[sg], 1)
                    dve.wait_ge(pair_free[pg], i + (mg + 1))
                    dve.wait_ge(slot_used[su], i + (ku + 1))
                    V_.tensor_tensor(fa[:, :, :], PS[:, 2 * pu:2 * pu + 2, :], fs[:, :, :], ALU.mult).then_inc(pair_free[pu], 1)
                    dve.wait_ge(pair_free[pu], i + ((m + 1) // 2 + 1))
                    V_.tensor_copy(small[:, 336:337], fa[:, 0, 0:1]).then_inc(S["ffn_a"], 1)
                    dve.wait_ge(S["ffn_hi"], i + (r0 + 1))
                    V_.tensor_tensor(alo[:, bass.ds(i * 2, 2), :], fa[:, :, :], ahi[:, bass.ds(i * 2, 2), :], ALU.subtract)\
                        .then_inc(S["ffn_lo"], 1)
                    dve.wait_ge(hi_ready[su], i + (ku + 2))
                    V_.tensor_tensor(wlo[:, su], raw[:, su], whi[:, su], ALU.subtract).then_inc(lo_ready[su], 1)
                w.at[S["ffn_hi"].name] = r0 + FFT // 2
                n, m = n + FFT, m + FFT
                for c in range(4 * -(-FFT // KT)):
                    split(n + 2)
                    n += 1
                residual(o_ffn, loads)

            residual(o_mix, 1)

            norm(X, xn, NT, V_MIX0, hhi, hlo)
            V_.memset(lv[:, :, :, ML_DV:ML_DV + 1], 1.0).then_inc(S["ones_ready"], 1)
            passed(13)
            norm(memx, memn, 2, V_MEM0, mhi, mlo)
            passed(2)
            w.next(S["gt_turned"])
            V_.tensor_tensor(lgt, PS[:, 4, 0:32].rearrange("p (t g) -> p t g", t=NT),
                             V[:, V_BG:V_BG + 8].unsqueeze(1).broadcast_to([P, NT, 8]), ALU.add).then_inc(S["gate_soft"], 1)
            w.next(S["gate_abs"])
            V_.tensor_scalar(lgt, lgt, SOFTCAP, None, ALU.mult).then_inc(S["gate_exp"], 1)
            w.next(S["la_exp"])
            V_.scalar_tensor_tensor(lgf, lgt[:, :, 4:8], 0.0, lex, ALU.min, ALU.subtract).then_inc(S["logf_ready"], 1)
            w.next(S["cl_psum"])
            for t in range(NT):
                last = V_.tensor_tensor(bi[:, t, t, :], lgt[:, t, 0:4], PS[:, 4, 4 * t:4 * t + 4], ALU.subtract)
            last.then_inc(S["bi_ready"], 1)
            w.next(S["bi_ready"])
            w.next(S["lb_ready"])
            for s in range(NT):
                for j in range(s + 1, NT):
                    w.link(V_.tensor_tensor(bi[:, s, j, :], bi[:, s, j - 1, :], Lb[:, :, j * P - 1], ALU.add))
            for h in range(ML_H):
                for s in range(NT):
                    ssl = slice(s * P, s * P + P)
                    last = V_.scalar_tensor_tensor(at[:, s, ssl], Lb[:, h, ssl], bi[:, s, s, h:h + 1], lcm, ALU.add, ALU.add)
                last.then_inc(S["lw_arg"], 1)
                w.next(S["lw_exp"])
                w.next(S["lsc_psum"])
                for s in range(NT):
                    last = V_.tensor_tensor(at[:, s, s * P:T], at[:, s, s * P:T], PS[:, 4 + s, s * P:T], ALU.mult)
                last.then_inc(S["at_ready"], 1)
                w.next(S["num_psum"])
                num = PS[:, 4:6, :].rearrange("p b (u c) -> p (b u) c", u=2)
                w.link(V_.tensor_copy(lden.unsqueeze(2), num[:, :, ML_DV:ML_DV + 1]))
                w.link(V_.scalar_tensor_tensor(lden, lden, -1.0, lden, ALU.mult, ALU.max))
                w.link(V_.tensor_scalar(lden, lden, 1.0, None, ALU.max))
                w.link(V_.reciprocal(lden, lden))
                V_.tensor_tensor(hm[:, :, h, :], num[:, :, 0:ML_DV], lden.unsqueeze(2).broadcast_to([P, NT, ML_DV]), ALU.mult)\
                    .then_inc(S["hm_ready"], 1)
            w.next(S["hm_root"])
            w.link(V_.reciprocal(rstd16, root[:, 0:16]))
            dve.wait_ge(S["gml_loaded"], 16)
            for t in range(NT):
                hr = hm[:, t].rearrange("p h d -> p (h d)")
                w.link(V_.tensor_tensor(hm[:, t], hm[:, t], rstd16[:, 4 * t:4 * t + 4].unsqueeze(2).broadcast_to([P, 4, ML_DV]), ALU.mult))
                w.link(V_.tensor_tensor(hr, hr, gmb[:, :], ALU.mult))
                V_.tensor_tensor(hr, hr, lo[:, t, :], ALU.mult).then_inc(S["hm_done"], 1)
            memory_attention(MEM_H, False)
            for k in range(6):
                w.next(S["y_hi"])
                V_.tensor_tensor(ylo[:, k, :], PS[:, 4 + k % 4, :], yhi[:, k, :], ALU.subtract).then_inc(S["y_lo"], 1)
            split_output(mo, 1, at_=6)
            passed(4)
            residual(o_mix, 2)
            feed_forward(V_FFN0, 3)

            norm(X, xn, NT, V_KV, hhi, hlo)
            passed(2)
            norm(X, xn, NT, V_MIX1, hhi, hlo, again=True)
            passed(4)
            norm(memx, memn, 2, V_MEM1, mhi, mlo)
            passed(2)
            ang, arg = ra[:, 0:128].rearrange("p (t d) -> p t d", t=NT), ra[:, 128:256].rearrange("p (t d) -> p t d", t=NT)
            ki, kf = rb[:, 0:128].bitcast(I32).rearrange("p (t d) -> p t d", t=NT), ra[:, 256:384].rearrange("p (t d) -> p t d", t=NT)
            dve.wait_ge(S["pos_loaded"], 16)
            w.link(V_.tensor_copy(posf, posi))
            w.link(V_.tensor_tensor(ang, posf.unsqueeze(2).broadcast_to([P, NT, 32]),
                                    inv.unsqueeze(1).broadcast_to([P, NT, 32]), ALU.mult))
            for j in range(2):
                w.link(V_.tensor_scalar(ki, ang, 1.0 / (2 * math.pi), 0.25 * (1 - j), ALU.mult, ALU.add))
                w.link(V_.tensor_copy(kf, ki))
                w.link(V_.scalar_tensor_tensor(arg, kf, -TURN[0], ang, ALU.mult, ALU.add))
                w.link(V_.scalar_tensor_tensor(arg, kf, -TURN[1], arg, ALU.mult, ALU.add))
                w.link(V_.scalar_tensor_tensor(arg, kf, -TURN[2], arg, ALU.mult, ALU.add))
                if j == 0:
                    w.link(V_.tensor_scalar(arg, arg, math.pi / 2, None, ALU.add))
                V_.tensor_scalar(cs[:, j], arg, PI_IN, -PI_IN, ALU.min, ALU.max).then_inc(S["rope_arg"], 1)
                w.next(S["rope_sin"])
            stored()
            for t in range(NT):
                for heads, src, dst in ((SW_KV, sk, skr), (SW_H, sq, sqr)):
                    x = src[:, t].rearrange("p (h a d) -> p h a d", a=2, d=32)
                    y = dst[:, t].rearrange("p (h a d) -> p h a d", a=2, d=32)
                    width = heads * SW_HD
                    xc = ra[:, 0:width].rearrange("p (h a d) -> p h a d", a=2, d=32)
                    xs = rb[:, 0:width].rearrange("p (h a d) -> p h a d", a=2, d=32)
                    sin = cs[:, 1, t, :].unsqueeze(1).broadcast_to([P, heads, 32])
                    V_.tensor_tensor(ra[:, 0:width].rearrange("p (h d) -> p h d", d=32), src[:, t].rearrange("p (h d) -> p h d", d=32),
                                     cs[:, 0, t, :].unsqueeze(1).broadcast_to([P, 2 * heads, 32]), ALU.mult)
                    V_.tensor_tensor(xs[:, :, 0, :], x[:, :, 1, :], sin, ALU.mult)
                    w.link(V_.tensor_tensor(xs[:, :, 1, :], x[:, :, 0, :], sin, ALU.mult))
                    V_.tensor_tensor(y[:, :, 0, :], xc[:, :, 0, :], xs[:, :, 0, :], ALU.subtract)
                    last = V_.tensor_tensor(y[:, :, 1, :], xc[:, :, 1, :], xs[:, :, 1, :], ALU.add)
                    if heads == SW_KV:
                        w.link(last)
                last.then_inc(S["rope_done"], 1)
                w.next(S["rope_done"])
            for h in range(SW_H):
                w.next(S["lg_psum"])
                ps_ = PS[:, 4:6, :].rearrange("p b (u c) -> p (b u) c", u=2)
                V_.memset(slg[:, 0, 0:P], NEG)
                V_.tensor_tensor(slg[:, 0, P:C], ps_[:, 0, P:C], swa[:, P:C], ALU.add)
                w.link(V_.tensor_tensor(slg[:, 1:NT], ps_[:, 1:NT, :], swa.unsqueeze(1).broadcast_to([P, NT - 1, C]), ALU.add))
                w.link(V_.tensor_reduce(nmax, slg[:, :, :], AX.X, ALU.max, negate=True))
                V_.tensor_scalar(nmax, nmax, nsink[:, h:h + 1], None, ALU.min).then_inc(S["lg_ready"], 1)
                w.next(S["p_exp"])
                w.link(V_.tensor_tensor(prec, psum_, esink, ALU.add))
                w.link(V_.reciprocal(prec, prec))
                V_.tensor_tensor(slg[:, :, :], slg[:, :, :], prec.unsqueeze(2).broadcast_to([P, NT, C]), ALU.mult).then_inc(S["p_norm"], 1)
            memory_attention(MEM_H, False)
            split_output(so, 3)
            split_output(mo, 1, at_=6)
            passed(4)
            residual(o_mix, 4)
            feed_forward(V_FFN1, 5)

        @block.gpsimd
        def _(pool):
            w = Waits(pool, S["pool_chain"])

            def gain(i):
                if i:
                    pool.wait_ge(S["x_new"], NT * i)
                pool.dma_start(gpost[:, :], gposts[i:i + 1, :].broadcast_to([P, D])).then_inc(S["gpost_loaded"], 16)

            gain(0)
            w.next(S["line_ready"])
            pool.dma_start(bass.AP(line.tensor, 0, [[LINE_HEAD, DSA_H], [LINE + 1, P], [1, 384]]),
                           linet[:, :].unsqueeze(1).broadcast_to([DSA_H, P, 384])).then_inc(S["line_stored"], 16)
            pool.wait_ge(S["line_stored"], 16)
            pool.dma_start(tbias[:, :, :], bass.AP(line.tensor, P - 1, [[LINE, P], [LINE_HEAD, DSA_H], [1, C]]))\
                .then_inc(S["tbias_loaded"], 16)
            for qt in range(1, NT):
                w.next(S["score_ready"])
                pool.affine_select(out=score[:, qt * P:qt * P + P], in_=score[:, qt * P:qt * P + P], pattern=[[-1, P]],
                                   compare_op=ALU.is_ge, fill=HIDDEN, base=0, channel_multiplier=1)\
                    .then_inc(S["score_masked"], 1)
            w.next(S["merged_ready"], 2)
            pool.dma_start(memx[:, :, :], mem_in.rearrange("(t p) d -> p t d", p=P)).then_inc(S["mem_loaded"], 16)
            gain(1)
            pool.dma_start(memx[:, :, :], mem2_in.rearrange("(t p) d -> p t d", p=P)).then_inc(S["mem_loaded"], 16)
            pool.dma_start(gmb[:, :], gmlb.broadcast_to([P, 768])).then_inc(S["gml_loaded"], 16)
            gain(2)
            gain(3)
            pool.dma_start(memx[:, :, :], mem2_in.rearrange("(t p) d -> p t d", p=P)).then_inc(S["mem_loaded"], 16)
            gain(4)

        @block.sync
        def _(sp):
            sp.dma_start(X[:, :, :], x_in.rearrange("(t p) d -> p t d", p=P)).then_inc(S["x_loaded"], 16)
            sp.dma_start(K[:, :], consts).then_inc(S["const_loaded"], 16)
            sp.dma_start(V[:, :], cols).then_inc(S["const_loaded"], 16)
            for p in range(2):
                sp.dma_start(raw[:, p], stream[0, p]).then_inc(raw_ready[p], 16)
            sp.dma_start(wup_s[:, :], wup[0:GLA_RANK, :]).then_inc(S["gate_w_loaded"], 16)
            sp.dma_start(ba_s[:, :], wup[GLA_RANK:GLA_RANK + 1, :]).then_inc(S["gate_w_loaded"], 16)
            sp.dma_start(posi, pos_in).then_inc(S["pos_loaded"], 16)
            with sp.Fori(1, NS // 2) as i:
                for p in range(2):
                    sp.wait_ge(lo_ready[p], i)
                    sp.dma_start(raw[:, p], stream[bass.ds(i, 1), p]).then_inc(raw_ready[p], 16)
            for t in range(NT):
                sp.wait_ge(S["x_new"], NT * 4 + t + 1)
                sp.dma_start(out[t * P:t * P + P, :], X[:, t, :]).then_inc(S["out_stored"], 16)
            sp.wait_ge(S["out_stored"], 16 * NT)



def t5_bucket(distance):
    exact = BUCKETS // 2
    if distance < exact:
        return max(distance, 0)
    return min(exact + int(math.log(distance / exact) / math.log(MAX_DIST / exact) * (BUCKETS - exact)), BUCKETS - 1)


def constants():
    a, b = np.arange(P)[:, None], np.arange(P)[None, :]
    k = np.zeros((P, K_ALL), np.float32)
    k[:, K_ID:K_ID + P] = a == b
    k[:, K_U64:K_U64 + P] = (a <= b) & (a // 64 == b // 64)
    k[:, K_U128:K_U128 + P] = a <= b
    k[:, K_ONE:K_ONE + P] = 1.0
    d = a + P - np.arange(C)[None, :]
    k[:, K_SWA:K_SWA + C] = np.where((d >= 0) & (d < P), 0.0, NEG)
    k[:, K_DCM:K_DCM + P] = np.where(b <= a, 0.0, NEG)
    k[:, K_LCM:K_LCM + P] = np.where(b >= a, 0.0, NEG)
    for i in range(384):
        k[t5_bucket(255 - i), K_HOT + i] += 1.0
        k[BUCKETS - 1, K_HOT + i] -= 1.0
    k[:, K_INV:K_INV + 32] = np.float32(1.0) / np.float32(10000.0) ** (np.arange(0, 64, 2, dtype=np.float32) / np.float32(64))
    k[:, K_EPS] = EPS
    return k


def kernel(**inputs):
    import concourse.bacc as bacc
    from concourse.bass_utils import run_bass_kernel_spmd

    a = {name: np.asarray(v) for name, v in inputs.items()}
    weights = {name: a[name][0] for name in
               ("w_in", "w_gla_out", "w_dsa_out", "w_x_out", "w_mem_kv", "w_o")}
    weights |= {"w_in_a": a["w_in_a_2"][0], "w_in_b": a["w_in_b_2"][0], "w_kv": a["w_kv_2"]}
    for layer in range(2):
        for name in ("w_mem_kv", "w_out", "w_ffn_in", "w_ffn_out"):
            weights[f"{name}_{layer}"] = a[f"{name}_2"][layer]
    stream = np.zeros((NS, P, KT, C), np.float32)
    for s, pieces in enumerate(slots()):
        for name, row, tiles, column, width, place in pieces:
            w = weights[name][row * P:(row + tiles) * P, column:column + width]
            stream[s, :, 0:tiles, place:place + width] = w.reshape(tiles, P, width).transpose(1, 0, 2)

    cols = np.zeros((P, V_COLS), np.float32)
    for at, v in ((V_PRE, a["g_pre"][0]), (V_MEM, a["g_mem"][0]), (V_GLA, a["g_gla"][0]),
                  (V_MIX0, a["g_mix_pre_2"][0]), (V_FFN0, a["g_ffn_pre_2"][0]), (V_KV, a["g_kv_2"]),
                  (V_MIX1, a["g_mix_pre_2"][1]), (V_FFN1, a["g_ffn_pre_2"][1]),
                  (V_MEM0, a["g_mem_2"][0]), (V_MEM1, a["g_mem_2"][1])):
        cols[:, at:at + v.size // P] = v.reshape(-1, P).T
    cols[:, V_BG:V_BG + 8] = a["b_gates_a_2"][0]
    cols[:, V_SINK:V_SINK + SW_H] = a["sinks_b_2"][0]
    cols[0:BUCKETS, V_ALL:V_COLS] = a["rel_bias"]

    arrays = {
        "stream": stream.reshape(NS // 2, 2, P, KT * C),
        "x": a["x"][0], "mem": a["mem"][0], "mem2": a["mem_2"][0],
        "consts": constants(), "cols": cols,
        "gposts": np.stack([a["g_post"][0], a["g_mix_post_2"][0], a["g_ffn_post_2"][0],
                            a["g_mix_post_2"][1], a["g_ffn_post_2"][1]]),
        "wup": np.concatenate([a["w_gla_a_up"][0], a["b_gla_a"]]),
        "gml": a["g_mlstm_out_2"],
        "positions": np.ascontiguousarray(a["positions_2"].reshape(NT, P).T),
    }
    arrays = {name: np.ascontiguousarray(v) for name, v in arrays.items()}
    nc = bacc.Bacc("TRN2", target_bir_lowering=False, num_devices=1)
    t = {name: nc.dram_tensor(f"in_{name}", v.shape, mybir.dt.from_np(v.dtype), kind="ExternalInput").ap()
         for name, v in arrays.items()}
    line = nc.dram_tensor("bias_line", (DSA_H, LINE_HEAD), F32, kind="Internal").ap()
    out = nc.dram_tensor("out", (T, D), F32, kind="ExternalOutput").ap()
    build(nc, t["stream"], t["x"], t["mem"], t["mem2"], t["consts"], t["cols"], t["gposts"], t["wup"], t["gml"],
          t["positions"], line, out)
    r = run_bass_kernel_spmd(nc, [{f"in_{name}": v for name, v in arrays.items()}], core_ids=[0])
    return r.results[0]["out"].reshape(1, T, D)
```

```python
import math
from contextlib import ExitStack

import numpy as np

import concourse.bass as bass
from concourse import mybir

F32 = mybir.dt.float32
F32R = mybir.dt.float32r
I32 = mybir.dt.int32
U32 = mybir.dt.uint32
ALU = mybir.AluOpType
ACT = mybir.ActivationFunctionType
AX = mybir.AxisListType

P = 128
D = 1024
T = 512
NT = T // P
KT = D // P
C = 256
M = 256
EPS = 1e-6
NEG = -1e30

GLA_H, GLA_DK, GLA_DV, GLA_RANK, GLA_NORM = 4, 128, 256, 16, 16.0
DSA_H, DSA_KV, DSA_HD = 8, 2, 128
IDX_H, IDX_D, TOPK = 8, 64, 128
BUCKETS, MAX_DIST = 32, 128
X_H, X_HD = 4, 256
ML_H, ML_DK, ML_DV = 4, 96, 192
SOFTCAP = 15.0
SW_H, SW_KV, SW_HD = 12, 4, 64
MEM_H, MEM_HD = 4, 64
FF = 2816
FFT = FF // P

MASK_COLS = (256, 384, 512)

TAKEN = -3.4e38
HIDDEN = -3.3e38

O_GQ, O_GK, O_GV, O_GA, O_GZ = 0, 512, 1024, 2048, 2064
O_DQ, O_DK, O_DV, O_IQ, O_IK, O_IW, O_DZ = 3088, 4112, 4368, 4624, 5136, 5200, 5208
O_XQ, O_XZ, O_GATES = 6232, 7256, 8280

K_ID, K_U64, K_U128, K_ONE, K_SWA, K_DCM, K_LCM, K_HOT, K_INV, K_EPS = (
    0, 128, 256, 384, 512, 768, 896, 1024, 1408, 1440)
K_ALL = 1441

V_PRE, V_MEM, V_GLA, V_MIX0, V_FFN0, V_KV, V_MIX1, V_FFN1, V_MEM0, V_MEM1 = (
    0, 8, 16, 18, 26, 34, 42, 50, 58, 66)
V_RB31, V_BG, V_SINK = 74, 82, 90
V_ALL = 102
V_COLS = V_ALL + DSA_H

LINE = 512
LINE_HEAD = (LINE + 1) * P

TURN = (6.28125, 0.0019350051879882812, 3.0199159795074593e-07)
PI_IN = 3.1415925


def swa_columns():
    order = []
    for block in range(SW_H // 2):
        for half in range(2):
            order.append(6 * (block // 3) + 3 * half + block % 3)
    return order


SWA_ORDER = swa_columns()


def slots():
    out = []

    def full(w, col, r0=0, rt=KT, n=C):
        out.append([(w, r0, rt, col, n, 0)])

    def run(w, col, n, **k):
        for c in range(0, n, C):
            full(w, col + c, **k)

    out.append([("w_in", 0, KT, O_IK, 64, 0), ("w_in", 0, KT, O_IK, 64, 64),
                ("w_in", 0, KT, O_GA, 16, 128), ("w_in", 0, KT, O_IW, 8, 144)])
    run("w_in", O_IQ, 512)
    run("w_in", O_GQ, 512)
    run("w_in", O_GK, 512)
    run("w_in", O_GV, 1024)
    run("w_in", O_GZ, 1024)
    for c in range(4):
        full("w_in", O_GATES + C * c)
        full("w_gla_out", C * c)
    run("w_in", O_DQ, 1024)
    run("w_in", O_DK, 256)
    run("w_in", O_DV, 256)
    run("w_in", O_DZ, 1024)
    for c in range(4):
        full("w_in", O_GATES + D + C * c)
        full("w_dsa_out", C * c)
    run("w_mem_kv", 0, 2048)
    run("w_in", O_XQ, 1024)
    run("w_in", O_XZ, 1024)
    for c in range(4):
        full("w_in", O_GATES + 2 * D + C * c)
        full("w_x_out", C * c)
    run("w_o", 0, 1024)
    for layer in range(2):
        if layer == 0:
            for c in range(8):
                full("w_in_a", 192 * c, n=192)
            run("w_in_a", 1536, 768)
            full("w_in_a", 2304, n=8)
            full("w_in_a", 2312)
        else:
            full("w_kv", 0)
            full("w_kv", 256)
            for c in range(3):
                out.append([("w_in_b", 0, KT, 64 * SWA_ORDER[4 * c + i], 64, 64 * i) for i in range(4)])
            full("w_in_b", 768)
        for c in range(2):
            full(f"w_mem_kv_{layer}", C * c)
        run(f"w_out_{layer}", 0, 1024)
        for c in range(FF // C):
            full(f"w_ffn_in_{layer}", C * c)
            full(f"w_ffn_in_{layer}", FF + C * c)
        for c in range(4):
            for r in range(0, FFT, KT):
                full(f"w_ffn_out_{layer}", C * c, r0=r, rt=min(KT, FFT - r))
    return out


NS = len(slots())


class Waits:

    def __init__(self, eng, chain):
        self.eng, self.chain, self.at, self.links = eng, chain, {}, 0

    def next(self, sem, by=1):
        self.at[sem.name] = self.at.get(sem.name, 0) + by
        self.eng.wait_ge(sem, self.at[sem.name])

    def link(self, instruction):
        self.links += 1
        instruction.then_inc(self.chain, 1)
        self.eng.wait_ge(self.chain, self.links)


def build(nc, stream, x_in, mem_in, mem2_in, consts, cols, gposts, wup, gmlb, pos_in, line, out):
    ctx = ExitStack()
    with ctx:
        def sb(name, shape, dt=F32):
            return ctx.enter_context(nc.sbuf_tensor(name, shape, dt))

        def region(name, kbytes):
            base = ctx.enter_context(ExitStack())

            def place(tensor, at, shape, dt=F32):
                with ExitStack() as inner:
                    if at:
                        inner.enter_context(nc.sbuf_tensor(f"before_{tensor}", [P, int(at * 256)], F32))
                    return inner.enter_context(nc.sbuf_tensor(tensor, shape, dt))

            def close():
                base.enter_context(nc.sbuf_tensor(name, [P, kbytes * 256], F32))
            return place, close

        raw = sb("raw", [P, 2, KT, C])
        whi = sb("whi", [P, 2, KT, C], F32R)
        wlo = sb("wlo", [P, 2, KT, C], F32R)
        K = sb("K", [P, K_ALL])
        V = sb("V", [P, V_COLS])
        gpost = sb("gpost", [P, D])
        small = sb("small", [P, 512])

        place, close = region("H", 32)
        hhi = place("hhi", 0, [P, KT, T], F32R)
        hlo = place("hlo", 16, [P, KT, T], F32R)
        o_ffn = place("o_ffn", 0, [P, NT, D])
        hm = place("hm", 0, [P, NT, ML_H, ML_DV])
        xp2 = place("xp2", 16, [P, 2, NT, M])
        xpt2 = place("xpt2", 24, [P, 2, T])
        mo = place("mo", 28, [P, 2, T])
        close()

        place, close = region("XR", 16)
        X = place("X", 0, [P, NT, D])
        maskt = place("maskt", 0, [P, sum(MASK_COLS)])
        close()

        place, close = region("R", 99)
        yhi = place("yhi", 0, [P, KT, T], F32R)
        ylo = place("ylo", 16, [P, KT, T], F32R)
        merged = place("merged", 32, [P, KT, T])
        xn = place("xn", 64, [P, NT, D])
        o_mix = place("o_mix", 48, [P, NT, D])
        ztmp = place("ztmp", 48, [P, 2, T])
        gsig = place("gsig", 52, [P, 2, T])
        gprod = place("gprod", 56, [P, 2, T])
        ikT = place("ikT", 96, [P, T])
        iq = place("iq", 32, [P, 4, T])
        relu = place("relu", 40, [P, 4, T])
        gq = place("gq", 48, [P, GLA_H, T])
        gk = place("gk", 56, [P, GLA_H, T])
        gv = place("gv", 64, [P, NT, D])
        go = place("go", 80, [P, KT, T])
        spT = place("spT", 80, [P, T])
        la = place("la", 0, [P, NT, 512])
        gkt = place("gkt", 8, [P, GLA_H, T])
        S_t = place("S_t", 0, [P, 4, GLA_H, GLA_DV])
        gktok = place("gktok", 16, [P, NT, 512])
        attm = place("attm", 24, [P, GLA_H, P])
        lscr = place("lscr", 16, [P, NT, 512])
        gsq = place("gsq", 48, [P, KT, T])
        ge = place("ge", 26, [P, 3, T])
        wup_s = place("wup_s", 26, [GLA_RANK, 512])
        ba_s = place("ba_s", 28, [1, 512])
        dq = place("dq", 48, [P, DSA_H, T])
        dk = place("dk", 64, [P, DSA_KV, T])
        dv = place("dv", 68, [P, NT, C])
        do = place("do", 80, [P, DSA_H, T])
        tbias = place("tbias", 0, [P, DSA_H, C])
        pt = place("pt", 12, [P, 2, NT, P])
        lg = place("lg", 20, [P, 2, 2, T])
        linet = place("linet", 28, [DSA_H, 384])
        xq = place("xq", 48, [P, 8, T])
        mk = place("mk", 64, [P, 8, M])
        mv = place("mv", 72, [P, 2, D])
        xo = place("xo", 80, [P, 8, T])
        memx = place("memx", 0, [P, 2, D])
        mhi = place("mhi", 8, [P, KT, M], F32R)
        mlo = place("mlo", 16, [P, KT, M], F32R)
        memn = place("memn", 24, [P, 2, D])
        xp = place("xp", 0, [P, 2, NT, M])
        xpt = place("xpt", 8, [P, 2, T])
        mk2 = place("mk2", 77, [P, 2, M])
        mv2 = place("mv2", 79, [P, 2, M])
        lq = place("lq", 32, [P, ML_H, T])
        lk = place("lk", 40, [P, ML_H, T])
        lv = place("lv", 48, [P, NT, ML_H, ML_DV + 1])
        lo = place("lo", 61, [P, NT, 768])
        mq = place("mq", 73, [P, 2, T])
        gT = place("gT", 81, [P, T])
        lw = place("lw", 81, [P, T])
        Lb = place("Lb", 83, [P, ML_H, T])
        at = place("at", 8, [P, 2, NT, T])
        ljunk = place("ljunk", 94, [P, ML_DV])
        gmb = place("gmb", 91, [P, 768])
        sk = place("sk", 32, [P, NT, C])
        sv = place("sv", 36, [P, NT, C])
        sq = place("sq", 40, [P, NT, 768])
        qrT = place("qrT", 40, [P, 6, T])
        mqb = place("mqb", 52, [P, 2, T])
        ra = place("ra", 56, [P, 768])
        rb = place("rb", 59, [P, 768])
        sqr = place("sqr", 62, [P, NT, 768])
        so = place("so", 62, [P, 6, T])
        skr = place("skr", 81, [P, NT, C])
        krT = place("krT", 85, [P, 2, T])
        slg = place("slg", 89, [P, 2, NT, C])
        spt = place("spt", 81, [P, 7, P])
        cs = place("cs", 97, [P, 2, NT, 32])
        ahi = place("ahi", 0, [P, FFT, T], F32R)
        alo = place("alo", 44, [P, FFT, T], F32R)
        fa = place("fa", 88, [P, 2, T])
        fs = place("fs", 92, [P, 2, T])
        close()

        PS = ctx.enter_context(nc.psum_tensor("PS", [P, 8, 512], F32))

        def col(tensor, a, n=1):
            return tensor[:, a:a + n]

        ident = K[:, K_ID:K_ID + P]
        u64 = K[:, K_U64:K_U64 + P]
        u128 = K[:, K_U128:K_U128 + P]
        ones = K[:, K_ONE:K_ONE + P]
        swa = K[:, K_SWA:K_SWA + C]
        dcm = K[:, K_DCM:K_DCM + P]
        lcm = K[:, K_LCM:K_LCM + P]
        hot = K[0:BUCKETS, K_HOT:K_HOT + 384]
        inv = K[:, K_INV:K_INV + 32]
        relb_v = V[0:BUCKETS, V_ALL:V_COLS]
        epsc = K[:, K_EPS:K_EPS + 1]

        ss = small[:, 0:16]
        root = small[:, 16:32]
        rstd = small[:, 32:48]
        iwt = small[:, 48:80].rearrange("p (t h) -> p t h", t=NT)
        nmax = small[:, 80:88].rearrange("p (b t) -> p b t", b=2)
        psum_ = small[:, 340:348].rearrange("p (b t) -> p b t", b=2)
        prec = small[:, 360:368].rearrange("p (b t) -> p b t", b=2)
        top8 = small[:, 96:104]
        dec = small[:, 104:136].rearrange("p (h c) -> p h c", h=GLA_H)
        lgt = small[:, 136:168].rearrange("p (t g) -> p t g", t=NT)
        lex = small[:, 184:200].rearrange("p (t h) -> p t h", t=NT)
        lgf = small[:, 200:216].rearrange("p (t h) -> p t h", t=NT)
        bi = small[:, 216:280].rearrange("p (s j h) -> p s j h", s=4, j=4)
        rstd16 = small[:, 280:296]
        nsink = small[:, 296:308]
        esink = small[:, 352:360].rearrange("p (b t) -> p b t", b=2)
        posf = small[:, 312:316]
        posi = small[:, 316:320].bitcast(I32)
        lden = small[:, 320:324]
        blast = small[:, 324:332]

        def seen(qt):
            return maskt[:, sum(MASK_COLS[:qt - 1]):sum(MASK_COLS[:qt])]

        def score_bank(h, s):
            bank, at_ = ((0, 0), (1, 0), (2, 0), (1, 384))[s]
            return PS[:, 3 * (h % 2) + bank, at_:at_ + T - s * P]

        S = {}

        def sem(name):
            S[name] = ctx.enter_context(nc.semaphore(name))
            return S[name]

        raw_ready = [sem(f"raw_ready{p}") for p in range(2)]
        hi_ready = [sem(f"hi_ready{p}") for p in range(2)]
        lo_ready = [sem(f"lo_ready{p}") for p in range(2)]
        slot_used = [sem(f"slot_used{p}") for p in range(2)]
        pair_free = [sem(f"pair_free{p}") for p in range(2)]
        for name in """x_loaded const_loaded gate_w_loaded gpost_loaded gpost_used gml_loaded
                out_stored norm_root xn_ready norm_turned hhi_ready hlo_ready act_chain dve_chain
                pool_chain z_silu z_prod y_hi y_lo g_sig merged_hi merged_ready
                special_ready iw_turned la_abs la_psum la_exp la_ready b_psum eb_ready ediff_ready ekt_ready
                gk_ready gkt_ready kt_turned kt_copied att_psum att_ready gla_upd S_ready
                go_psum go_copied sq_ready ssq_psum gla_root gla_rstd rs_psum go_ready
                store_act store_dve mem_loaded
                rel_loaded line_psum line_ready line_stored tbias_loaded idx_psum relu_ready relu_used
                score_masked lg_psum lg_ready p_exp p_norm p_turned pt_ready
                pv_psum o_copied o_sq o_root x_new
                gt_ready gt_turned gate_soft gate_abs gate_exp logf_ready cl_psum bi_ready lb_psum lb_ready
                lsc_psum lw_arg lw_exp at_ready num_psum hm_ready hm_sq hm_root hm_done hm_turned
                mem_first rope_arg rope_sin rope_done rope_turned rot_copied ffn_silu ffn_a ffn_hi ffn_lo
                ffo_free ones_ready pos_loaded x_again""".split():
            sem(name)

        block = ctx.enter_context(nc.Block())

        @block.tensor
        def _(pe):
            w = Waits(pe, S["pool_chain"])
            n = m = 0

            def three(out, k, n_k, lhs, rhs):
                (lh, ll), (rh, rl) = lhs, rhs
                nc.tensor.matmul(out, lh, rh, start=(k == 0), stop=False)
                nc.tensor.matmul(out, lh, rl, start=False, stop=False)
                return nc.tensor.matmul(out, ll, rh, start=False, stop=(k == n_k - 1))

            def slot_begin():
                pe.wait_ge(lo_ready[n % 2], n // 2 + 1)
                if m >= 2:
                    pe.wait_ge(pair_free[m % 2], m // 2)

            def gemm_features(hi, lo, groups=(0, P), tokens=T):
                nonlocal n, m
                slot_begin()
                p = n % 2
                for g, c in enumerate(groups):
                    for k in range(KT):
                        last = three(PS[:, 2 * (m % 2) + g, 0:tokens], k, KT,
                                     (whi[:, p, k, c:c + P], wlo[:, p, k, c:c + P]), (hi[:, k, :], lo[:, k, :]))
                last.then_inc(slot_used[p], 1)
                n, m = n + 1, m + 1

            def gemm_tokens(hi, lo, width=C, tiles=NT):
                nonlocal n, m
                slot_begin()
                p = n % 2
                for t in range(tiles):
                    out_ = PS[:, 2 * (m % 2) + t // 2, (t % 2) * C:(t % 2) * C + width]
                    for k in range(KT):
                        last = three(out_, k, KT, (hi[:, k, t * P:t * P + P], lo[:, k, t * P:t * P + P]),
                                     (whi[:, p, k, 0:width], wlo[:, p, k, 0:width]))
                last.then_inc(slot_used[p], 1)
                n, m = n + 1, m + 1

            def stored():
                for b in range(2):
                    pe.wait_ge(pair_free[b], (m + 1 - b) // 2)

            def turn_normed(src, tiles, again=False):
                for k in range(KT):
                    if k >= 4:
                        w.next(S["hlo_ready"])
                    for t in range(tiles):
                        if k == 0 and not again:
                            w.next(S["xn_ready"])
                        last = nc.tensor.transpose(PS[:, 4 + k % 4, t * P:t * P + P],
                                                   src[:, t, k * P:k * P + P], ident)
                    last.then_inc(S["norm_turned"], 1)
                w.next(S["hlo_ready"], 4)

            def attention(units, logits, turn, values):
                for u in range(-2, units):
                    if u >= 0:
                        w.next(S["p_norm"])
                        turn(u).then_inc(S["p_turned"], 1)
                    if u + 2 < units:
                        logits(u + 2, 2 * (u % 2)).then_inc(S["lg_psum"], 1)
                    if u >= 0:
                        w.next(S["pt_ready"])
                        if u:
                            w.next(S["o_copied"])
                        values(u).then_inc(S["pv_psum"], 1)
                w.next(S["o_copied"])

            def memory_attention(heads, parts, values_, cross):
                p_, pt_ = (xp, xpt) if cross else (xp2, xpt2)

                def logits(h, b):
                    ps_ = parts(h)
                    for t in range(NT):
                        for i, (q_, k_, (rows, kt)) in enumerate(ps_):
                            last = nc.tensor.matmul(PS[:, b + t // 2, (t % 2) * C:(t % 2) * C + M],
                                                    q_[rows, kt, t * P:t * P + P], k_[rows, kt, :],
                                                    start=(i == 0), stop=(i == len(ps_) - 1))
                    return last

                def turn(h):
                    for j in range(2):
                        for t in range(NT):
                            last = nc.tensor.transpose(PS[:, 4 + j, t * P:t * P + P], p_[:, h % 2, t, j * P:j * P + P], ident)
                    return last

                def values(h):
                    for v in range(2 if cross else 1):
                        for j in range(2):
                            if cross:
                                last = nc.tensor.matmul(PS[:, 6 + v, :], values_[:, j, h * X_HD + v * P:h * X_HD + v * P + P],
                                                        pt_[:, j, :], start=(j == 0), stop=(j == 1))
                            else:
                                r = MEM_HD * (h % 2)
                                last = nc.tensor.matmul(PS[r:r + MEM_HD, 6, :], values_[:, j, h * MEM_HD:h * MEM_HD + MEM_HD],
                                                        pt_[:, j, :], start=(j == 0), stop=(j == 1))
                    return last

                attention(heads, logits, turn, values)

            def index_scores(qt, half):
                for h in range(4 * half, 4 * half + 4):
                    if qt > 1 or half:
                        w.next(S["relu_ready"])
                    r = slice(IDX_D * (h % 2), IDX_D * (h % 2) + IDX_D)
                    nc.tensor.matmul(PS[:, 4 + h % 4, 0:(qt + 1) * P], iq[r, h // 2, qt * P:qt * P + P], ikT[r, 0:(qt + 1) * P],
                                     start=True, stop=True).then_inc(S["idx_psum"], 1)

            def z_and_merge():
                for c in range(4):
                    gemm_features(hhi, hlo)
                w.next(S["y_lo"], 4)
                for c in range(4):
                    gemm_features(hhi, hlo)
                    gemm_features(yhi, ylo)

            pe.wait_ge(S["const_loaded"], 32)
            turn_normed(xn, NT)
            gemm_features(hhi, hlo)
            for c in range(2):
                gemm_features(hhi, hlo)
            stored()
            for t in range(NT):
                last = nc.tensor.transpose(PS[:, 4, t * 32:t * 32 + 32], spT[0:32, t * P:t * P + P], ident[0:32, 0:32])
            last.then_inc(S["iw_turned"], 1)
            w.next(S["special_ready"])
            for c in range(4):
                gemm_features(hhi, hlo)
                index_scores(1 + c // 2, c % 2)
            for c in range(4):
                gemm_tokens(hhi, hlo)
                if c < 2:
                    index_scores(3, c)
            w.next(S["relu_ready"], 4)

            stored()
            pe.wait_ge(S["gate_w_loaded"], 32)
            for t in range(NT):
                nc.tensor.matmul(PS[:, 4 + t, :], spT[0:GLA_RANK, t * P:t * P + P], wup_s[:, :], start=True, stop=False)
                last = nc.tensor.matmul(PS[:, 4 + t, :], ones[0:1, :], ba_s[:, :], start=False, stop=True)
            last.then_inc(S["la_psum"], 1)
            w.next(S["la_ready"])
            for h in range(GLA_H):
                for t in range(NT):
                    last = nc.tensor.matmul(PS[:, 4 + h, t * P:t * P + P], la[:, t, h * P:h * P + P], u64, start=True, stop=True)
                last.then_inc(S["b_psum"], 1)
            for h in range(GLA_H):
                w.next(S["gk_ready"])
                for t in range(NT):
                    last = nc.tensor.transpose(PS[:, 4 + h, t * P:t * P + P], gkt[:, h, t * P:t * P + P], ident)
                last.then_inc(S["kt_turned"], 1)
            w.next(S["kt_copied"], GLA_H)
            for t in range(NT):
                tk = slice(t * P, t * P + P)
                if t:
                    w.next(S["go_copied"])
                for h in range(GLA_H):
                    last = nc.tensor.matmul(PS[:, 4, h * P:h * P + P], gk[:, h, tk], gq[:, h, tk], start=True, stop=True)
                last.then_inc(S["att_psum"], 1)
                for j in range(2):
                    c = 2 * t + j
                    if c == 2 * NT - 1:
                        break
                    if c:
                        w.next(S["S_ready"])
                    r = slice(64 * j, 64 * j + 64)
                    for h in range(GLA_H):
                        last = nc.tensor.matmul(PS[:, 5 + h // 2, (h % 2) * C:(h % 2) * C + GLA_DV],
                                                gktok[r, t, h * P:h * P + P], gv[r, t, h * GLA_DV:(h + 1) * GLA_DV],
                                                start=True, stop=True)
                    last.then_inc(S["gla_upd"], 1)
                w.next(S["att_ready"])
                if t == NT - 1:
                    w.next(S["S_ready"])
                for h in range(GLA_H):
                    for v in range(2):
                        i = (h % 2) * 2 + v
                        vc = slice(h * GLA_DV + v * P, h * GLA_DV + v * P + P)
                        bank = 4 if h < 2 else 7
                        nc.tensor.matmul(PS[:, bank, i * P:i * P + P], gv[:, t, vc], attm[:, h, :], start=True, stop=False)
                        if t:
                            nc.tensor.matmul(PS[:, bank, i * P:i * P + 64], S_t[:, (2 * t) % 4, h, v * P:v * P + P],
                                             gq[:, h, t * P:t * P + 64], start=False, stop=False)
                        last = nc.tensor.matmul(PS[:, bank, i * P + 64:i * P + P], S_t[:, (2 * t + 1) % 4, h, v * P:v * P + P],
                                                gq[:, h, t * P + 64:t * P + P], start=False, stop=True)
                last.then_inc(S["go_psum"], 1)
            w.next(S["go_copied"])
            w.next(S["sq_ready"])
            for t in range(NT):
                for h in range(GLA_H):
                    for v in range(2):
                        last = nc.tensor.matmul(PS[:, 4, 4 * t + h:4 * t + h + 1], gsq[:, 2 * h + v, t * P:t * P + P],
                                                ones[:, 0:1], start=(v == 0), stop=(v == 1))
            last.then_inc(S["ssq_psum"], 1)
            w.next(S["gla_rstd"])
            for h in range(GLA_H):
                for t in range(NT):
                    last = nc.tensor.matmul(PS[:, 4 + h, t * P:t * P + P],
                                            rstd16[:, 4 * t + h:4 * t + h + 1].broadcast_to([P, P]), ident, start=True, stop=True)
            last.then_inc(S["rs_psum"], 1)
            z_and_merge()

            for c in range(5):
                gemm_features(hhi, hlo)
            gemm_tokens(hhi, hlo)
            nc.tensor.matmul(PS[0:DSA_H, 4, 0:384], relb_v, hot, start=True, stop=True).then_inc(S["line_psum"], 1)
            stored()
            w.next(S["line_ready"])

            def logits(u, b):
                qt, heads = u // 4, 2 * (u % 4)
                for i in range(2):
                    last = nc.tensor.matmul(PS[:, b + i, 0:(qt + 1) * P], dq[:, heads + i, qt * P:qt * P + P],
                                            dk[:, heads // 4, 0:(qt + 1) * P], start=True, stop=True)
                return last

            def turn(u):
                for i in range(2):
                    for b in range(u // 4 + 1):
                        last = nc.tensor.transpose(PS[:, 4 + i, b * P:b * P + P], lg[:, u % 2, i, b * P:b * P + P], ident)
                return last

            def values(u):
                qt, kv = u // 4, u % 4 // 2
                for i in range(2):
                    for b in range(qt + 1):
                        last = nc.tensor.matmul(PS[:, 6, i * P:i * P + P], dv[:, b, kv * P:kv * P + P], pt[:, i, b, :],
                                                start=(b == 0), stop=(b == qt))
                return last

            attention(4 * NT, logits, turn, values)
            z_and_merge()

            turn_normed(memn, 2)
            for c in range(4):
                gemm_features(mhi, mlo, tokens=M)
            for c in range(4):
                gemm_tokens(mhi, mlo, tiles=2)
            for c in range(4):
                gemm_features(hhi, hlo)
            stored()
            memory_attention(X_H, lambda h: [(xq, mk, (slice(0, P), 2 * h + i)) for i in range(2)], mv, True)
            z_and_merge()
            w.next(S["y_lo"], 4)
            for c in range(4):
                gemm_tokens(yhi, ylo)

            def feed_forward():
                nonlocal n, m
                turn_normed(xn, NT)
                k0, m0 = n // 2, m // 2
                a, b = n % 2, (n + 1) % 2
                ga, gb = m % 2, (m + 1) % 2
                ka, kb = n // 2, (n + 1) // 2
                ma, mb = m // 2, (m + 1) // 2
                with pe.Fori(0, FFT // 2) as i:
                    for p, g, kk, mm in ((a, ga, ka, ma), (b, gb, kb, mb)):
                        pe.wait_ge(lo_ready[p], i + (kk + 1))
                        pe.wait_ge(pair_free[g], i + mm)
                        for j in range(2):
                            for k in range(KT):
                                last = three(PS[:, 2 * g + j, :], k, KT,
                                             (whi[:, p, k, j * P:j * P + P], wlo[:, p, k, j * P:j * P + P]),
                                             (hhi[:, k, :], hlo[:, k, :]))
                        last.then_inc(slot_used[p], 1)
                n, m = n + FFT, m + FFT
                w.next(S["ffn_lo"], FFT // 2)
                stored()
                for c in range(4):
                    if c >= 2:
                        w.next(S["ffo_free"])
                    for r in range(0, FFT, KT):
                        pe.wait_ge(lo_ready[n % 2], n // 2 + 1)
                        p = n % 2
                        rows = min(KT, FFT - r)
                        for t in range(NT):
                            for k in range(rows):
                                last = three(PS[:, 4 * (c % 2) + t, 0:C], r + k, FFT,
                                             (ahi[:, r + k, t * P:t * P + P], alo[:, r + k, t * P:t * P + P]),
                                             (whi[:, p, k, :], wlo[:, p, k, :]))
                        last.then_inc(slot_used[p], 1)
                        n += 1
                w.next(S["ffo_free"], 2)

            def memory_parts(q_):
                return lambda h: [(q_, mk2, (slice(MEM_HD * (h % 2), MEM_HD * (h % 2) + MEM_HD), h // 2))]

            turn_normed(xn, NT)
            for c in range(4):
                gemm_features(hhi, hlo, groups=(0, ML_DK))
            for c in range(4):
                gemm_tokens(hhi, hlo, width=ML_DV)
            for c in range(3):
                gemm_tokens(hhi, hlo)
            gemm_features(hhi, hlo, groups=(0,))
            gemm_features(hhi, hlo)
            turn_normed(memn, 2)
            gemm_features(mhi, mlo, tokens=M)
            gemm_tokens(mhi, mlo, tiles=2)
            stored()
            for t in range(NT):
                last = nc.tensor.transpose(PS[:, 4, t * 8:t * 8 + 8], gT[0:8, t * P:t * P + P], ident[0:8, 0:8])
            last.then_inc(S["gt_turned"], 1)
            w.next(S["logf_ready"])
            nc.tensor.matmul(PS[:, 4, 0:16], u128, small[:, 200:216], start=True, stop=True).then_inc(S["cl_psum"], 1)
            w.next(S["bi_ready"])
            for h in range(ML_H):
                for t in range(NT):
                    last = nc.tensor.matmul(PS[:, 4 + h, t * P:t * P + P], lgf[:, t, h:h + 1].broadcast_to([P, P]), u128,
                                            start=True, stop=True)
            last.then_inc(S["lb_psum"], 1)
            w.next(S["lb_ready"])
            for h in range(-1, ML_H):
                if h + 1 < ML_H:
                    for s in range(NT):
                        last = nc.tensor.matmul(score_bank(h + 1, s), lk[0:ML_DK, h + 1, s * P:s * P + P], lq[0:ML_DK, h + 1, s * P:T],
                                                start=True, stop=True)
                    last.then_inc(S["lsc_psum"], 1)
                if h >= 0:
                    w.next(S["at_ready"])
                    if h:
                        w.next(S["hm_ready"])
                    for t in range(NT):
                        for s in range(t + 1):
                            last = nc.tensor.matmul(PS[:, 6 + t // 2, (t % 2) * C:(t % 2) * C + ML_DV + 1],
                                                    at[:, h % 2, s, t * P:t * P + P], lv[:, s, h, :], start=(s == 0), stop=(s == t))
                    last.then_inc(S["num_psum"], 1)
            w.next(S["hm_ready"])
            memory_attention(MEM_H, memory_parts(mq), mv2, False)
            for k in range(6):
                if k >= 4:
                    w.next(S["y_lo"])
                for t in range(NT):
                    if k == 0:
                        w.next(S["hm_done"])
                    last = nc.tensor.transpose(PS[:, 4 + k % 4, t * P:t * P + P],
                                               hm[:, t].rearrange("p h d -> p (h d)")[:, k * P:k * P + P], ident)
                last.then_inc(S["hm_turned"], 1)
            w.next(S["y_lo"], 5)
            for c in range(4):
                gemm_tokens(yhi, ylo)
            feed_forward()

            turn_normed(xn, NT)
            gemm_tokens(hhi, hlo)
            gemm_tokens(hhi, hlo)
            turn_normed(xn, NT, again=True)
            for c in range(3):
                gemm_tokens(hhi, hlo)
            gemm_features(hhi, hlo)
            turn_normed(memn, 2)
            gemm_features(mhi, mlo, tokens=M)
            gemm_tokens(mhi, mlo, tiles=2)
            stored()
            for b in range(8):
                if b >= 4:
                    w.next(S["rot_copied"])
                for t in range(NT):
                    if b == 0:
                        w.next(S["rope_done"])
                    src = skr[:, t, b * P:b * P + P] if b < 2 else sqr[:, t, (b - 2) * P:(b - 1) * P]
                    last = nc.tensor.transpose(PS[:, 4 + b % 4, t * P:t * P + P], src, ident)
                last.then_inc(S["rope_turned"], 1)
            w.next(S["rot_copied"], 4)
            def logits(h, bank):
                place_, kv = SWA_ORDER.index(h), h // 3
                r = slice(SW_HD * (kv % 2), SW_HD * (kv % 2) + SW_HD)
                for t in range(NT):
                    k0 = max(t - 1, 0) * P
                    o0 = 0 if t else P
                    last = nc.tensor.matmul(PS[:, bank + t // 2, (t % 2) * C + o0:(t % 2) * C + C],
                                            qrT[r, place_ // 2, t * P:t * P + P], krT[r, kv // 2, k0:t * P + P], start=True, stop=True)
                return last

            def turn(h):
                for j in range(7):
                    t, b = (j + 1) // 2, (j + 1) % 2
                    last = nc.tensor.transpose(PS[:, 4 + j // 4, (j % 4) * P:(j % 4) * P + P], slg[:, h % 2, t, b * P:b * P + P], ident)
                return last

            def values(h):
                kv = h // 3
                ro = slice(SW_HD * (h % 2), SW_HD * (h % 2) + SW_HD)
                for t in range(NT):
                    for b in range(0 if t else 1, 2):
                        last = nc.tensor.matmul(PS[ro, 6, t * P:t * P + P], sv[:, t + b - 1, kv * SW_HD:(kv + 1) * SW_HD],
                                                spt[:, 2 * t + b - 1, :], start=(b == (0 if t else 1)), stop=(b == 1))
                return last

            attention(SW_H, logits, turn, values)
            memory_attention(MEM_H, memory_parts(mqb), mv2, False)
            w.next(S["y_lo"], 4)
            for c in range(4):
                gemm_tokens(yhi, ylo)
            feed_forward()
            assert n == NS

        @block.scalar
        def _(act):
            w = Waits(act, S["act_chain"])
            n = m = 0

            def copy(out_, in_, scale=1.0, func=ACT.Copy):
                return nc.scalar.activation(out_, in_, func, scale=scale)

            def split(s):
                if s < NS:
                    act.wait_ge(raw_ready[s % 2], 16 * (s // 2 + 1))
                    if s >= 2:
                        act.wait_ge(slot_used[s % 2], s // 2)
                    copy(whi[:, s % 2], raw[:, s % 2]).then_inc(hi_ready[s % 2], 1)

            def pair():
                return PS[:, 2 * (m % 2):2 * (m % 2) + 2, :]

            def pair_tokens():
                return pair().rearrange("p b (u c) -> p (b u) c", u=2)

            def taken(instruction):
                nonlocal n, m
                instruction.then_inc(pair_free[m % 2], 1)
                split(n + 2)
                n, m = n + 1, m + 1

            def computed():
                act.wait_ge(slot_used[n % 2], n // 2 + 1)

            def store_features(dst, c, scale=1.0, tokens=T):
                computed()
                taken(copy(dst[:, 2 * c:2 * c + 2, :], pair()[:, :, 0:tokens], scale))

            def store_tokens(dst, c, scale=1.0, tiles=NT, func=ACT.Copy):
                computed()
                taken(copy(dst[:, :, c * C:(c + 1) * C], pair_tokens()[:, 0:tiles, :], scale, func))

            def passed():
                nonlocal n, m
                split(n + 2)
                n, m = n + 1, m + 1

            def square_sums(src, tiles, sources=None):
                for t in range(tiles):
                    if sources is not None:
                        w.next(sources)
                    last = nc.scalar.activation(PS[:, 6:8, :].rearrange("p b c -> p (b c)"), src[:, t], ACT.Square,
                                                accum_out=ss[:, t:t + 1])
                    w.link(last)

            def roots(signal, tiles=NT):
                nc.scalar.activation(root[:, 0:tiles], ss[:, 0:tiles], ACT.Sqrt, bias=epsc, scale=1.0 / D)\
                    .then_inc(S[signal], 1)

            def norm(src, tiles, gain, hi, source=None, again=False):
                if not again:
                    square_sums(src, tiles, source)
                    roots("norm_root", tiles)
                for k in range(KT):
                    w.next(S["norm_turned"])
                    copy(hi[:, k, :], PS[:, 4 + k % 4, 0:tiles * P], V[:, gain + k:gain + k + 1]).then_inc(S["hhi_ready"], 1)

            def split_output(src, count, at=0):
                for c in range(count):
                    copy(yhi[:, at + 2 * c:at + 2 * c + 2, :], src[:, 2 * c:2 * c + 2, :]).then_inc(S["y_hi"], 1)

            def z_and_merge():
                for c in range(4):
                    computed()
                    taken(copy(ztmp[:, :, :], pair(), func=ACT.Silu))
                    w.next(S["z_prod"])
                    copy(yhi[:, 2 * c:2 * c + 2, :], ZO[0][:, 2 * c:2 * c + 2, :]).then_inc(S["y_hi"], 1)
                for c in range(4):
                    computed()
                    if c:
                        act.wait_ge(pair_free[(m + 1) % 2], (m + 1) // 2)
                    taken(copy(gsig[:, :, :], pair(), func=ACT.Sigmoid))
                    passed()

            ZO = [None]

            def attention(units, exps, turned, output):
                for u in range(-2, units):
                    if u >= 0:
                        w.next(S["p_turned"])
                        turned(u).then_inc(S["pt_ready"], 1)
                    if u + 2 < units:
                        w.next(S["lg_ready"])
                        exps(u + 2).then_inc(S["p_exp"], 1)
                    if u >= 0:
                        w.next(S["pv_psum"])
                        output(u).then_inc(S["o_copied"], 1)
                w.next(S["o_copied"], units)

            def memory_attention(heads, cross, dst):
                p_, pt_ = (xp, xpt) if cross else (xp2, xpt2)

                def exps(h):
                    for t in range(NT):
                        last = nc.scalar.activation(p_[:, h % 2, t, :],
                                                    PS[:, 2 * (h % 2) + t // 2, (t % 2) * C:(t % 2) * C + C], ACT.Exp,
                                                    bias=nmax[:, h % 2, t:t + 1], accum_out=psum_[:, h % 2, t:t + 1])
                    return last

                def output(h):
                    if cross:
                        return copy(dst[:, 2 * h:2 * h + 2, :], PS[:, 6:8, :])
                    r = slice(MEM_HD * (h % 2), MEM_HD * (h % 2) + MEM_HD)
                    return copy(dst[r, h // 2, :], PS[r, 6, :])

                attention(heads, exps, lambda h: copy(pt_[:, :, :], PS[:, 4:6, :]), output)

            def index_relu(qt, half):
                for h in range(4 * half, 4 * half + 4):
                    if qt > 1 or half:
                        w.next(S["relu_used"])
                    w.next(S["idx_psum"])
                    copy(relu[:, h % 4, 0:(qt + 1) * P], PS[:, 4 + h % 4, 0:(qt + 1) * P], func=ACT.Relu)\
                        .then_inc(S["relu_ready"], 1)

            act.wait_ge(S["x_loaded"], 16)
            act.wait_ge(S["const_loaded"], 32)
            norm(X, NT, V_PRE, hhi)
            split(0)
            split(1)
            computed()
            copy(ikT[:, :], PS[:, 0, :])
            taken(copy(spT[0:32, :], PS[0:32, 1, :]))
            for c in range(2):
                store_features(iq, c)
            for c in range(2):
                store_features(gq, c, GLA_DK ** -0.5)
                index_relu(1, c)
            for c in range(2):
                store_features(gk, c)
                index_relu(2, c)
            for c in range(4):
                store_tokens(gv, c)
                if c < 2:
                    index_relu(3, c)

            w.next(S["la_psum"])
            w.link(copy(lscr[:, :, :], PS[:, 4:8, :], func=ACT.Abs))
            w.link(copy(lscr[:, :, :], lscr[:, :, :], -1.0, ACT.Exp))
            nc.scalar.activation(lscr[:, :, :], lscr[:, :, :], ACT.Ln, bias=1.0).then_inc(S["la_exp"], 1)
            for h in range(GLA_H):
                w.next(S["b_psum"])
                if h:
                    w.next(S["gk_ready"])
                copy(ge[:, 0, :], PS[:, 4 + h, :], 1.0 / GLA_NORM, ACT.Exp)
                copy(ge[:, 1, :], PS[:, 4 + h, :], -1.0 / GLA_NORM, ACT.Exp).then_inc(S["eb_ready"], 1)
                w.next(S["ediff_ready"])
                copy(ge[:, 2, :], ge[:, 2, :], 1.0 / GLA_NORM, ACT.Exp).then_inc(S["ekt_ready"], 1)
            for h in range(GLA_H):
                w.next(S["kt_turned"])
                copy(gktok[:, :, h * P:h * P + P], PS[:, 4 + h, :].rearrange("p (t d) -> p t d", t=NT))\
                    .then_inc(S["kt_copied"], 1)
            for t in range(NT):
                w.next(S["go_psum"])
                copy(go[:, 0:4, t * P:t * P + P], PS[:, 4, :].rearrange("p (v t) -> p v t", v=4))
                copy(go[:, 4:8, t * P:t * P + P], PS[:, 7, :].rearrange("p (v t) -> p v t", v=4)).then_inc(S["go_copied"], 1)
            w.next(S["go_copied"], NT)
            copy(gsq[:, :, :], go[:, :, :], func=ACT.Square).then_inc(S["sq_ready"], 1)
            w.next(S["ssq_psum"])
            nc.scalar.activation(root[:, 0:16], PS[:, 4, 0:16], ACT.Sqrt, bias=epsc, scale=1.0 / GLA_DV)\
                .then_inc(S["gla_root"], 1)
            ZO[0] = go
            z_and_merge()

            for c in range(4):
                store_features(dq, c, DSA_HD ** -0.5)
            store_features(dk, 0)
            store_tokens(dv, 0)
            w.next(S["line_psum"])
            copy(linet[:, :], PS[0:DSA_H, 4, 0:384]).then_inc(S["line_ready"], 1)

            def exps(u):
                L = (u // 4 + 1) * P
                for i in range(2):
                    last = nc.scalar.activation(lg[:, u % 2, i, 0:L], lg[:, u % 2, i, 0:L], ACT.Exp,
                                                bias=nmax[:, u % 2, i:i + 1], accum_out=psum_[:, u % 2, i:i + 1])
                return last

            def turned(u):
                blocks = u // 4 + 1
                return copy(pt[:, :, 0:blocks, :], PS[:, 4:6, 0:blocks * P].rearrange("p i (b q) -> p i b q", q=P))

            def output(u):
                qt, heads = u // 4, 2 * (u % 4)
                return copy(do[:, heads:heads + 2, qt * P:(qt + 1) * P], PS[:, 6, 0:2 * P].rearrange("p (i q) -> p i q", i=2))

            attention(4 * NT, exps, turned, output)
            ZO[0] = do
            z_and_merge()

            act.wait_ge(S["mem_loaded"], 16)
            norm(memx, 2, V_MEM, mhi)
            for c in range(4):
                store_features(mk, c, tokens=M)
            for c in range(4):
                store_tokens(mv, c, tiles=2)
            for c in range(4):
                store_features(xq, c, X_HD ** -0.5)
            memory_attention(X_H, True, xo)
            ZO[0] = xo
            z_and_merge()
            w.next(S["merged_ready"], 2)
            split_output(merged, 4)
            for c in range(4):
                store_tokens(o_mix, c)

            def after(o):
                if o is o_ffn:
                    w.next(S["ffo_free"], 4)
                else:
                    for b in range(2):
                        act.wait_ge(pair_free[b], (m + 1 - b) // 2)
                square_sums(o, NT)
                roots("o_root")

            def feed_forward(gain):
                nonlocal n, m
                norm(X, NT, gain, hhi, S["x_new"])
                sg, su = n % 2, (n + 1) % 2
                kg, ku = n // 2, (n + 1) // 2
                pg = m % 2
                r0 = w.at.get(S["ffn_a"].name, 0)
                with act.Fori(0, FFT // 2) as i:
                    act.wait_ge(slot_used[sg], i + (kg + 1))
                    copy(fs[:, :, :], PS[:, 2 * pg:2 * pg + 2, :], func=ACT.Silu).then_inc(pair_free[pg], 1)
                    act.wait_ge(raw_ready[sg], i * 16 + 16 * (kg + 2))
                    copy(whi[:, sg], raw[:, sg]).then_inc(hi_ready[sg], 1)
                    act.wait_ge(S["ffn_a"], i + (r0 + 1))
                    copy(ahi[:, bass.ds(i * 2, 2), :], fa[:, :, :]).then_inc(S["ffn_hi"], 1)
                    act.wait_ge(slot_used[su], i + (ku + 1))
                    act.wait_ge(raw_ready[su], i * 16 + 16 * (ku + 2))
                    copy(whi[:, su], raw[:, su]).then_inc(hi_ready[su], 1)
                w.at[S["ffn_a"].name] = r0 + FFT // 2
                n, m = n + FFT, m + FFT
                for c in range(4):
                    for r in range(0, FFT, KT):
                        act.wait_ge(slot_used[n % 2], n // 2 + 1)
                        if r + KT >= FFT:
                            copy(o_ffn[:, :, c * C:(c + 1) * C], PS[:, 4 * (c % 2):4 * (c % 2) + 4, 0:C])\
                                .then_inc(S["ffo_free"], 1)
                        split(n + 2)
                        n += 1
                after(o_ffn)

            after(o_mix)

            norm(X, NT, V_MIX0, hhi, S["x_new"])
            for c in range(4):
                computed()
                dst = (lq if c < 2 else lk)[0:ML_DK, 2 * (c % 2):2 * (c % 2) + 2, :]
                taken(copy(dst, pair()[0:ML_DK], 1.0 if c < 2 else ML_DK ** -0.5))
            for h in range(ML_H):
                computed()
                taken(copy(lv[:, :, h, 0:ML_DV], pair_tokens()[:, :, 0:ML_DV]))
            for c in range(3):
                store_tokens(lo, c, func=ACT.Sigmoid)
            computed()
            taken(copy(gT[0:8, :], pair()[0:8, 0, :]))
            store_features(mq, 0, MEM_HD ** -0.5)
            act.wait_ge(S["mem_loaded"], 32)
            norm(memx, 2, V_MEM0, mhi)
            store_features(mk2, 0, tokens=M)
            store_tokens(mv2, 0, tiles=2)
            w.next(S["gate_soft"])
            copy(lgt[:, :, :], lgt[:, :, :], 1.0 / SOFTCAP, ACT.Tanh).then_inc(S["gate_abs"], 1)
            w.next(S["gate_exp"])
            w.link(copy(lex[:, :, :], lgt[:, :, 4:8], func=ACT.Abs))
            w.link(copy(lex[:, :, :], lex[:, :, :], -1.0, ACT.Exp))
            nc.scalar.activation(lex[:, :, :], lex[:, :, :], ACT.Ln, bias=1.0).then_inc(S["la_exp"], 1)
            w.next(S["lb_psum"])
            copy(Lb[:, :, :], PS[:, 4:8, :]).then_inc(S["lb_ready"], 1)
            for h in range(-1, ML_H):
                if h + 1 < ML_H:
                    w.next(S["lw_arg"])
                    b_ = (h + 1) % 2
                    for s in range(NT):
                        for j in range(s, NT):
                            js = slice(j * P, j * P + P)
                            src, bias = (at[:, b_, s, js], 0.0) if j == s else (Lb[:, h + 1, js], bi[:, s, j, h + 1:h + 2])
                            last = nc.scalar.activation(at[:, b_, s, js], src, ACT.Exp, bias=bias)
                    last.then_inc(S["lw_exp"], 1)
                if h >= 0:
                    w.next(S["hm_ready"])
                    for t in range(NT):
                        w.link(nc.scalar.activation(ljunk[:, :], hm[:, t, h, :], ACT.Square,
                                                    accum_out=ss[:, 4 * t + h:4 * t + h + 1]))
            nc.scalar.activation(root[:, 0:16], ss[:, 0:16], ACT.Sqrt, bias=epsc, scale=1.0 / ML_DV).then_inc(S["hm_root"], 1)
            memory_attention(MEM_H, False, mo)
            for k in range(6):
                w.next(S["hm_turned"])
                copy(yhi[:, k, :], PS[:, 4 + k % 4, :]).then_inc(S["y_hi"], 1)
            split_output(mo, 1, at=6)
            for c in range(4):
                store_tokens(o_mix, c)
            after(o_mix)
            feed_forward(V_FFN0)

            norm(X, NT, V_KV, hhi, S["x_new"])
            store_tokens(sk, 0)
            store_tokens(sv, 0)
            norm(X, NT, V_MIX1, hhi, again=True)
            for c in range(3):
                store_tokens(sq, c, SW_HD ** -0.5)
            store_features(mqb, 0, MEM_HD ** -0.5)
            act.wait_ge(S["mem_loaded"], 48)
            norm(memx, 2, V_MEM1, mhi)
            store_features(mk2, 0, tokens=M)
            store_tokens(mv2, 0, tiles=2)
            for j in range(2):
                w.next(S["rope_arg"])
                copy(cs[:, j], cs[:, j], func=ACT.Sin).then_inc(S["rope_sin"], 1)
            for b in range(8):
                w.next(S["rope_turned"])
                copy(krT[:, b, :] if b < 2 else qrT[:, b - 2, :], PS[:, 4 + b % 4, :]).then_inc(S["rot_copied"], 1)

            def exps(h):
                for t in range(NT):
                    nc.scalar.activation(slg[:, h % 2, t, :], slg[:, h % 2, t, :], ACT.Exp, bias=nmax[:, h % 2, t:t + 1],
                                         accum_out=psum_[:, h % 2, t:t + 1])
                return nc.scalar.activation(esink[:, h % 2, :], nmax[:, h % 2, :], ACT.Exp, bias=V[:, V_SINK + h:V_SINK + h + 1])

            def output(h):
                r = slice(SW_HD * (h % 2), SW_HD * (h % 2) + SW_HD)
                return copy(so[r, h // 2, :], PS[r, 6, :])

            attention(SW_H, exps, lambda h: copy(spt[:, :, :], PS[:, 4:6, :].rearrange("p b (j q) -> p (b j) q", q=P)[:, 0:7, :]),
                      output)
            memory_attention(MEM_H, False, mo)
            split_output(so, 3)
            split_output(mo, 1, at=6)
            for c in range(4):
                store_tokens(o_mix, c)
            after(o_mix)
            feed_forward(V_FFN1)

        @block.vector
        def _(dve):
            w = Waits(dve, S["dve_chain"])
            V_ = nc.vector
            n = m = 0

            def split(s):
                if s < NS:
                    dve.wait_ge(hi_ready[s % 2], s // 2 + 1)
                    V_.tensor_tensor(wlo[:, s % 2], raw[:, s % 2], whi[:, s % 2], ALU.subtract).then_inc(lo_ready[s % 2], 1)

            def pair():
                return PS[:, 2 * (m % 2):2 * (m % 2) + 2, :]

            def passed(count=1):
                nonlocal n, m
                for _ in range(count):
                    split(n + 2)
                    n, m = n + 1, m + 1

            def stored():
                for b in range(2):
                    dve.wait_ge(pair_free[b], (m + 1 - b) // 2)

            def norm(src, dst, tiles, gain, hi, lo, again=False):
                if not again:
                    w.next(S["norm_root"])
                    w.link(V_.reciprocal(rstd[:, 0:tiles], root[:, 0:tiles]))
                    for t in range(tiles):
                        V_.tensor_scalar(dst[:, t], src[:, t], rstd[:, t:t + 1], None, ALU.mult).then_inc(S["xn_ready"], 1)
                for k in range(KT):
                    w.next(S["hhi_ready"])
                    V_.scalar_tensor_tensor(lo[:, k, :], PS[:, 4 + k % 4, 0:tiles * P], V[:, gain + k:gain + k + 1],
                                            hi[:, k, :], ALU.mult, ALU.subtract).then_inc(S["hlo_ready"], 1)

            def split_output(src, count, at_=0):
                for c in range(count):
                    w.next(S["y_hi"])
                    V_.tensor_tensor(ylo[:, at_ + 2 * c:at_ + 2 * c + 2, :], src[:, 2 * c:2 * c + 2, :],
                                     yhi[:, at_ + 2 * c:at_ + 2 * c + 2, :], ALU.subtract).then_inc(S["y_lo"], 1)

            def z_and_merge(o, branch):
                nonlocal n, m
                for c in range(4):
                    oc = o[:, 2 * c:2 * c + 2, :]
                    dve.wait_ge(pair_free[m % 2], m // 2 + 1)
                    V_.tensor_tensor(oc, oc, ztmp[:, :, :], ALU.mult).then_inc(S["z_prod"], 1)
                    passed()
                    w.next(S["y_hi"])
                    V_.tensor_tensor(ylo[:, 2 * c:2 * c + 2, :], oc, yhi[:, 2 * c:2 * c + 2, :], ALU.subtract)\
                        .then_inc(S["y_lo"], 1)
                    if not branch:
                        take(2, 2, last=(c == 3))
                for c in range(4):
                    mc = merged[:, 2 * c:2 * c + 2, :]
                    dve.wait_ge(pair_free[m % 2], m // 2 + 1)
                    passed()
                    dve.wait_ge(slot_used[n % 2], n // 2 + 1)
                    if branch == 0:
                        last = V_.tensor_tensor(mc, pair(), gsig[:, :, :], ALU.mult)
                        last.then_inc(pair_free[m % 2], 1)
                    else:
                        V_.tensor_tensor(gprod[:, :, :], pair(), gsig[:, :, :], ALU.mult).then_inc(pair_free[m % 2], 1)
                        dve.wait_ge(pair_free[m % 2], m // 2 + 1)
                        last = V_.tensor_tensor(mc, mc, gprod[:, :, :], ALU.add)
                        if c < 3:
                            w.link(last)
                    if c == 3 and branch:
                        last.then_inc(S["merged_ready"], 1)
                    passed()
                    if not branch:
                        take(3, 4, first=(c == 0), last=(c == 3))

            def attention(units, p, count, peaks, sink=False):
                def scale(u):
                    w.next(S["p_exp"])
                    sums, r = psum_[:, u % 2, 0:count], prec[:, u % 2, 0:count]
                    if sink:
                        w.link(V_.tensor_tensor(r, sums, esink[:, u % 2, :], ALU.add))
                        sums = r
                    w.link(V_.reciprocal(r, sums))
                    V_.tensor_tensor(p(u), p(u), r.unsqueeze(2).broadcast_to([P, count, p(u).shape[2]]), ALU.mult)\
                        .then_inc(S["p_norm"], 1)

                for u in range(units + 1):
                    if u >= 2:
                        scale(u - 1)
                    if u < units:
                        w.next(S["lg_psum"])
                        peaks(u).then_inc(S["lg_ready"], 1)
                    if u == 1:
                        scale(0)

            def memory_attention(heads, cross):
                attention(heads, lambda h: (xp if cross else xp2)[:, h % 2], NT,
                          lambda h: V_.tensor_reduce(nmax[:, h % 2, :], PS[:, 2 * (h % 2):2 * (h % 2) + 2, :]
                                                     .rearrange("p b (u c) -> p (b u) c", u=2), AX.X, ALU.max, negate=True))

            def index_sum(qt, half):
                score = seen(qt)
                for h in range(4 * half, 4 * half + 4):
                    w.next(S["relu_ready"])
                    r_, iw = relu[:, h % 4, 0:(qt + 1) * P], iwt[:, qt, h:h + 1]
                    if h == 0:
                        last = V_.tensor_scalar(score, r_, iw, None, ALU.mult)
                    else:
                        last = V_.scalar_tensor_tensor(score, r_, iw, score, ALU.mult, ALU.add)
                    last.then_inc(S["relu_used"], 1)
                    w.next(S["relu_used"])

            def take(qt, rounds, first=False, last=False):
                if first:
                    w.next(S["score_masked"])
                for r in range(rounds):
                    w.link(V_.max(top8, seen(qt)))
                    w.link(V_.match_replace(seen(qt), top8, seen(qt), TAKEN))
                if last:
                    w.link(V_.tensor_scalar(seen(qt), seen(qt), TAKEN, NEG, ALU.not_equal, ALU.mult))

            dve.wait_ge(S["const_loaded"], 32)
            norm(X, xn, NT, V_PRE, hhi, hlo)
            split(0)
            split(1)
            passed(3)
            w.next(S["iw_turned"])
            V_.tensor_scalar(iwt, PS[:, 4, 0:128].rearrange("p (t c) -> p t c", t=NT)[:, :, 16:24],
                             IDX_H ** -0.5, IDX_D ** -0.5, ALU.mult, ALU.mult).then_inc(S["special_ready"], 1)
            w.next(S["special_ready"])
            V_.tensor_scalar(nsink, V[:, V_SINK:V_SINK + SW_H], -1.0, None, ALU.mult)
            for c in range(2):
                passed()
                index_sum(1, c)
            for c in range(2):
                passed()
                index_sum(2, c)
                take(1, 4, first=(c == 0))
            for c in range(4):
                passed()
                if c < 2:
                    index_sum(3, c)
                    take(1, 4, last=(c == 1))
                else:
                    take(2, 4, first=(c == 2))

            V_.memset(attm[:, :, :], 0.0)
            w.next(S["la_exp"])
            V_.scalar_tensor_tensor(la[:, :, :], PS[:, 4:8, :], 0.0, lscr[:, :, :], ALU.min, ALU.subtract)\
                .then_inc(S["la_ready"], 1)
            for h in range(GLA_H):
                w.next(S["eb_ready"])
                b_ = PS[:, 4 + h, :].rearrange("p (c t) -> p c t", t=64)
                w.link(V_.tensor_copy(blast, b_[:, :, 63]))
                V_.tensor_tensor(ge[:, 2, :].rearrange("p (c t) -> p c t", t=64), blast.unsqueeze(2).broadcast_to([P, 8, 64]), b_,
                                 ALU.subtract).then_inc(S["ediff_ready"], 1)
                V_.tensor_copy(dec[:, h, :], ge[:, 0, :].rearrange("p (c t) -> p c t", t=64)[:, :, 63])
                V_.tensor_tensor(gq[:, h, :], gq[:, h, :], ge[:, 0, :], ALU.mult)
                w.next(S["ekt_ready"])
                w.link(V_.tensor_tensor(gkt[:, h, :], gk[:, h, :], ge[:, 2, :], ALU.mult))
                V_.tensor_tensor(gk[:, h, :], gk[:, h, :], ge[:, 1, :], ALU.mult).then_inc(S["gk_ready"], 1)
            w.next(S["kt_copied"], GLA_H)
            for t in range(NT):
                w.next(S["att_psum"])
                V_.copy_predicated(attm[:, :, :], u64.bitcast(U32).unsqueeze(1).broadcast_to([P, GLA_H, P]),
                                   PS[:, 4, :].rearrange("p (h t) -> p h t", h=GLA_H)).then_inc(S["att_ready"], 1)
                for c in (2 * t, 2 * t + 1):
                    if c == 2 * NT - 1:
                        break
                    w.next(S["gla_upd"])
                    for h in range(GLA_H):
                        new, upd = S_t[:, (c + 1) % 4, h, :], PS[:, 5 + h // 2, (h % 2) * C:(h % 2) * C + C]
                        if c:
                            last = V_.scalar_tensor_tensor(new, S_t[:, c % 4, h, :], dec[:, h, c:c + 1], upd, ALU.mult, ALU.add)
                        else:
                            last = V_.tensor_copy(new, upd)
                    last.then_inc(S["S_ready"], 1)
                    w.next(S["S_ready"])
            w.next(S["gla_root"])
            V_.reciprocal(rstd16, root[:, 0:16]).then_inc(S["gla_rstd"], 1)
            w.next(S["rs_psum"])
            for h in range(GLA_H):
                for v in range(2):
                    i = 2 * h + v
                    last = V_.scalar_tensor_tensor(go[:, i, :], go[:, i, :], V[:, V_GLA + v:V_GLA + v + 1], PS[:, 4 + h, :],
                                                   ALU.mult, ALU.mult)
            w.link(last)
            z_and_merge(go, 0)

            passed(6)
            dve.wait_ge(S["tbias_loaded"], 16)

            def peaks(u):
                qt, heads = u // 4, 2 * (u % 4)
                L = (qt + 1) * P
                near = min(L, C)
                l_ = lg[:, u % 2, :, 0:L]
                mask = seen(qt) if qt else dcm
                w.link(V_.tensor_tensor(l_, PS[:, 2 * (u % 2):2 * (u % 2) + 2, 0:L], mask.unsqueeze(1).broadcast_to([P, 2, L]), ALU.add))
                w.link(V_.tensor_tensor(l_[:, :, L - near:L], l_[:, :, L - near:L], tbias[:, heads:heads + 2, C - near:C], ALU.add))
                return V_.tensor_reduce(nmax[:, u % 2, 0:2], l_, AX.X, ALU.max, negate=True)

            attention(4 * NT, lambda u: lg[:, u % 2, :, 0:(u // 4 + 1) * P], 2, peaks)
            w.next(S["o_copied"], 4 * NT)
            z_and_merge(do, 1)

            norm(memx, memn, 2, V_MEM, mhi, mlo)
            passed(12)
            memory_attention(X_H, True)
            w.next(S["o_copied"], X_H)
            z_and_merge(xo, 2)
            split_output(merged, 4)
            passed(4)

            def residual(o, loads):
                w.next(S["o_root"])
                w.link(V_.reciprocal(rstd[:, 0:NT], root[:, 0:NT]))
                dve.wait_ge(S["gpost_loaded"], 16 * loads)
                for t in range(NT):
                    w.link(V_.scalar_tensor_tensor(o[:, t], o[:, t], rstd[:, t:t + 1], gpost[:, :], ALU.mult, ALU.mult))
                    V_.tensor_tensor(X[:, t], X[:, t], o[:, t], ALU.add).then_inc(S["x_new"], 1)

            def feed_forward(gain, loads):
                nonlocal n, m
                norm(X, xn, NT, gain, hhi, hlo)
                sg, su = n % 2, (n + 1) % 2
                kg, ku = n // 2, (n + 1) // 2
                pg, pu, mg = m % 2, (m + 1) % 2, m // 2
                r0 = w.at.get(S["ffn_hi"].name, 0)
                with dve.Fori(0, FFT // 2) as i:
                    dve.wait_ge(hi_ready[sg], i + (kg + 2))
                    V_.tensor_tensor(wlo[:, sg], raw[:, sg], whi[:, sg], ALU.subtract).then_inc(lo_ready[sg], 1)
                    dve.wait_ge(pair_free[pg], i + (mg + 1))
                    dve.wait_ge(slot_used[su], i + (ku + 1))
                    V_.tensor_tensor(fa[:, :, :], PS[:, 2 * pu:2 * pu + 2, :], fs[:, :, :], ALU.mult).then_inc(pair_free[pu], 1)
                    dve.wait_ge(pair_free[pu], i + ((m + 1) // 2 + 1))
                    V_.tensor_copy(small[:, 336:337], fa[:, 0, 0:1]).then_inc(S["ffn_a"], 1)
                    dve.wait_ge(S["ffn_hi"], i + (r0 + 1))
                    V_.tensor_tensor(alo[:, bass.ds(i * 2, 2), :], fa[:, :, :], ahi[:, bass.ds(i * 2, 2), :], ALU.subtract)\
                        .then_inc(S["ffn_lo"], 1)
                    dve.wait_ge(hi_ready[su], i + (ku + 2))
                    V_.tensor_tensor(wlo[:, su], raw[:, su], whi[:, su], ALU.subtract).then_inc(lo_ready[su], 1)
                w.at[S["ffn_hi"].name] = r0 + FFT // 2
                n, m = n + FFT, m + FFT
                for c in range(4 * -(-FFT // KT)):
                    split(n + 2)
                    n += 1
                residual(o_ffn, loads)

            dve.wait_ge(S["x_again"], 16)
            residual(o_mix, 1)

            norm(X, xn, NT, V_MIX0, hhi, hlo)
            V_.memset(lv[:, :, :, ML_DV:ML_DV + 1], 1.0).then_inc(S["ones_ready"], 1)
            passed(13)
            norm(memx, memn, 2, V_MEM0, mhi, mlo)
            passed(2)
            w.next(S["gt_turned"])
            V_.tensor_tensor(lgt, PS[:, 4, 0:32].rearrange("p (t g) -> p t g", t=NT),
                             V[:, V_BG:V_BG + 8].unsqueeze(1).broadcast_to([P, NT, 8]), ALU.add).then_inc(S["gate_soft"], 1)
            w.next(S["gate_abs"])
            V_.tensor_scalar(lgt, lgt, SOFTCAP, None, ALU.mult).then_inc(S["gate_exp"], 1)
            w.next(S["la_exp"])
            V_.scalar_tensor_tensor(lgf, lgt[:, :, 4:8], 0.0, lex, ALU.min, ALU.subtract).then_inc(S["logf_ready"], 1)
            w.next(S["cl_psum"])
            for t in range(NT):
                last = V_.tensor_tensor(bi[:, t, t, :], lgt[:, t, 0:4], PS[:, 4, 4 * t:4 * t + 4], ALU.subtract)
            last.then_inc(S["bi_ready"], 1)
            w.next(S["bi_ready"])
            w.next(S["lb_ready"])
            for s in range(NT):
                for j in range(s + 1, NT):
                    w.link(V_.tensor_tensor(bi[:, s, j, :], bi[:, s, j - 1, :], Lb[:, :, j * P - 1], ALU.add))
            for h in range(-1, ML_H):
                if h + 1 < ML_H:
                    aw = at[:, (h + 1) % 2]
                    for s in range(NT):
                        ssl = slice(s * P, s * P + P)
                        last = V_.scalar_tensor_tensor(aw[:, s, ssl], Lb[:, h + 1, ssl], bi[:, s, s, h + 1:h + 2], lcm, ALU.add, ALU.add)
                    last.then_inc(S["lw_arg"], 1)
                if h >= 0:
                    w.next(S["num_psum"])
                    num = PS[:, 6:8, :].rearrange("p b (u c) -> p (b u) c", u=2)
                    w.link(V_.tensor_copy(lden.unsqueeze(2), num[:, :, ML_DV:ML_DV + 1]))
                    w.link(V_.scalar_tensor_tensor(lden, lden, -1.0, lden, ALU.mult, ALU.max))
                    w.link(V_.tensor_scalar(lden, lden, 1.0, None, ALU.max))
                    w.link(V_.reciprocal(lden, lden))
                    V_.tensor_tensor(hm[:, :, h, :], num[:, :, 0:ML_DV], lden.unsqueeze(2).broadcast_to([P, NT, ML_DV]), ALU.mult)\
                        .then_inc(S["hm_ready"], 1)
                if h + 1 < ML_H:
                    w.next(S["lw_exp"])
                    w.next(S["lsc_psum"])
                    for s in range(NT):
                        last = V_.tensor_tensor(aw[:, s, s * P:T], aw[:, s, s * P:T], score_bank(h + 1, s), ALU.mult)
                    last.then_inc(S["at_ready"], 1)
            w.next(S["hm_root"])
            w.link(V_.reciprocal(rstd16, root[:, 0:16]))
            dve.wait_ge(S["gml_loaded"], 16)
            for t in range(NT):
                hr = hm[:, t].rearrange("p h d -> p (h d)")
                w.link(V_.tensor_tensor(hm[:, t], hm[:, t], rstd16[:, 4 * t:4 * t + 4].unsqueeze(2).broadcast_to([P, 4, ML_DV]), ALU.mult))
                w.link(V_.tensor_tensor(hr, hr, gmb[:, :], ALU.mult))
                V_.tensor_tensor(hr, hr, lo[:, t, :], ALU.mult).then_inc(S["hm_done"], 1)
            memory_attention(MEM_H, False)
            for k in range(6):
                w.next(S["y_hi"])
                V_.tensor_tensor(ylo[:, k, :], PS[:, 4 + k % 4, :], yhi[:, k, :], ALU.subtract).then_inc(S["y_lo"], 1)
            split_output(mo, 1, at_=6)
            passed(4)
            residual(o_mix, 2)
            feed_forward(V_FFN0, 3)

            norm(X, xn, NT, V_KV, hhi, hlo)
            passed(2)
            norm(X, xn, NT, V_MIX1, hhi, hlo, again=True)
            passed(4)
            norm(memx, memn, 2, V_MEM1, mhi, mlo)
            passed(2)
            ang, arg = ra[:, 0:128].rearrange("p (t d) -> p t d", t=NT), ra[:, 128:256].rearrange("p (t d) -> p t d", t=NT)
            ki, kf = rb[:, 0:128].bitcast(I32).rearrange("p (t d) -> p t d", t=NT), ra[:, 256:384].rearrange("p (t d) -> p t d", t=NT)
            dve.wait_ge(S["pos_loaded"], 16)
            w.link(V_.tensor_copy(posf, posi))
            w.link(V_.tensor_tensor(ang, posf.unsqueeze(2).broadcast_to([P, NT, 32]),
                                    inv.unsqueeze(1).broadcast_to([P, NT, 32]), ALU.mult))
            for j in range(2):
                w.link(V_.tensor_scalar(ki, ang, 1.0 / (2 * math.pi), 0.25 * (1 - j), ALU.mult, ALU.add))
                w.link(V_.tensor_copy(kf, ki))
                w.link(V_.scalar_tensor_tensor(arg, kf, -TURN[0], ang, ALU.mult, ALU.add))
                w.link(V_.scalar_tensor_tensor(arg, kf, -TURN[1], arg, ALU.mult, ALU.add))
                w.link(V_.scalar_tensor_tensor(arg, kf, -TURN[2], arg, ALU.mult, ALU.add))
                if j == 0:
                    w.link(V_.tensor_scalar(arg, arg, math.pi / 2, None, ALU.add))
                V_.tensor_scalar(cs[:, j], arg, PI_IN, -PI_IN, ALU.min, ALU.max).then_inc(S["rope_arg"], 1)
                w.next(S["rope_sin"])
            stored()
            for t in range(NT):
                for heads, src, dst in ((SW_KV, sk, skr), (SW_H, sq, sqr)):
                    x = src[:, t].rearrange("p (h a d) -> p h a d", a=2, d=32)
                    y = dst[:, t].rearrange("p (h a d) -> p h a d", a=2, d=32)
                    width = heads * SW_HD
                    xc = ra[:, 0:width].rearrange("p (h a d) -> p h a d", a=2, d=32)
                    xs = rb[:, 0:width].rearrange("p (h a d) -> p h a d", a=2, d=32)
                    sin = cs[:, 1, t, :].unsqueeze(1).broadcast_to([P, heads, 32])
                    V_.tensor_tensor(ra[:, 0:width].rearrange("p (h d) -> p h d", d=32), src[:, t].rearrange("p (h d) -> p h d", d=32),
                                     cs[:, 0, t, :].unsqueeze(1).broadcast_to([P, 2 * heads, 32]), ALU.mult)
                    V_.tensor_tensor(xs[:, :, 0, :], x[:, :, 1, :], sin, ALU.mult)
                    w.link(V_.tensor_tensor(xs[:, :, 1, :], x[:, :, 0, :], sin, ALU.mult))
                    V_.tensor_tensor(y[:, :, 0, :], xc[:, :, 0, :], xs[:, :, 0, :], ALU.subtract)
                    last = V_.tensor_tensor(y[:, :, 1, :], xc[:, :, 1, :], xs[:, :, 1, :], ALU.add)
                    if heads == SW_KV:
                        w.link(last)
                last.then_inc(S["rope_done"], 1)
                w.next(S["rope_done"])

            def peaks(h):
                b, ps_ = h % 2, PS[:, 2 * (h % 2):2 * (h % 2) + 2, :].rearrange("p b (u c) -> p (b u) c", u=2)
                V_.memset(slg[:, b, 0, 0:P], NEG)
                V_.tensor_tensor(slg[:, b, 0, P:C], ps_[:, 0, P:C], swa[:, P:C], ALU.add)
                w.link(V_.tensor_tensor(slg[:, b, 1:NT], ps_[:, 1:NT, :], swa.unsqueeze(1).broadcast_to([P, NT - 1, C]), ALU.add))
                w.link(V_.tensor_reduce(nmax[:, b, :], slg[:, b], AX.X, ALU.max, negate=True))
                return V_.tensor_scalar(nmax[:, b, :], nmax[:, b, :], nsink[:, h:h + 1], None, ALU.min)

            attention(SW_H, lambda h: slg[:, h % 2], NT, peaks, sink=True)
            memory_attention(MEM_H, False)
            split_output(so, 3)
            split_output(mo, 1, at_=6)
            passed(4)
            residual(o_mix, 4)
            feed_forward(V_FFN1, 5)

        @block.gpsimd
        def _(pool):
            w = Waits(pool, S["pool_chain"])

            def gain(i):
                if i:
                    pool.wait_ge(S["x_new"], NT * i)
                pool.dma_start(gpost[:, :], gposts[i:i + 1, :].broadcast_to([P, D])).then_inc(S["gpost_loaded"], 16)

            gain(0)
            for qt in range(1, NT):
                w.next(S["relu_used"], IDX_H)
                diagonal = seen(qt)[:, qt * P:qt * P + P]
                pool.affine_select(out=diagonal, in_=diagonal, pattern=[[-1, P]], compare_op=ALU.is_ge, fill=HIDDEN,
                                   base=0, channel_multiplier=1).then_inc(S["score_masked"], 1)
            w.next(S["line_ready"])
            pool.dma_start(bass.AP(line.tensor, 0, [[LINE_HEAD, DSA_H], [LINE + 1, P], [1, 384]]),
                           linet[:, :].unsqueeze(1).broadcast_to([DSA_H, P, 384])).then_inc(S["line_stored"], 16)
            pool.wait_ge(S["line_stored"], 16)
            pool.dma_start(tbias[:, :, :], bass.AP(line.tensor, P - 1, [[LINE, P], [LINE_HEAD, DSA_H], [1, C]]))\
                .then_inc(S["tbias_loaded"], 16)
            w.next(S["merged_ready"])
            pool.dma_start(X[:, :, :], x_in.rearrange("(t p) d -> p t d", p=P)).then_inc(S["x_again"], 16)
            pool.dma_start(memx[:, :, :], mem_in.rearrange("(t p) d -> p t d", p=P)).then_inc(S["mem_loaded"], 16)
            gain(1)
            pool.dma_start(memx[:, :, :], mem2_in.rearrange("(t p) d -> p t d", p=P)).then_inc(S["mem_loaded"], 16)
            pool.dma_start(gmb[:, :], gmlb.broadcast_to([P, 768])).then_inc(S["gml_loaded"], 16)
            gain(2)
            gain(3)
            pool.dma_start(memx[:, :, :], mem2_in.rearrange("(t p) d -> p t d", p=P)).then_inc(S["mem_loaded"], 16)
            gain(4)

        @block.sync
        def _(sp):
            sp.dma_start(X[:, :, :], x_in.rearrange("(t p) d -> p t d", p=P)).then_inc(S["x_loaded"], 16)
            sp.dma_start(K[:, :], consts).then_inc(S["const_loaded"], 16)
            sp.dma_start(V[:, :], cols).then_inc(S["const_loaded"], 16)
            for p in range(2):
                sp.dma_start(raw[:, p], stream[0, p]).then_inc(raw_ready[p], 16)
            sp.dma_start(wup_s[:, :], wup[0:GLA_RANK, :]).then_inc(S["gate_w_loaded"], 16)
            sp.dma_start(ba_s[:, :], wup[GLA_RANK:GLA_RANK + 1, :]).then_inc(S["gate_w_loaded"], 16)
            sp.dma_start(posi, pos_in).then_inc(S["pos_loaded"], 16)
            with sp.Fori(1, NS // 2) as i:
                for p in range(2):
                    sp.wait_ge(lo_ready[p], i)
                    sp.dma_start(raw[:, p], stream[bass.ds(i, 1), p]).then_inc(raw_ready[p], 16)
            for t in range(NT):
                sp.wait_ge(S["x_new"], NT * 4 + t + 1)
                sp.dma_start(out[t * P:t * P + P, :], X[:, t, :]).then_inc(S["out_stored"], 16)
            sp.wait_ge(S["out_stored"], 16 * NT)



def t5_bucket(distance):
    exact = BUCKETS // 2
    if distance < exact:
        return max(distance, 0)
    return min(exact + int(math.log(distance / exact) / math.log(MAX_DIST / exact) * (BUCKETS - exact)), BUCKETS - 1)


def constants():
    a, b = np.arange(P)[:, None], np.arange(P)[None, :]
    k = np.zeros((P, K_ALL), np.float32)
    k[:, K_ID:K_ID + P] = a == b
    k[:, K_U64:K_U64 + P] = (a <= b) & (a // 64 == b // 64)
    k[:, K_U128:K_U128 + P] = a <= b
    k[:, K_ONE:K_ONE + P] = 1.0
    d = a + P - np.arange(C)[None, :]
    k[:, K_SWA:K_SWA + C] = np.where((d >= 0) & (d < P), 0.0, NEG)
    k[:, K_DCM:K_DCM + P] = np.where(b <= a, 0.0, NEG)
    k[:, K_LCM:K_LCM + P] = np.where(b >= a, 0.0, NEG)
    for i in range(384):
        k[t5_bucket(255 - i), K_HOT + i] += 1.0
        k[BUCKETS - 1, K_HOT + i] -= 1.0
    k[:, K_INV:K_INV + 32] = np.float32(1.0) / np.float32(10000.0) ** (np.arange(0, 64, 2, dtype=np.float32) / np.float32(64))
    k[:, K_EPS] = EPS
    return k


def kernel(**inputs):
    import concourse.bacc as bacc
    from concourse.bass_utils import run_bass_kernel_spmd

    a = {name: np.asarray(v) for name, v in inputs.items()}
    weights = {name: a[name][0] for name in
               ("w_in", "w_gla_out", "w_dsa_out", "w_x_out", "w_mem_kv", "w_o")}
    weights |= {"w_in_a": a["w_in_a_2"][0], "w_in_b": a["w_in_b_2"][0], "w_kv": a["w_kv_2"]}
    for layer in range(2):
        for name in ("w_mem_kv", "w_out", "w_ffn_in", "w_ffn_out"):
            weights[f"{name}_{layer}"] = a[f"{name}_2"][layer]
    stream = np.zeros((NS, P, KT, C), np.float32)
    for s, pieces in enumerate(slots()):
        for name, row, tiles, column, width, place in pieces:
            w = weights[name][row * P:(row + tiles) * P, column:column + width]
            stream[s, :, 0:tiles, place:place + width] = w.reshape(tiles, P, width).transpose(1, 0, 2)

    cols = np.zeros((P, V_COLS), np.float32)
    for at, v in ((V_PRE, a["g_pre"][0]), (V_MEM, a["g_mem"][0]), (V_GLA, a["g_gla"][0]),
                  (V_MIX0, a["g_mix_pre_2"][0]), (V_FFN0, a["g_ffn_pre_2"][0]), (V_KV, a["g_kv_2"]),
                  (V_MIX1, a["g_mix_pre_2"][1]), (V_FFN1, a["g_ffn_pre_2"][1]),
                  (V_MEM0, a["g_mem_2"][0]), (V_MEM1, a["g_mem_2"][1])):
        cols[:, at:at + v.size // P] = v.reshape(-1, P).T
    cols[:, V_BG:V_BG + 8] = a["b_gates_a_2"][0]
    cols[:, V_SINK:V_SINK + SW_H] = a["sinks_b_2"][0]
    cols[0:BUCKETS, V_ALL:V_COLS] = a["rel_bias"]

    arrays = {
        "stream": stream.reshape(NS // 2, 2, P, KT * C),
        "x": a["x"][0], "mem": a["mem"][0], "mem2": a["mem_2"][0],
        "consts": constants(), "cols": cols,
        "gposts": np.stack([a["g_post"][0], a["g_mix_post_2"][0], a["g_ffn_post_2"][0],
                            a["g_mix_post_2"][1], a["g_ffn_post_2"][1]]),
        "wup": np.concatenate([a["w_gla_a_up"][0], a["b_gla_a"]]),
        "gml": a["g_mlstm_out_2"],
        "positions": np.ascontiguousarray(a["positions_2"].reshape(NT, P).T),
    }
    arrays = {name: np.ascontiguousarray(v) for name, v in arrays.items()}
    nc = bacc.Bacc("TRN2", target_bir_lowering=False, num_devices=1)
    t = {name: nc.dram_tensor(f"in_{name}", v.shape, mybir.dt.from_np(v.dtype), kind="ExternalInput").ap()
         for name, v in arrays.items()}
    line = nc.dram_tensor("bias_line", (DSA_H, LINE_HEAD), F32, kind="Internal").ap()
    out = nc.dram_tensor("out", (T, D), F32, kind="ExternalOutput").ap()
    build(nc, t["stream"], t["x"], t["mem"], t["mem2"], t["consts"], t["cols"], t["gposts"], t["wup"], t["gml"],
          t["positions"], line, out)
    r = run_bass_kernel_spmd(nc, [{f"in_{name}": v for name, v in arrays.items()}], core_ids=[0])
    return r.results[0]["out"].reshape(1, T, D)
```

```python
import math
from contextlib import ExitStack

import numpy as np

import concourse.bass as bass
from concourse import mybir

F32 = mybir.dt.float32
F32R = mybir.dt.float32r
I32 = mybir.dt.int32
U32 = mybir.dt.uint32
ALU = mybir.AluOpType
ACT = mybir.ActivationFunctionType
AX = mybir.AxisListType

P = 128
D = 1024
T = 512
NT = T // P
KT = D // P
C = 256
M = 256
EPS = 1e-6
NEG = -1e30

GLA_H, GLA_DK, GLA_DV, GLA_RANK, GLA_NORM = 4, 128, 256, 16, 16.0
DSA_H, DSA_KV, DSA_HD = 8, 2, 128
IDX_H, IDX_D, TOPK = 8, 64, 128
BUCKETS, MAX_DIST = 32, 128
X_H, X_HD = 4, 256
ML_H, ML_DK, ML_DV = 4, 96, 192
SOFTCAP = 15.0
SW_H, SW_KV, SW_HD = 12, 4, 64
MEM_H, MEM_HD = 4, 64
FF = 2816
FFT = FF // P

MASK_COLS = (256, 384, 512)

TAKEN = -3.4e38
HIDDEN = -3.3e38

O_GQ, O_GK, O_GV, O_GA, O_GZ = 0, 512, 1024, 2048, 2064
O_DQ, O_DK, O_DV, O_IQ, O_IK, O_IW, O_DZ = 3088, 4112, 4368, 4624, 5136, 5200, 5208
O_XQ, O_XZ, O_GATES = 6232, 7256, 8280

K_ID, K_U64, K_U128, K_ONE, K_SWA, K_DCM, K_LCM, K_HOT, K_INV = (
    0, 128, 256, 384, 512, 768, 896, 1024, 1408)
K_ALL = 1440

V_PRE, V_MEM, V_GLA, V_MIX0, V_FFN0, V_KV, V_MIX1, V_FFN1, V_MEM0, V_MEM1 = (
    0, 8, 16, 18, 26, 34, 42, 50, 58, 66)
V_EPS, V_BG, V_SINK = 74, 82, 90
V_ALL = 102
V_COLS = V_ALL + DSA_H

LINE = 512
LINE_HEAD = (LINE + 1) * P

TURN = (6.28125, 0.0019350051879882812, 3.0199159795074593e-07)
PI_IN = 3.1415925


def swa_columns():
    order = []
    for block in range(SW_H // 2):
        for half in range(2):
            order.append(6 * (block // 3) + 3 * half + block % 3)
    return order


SWA_ORDER = swa_columns()


def slots():
    out = []

    def full(w, col, r0=0, rt=KT, n=C):
        out.append([(w, r0, rt, col, n, 0)])

    def run(w, col, n, **k):
        for c in range(0, n, C):
            full(w, col + c, **k)

    out.append([("w_in", 0, KT, O_IK, 64, 0), ("w_in", 0, KT, O_IK, 64, 64),
                ("w_in", 0, KT, O_GA, 16, 128), ("w_in", 0, KT, O_IW, 8, 144)])
    run("w_in", O_IQ, 512)
    run("w_in", O_GQ, 512)
    run("w_in", O_GK, 512)
    run("w_in", O_GV, 1024)
    run("w_in", O_GZ, 1024)
    for c in range(4):
        full("w_in", O_GATES + C * c)
        full("w_gla_out", C * c)
    run("w_in", O_DK, 256)
    run("w_in", O_DQ, 1024)
    run("w_in", O_DV, 256)
    run("w_in", O_DZ, 1024)
    for c in range(4):
        full("w_in", O_GATES + D + C * c)
        full("w_dsa_out", C * c)
    run("w_mem_kv", 0, 2048)
    run("w_in", O_XQ, 1024)
    run("w_in", O_XZ, 1024)
    for c in range(4):
        full("w_in", O_GATES + 2 * D + C * c)
        full("w_x_out", C * c)
    run("w_o", 0, 1024)
    for layer in range(2):
        if layer == 0:
            out.append([("w_in_a", 0, KT, 0, 192, 0), ("w_in_a", 0, KT, 2304, 8, 192)])
            for c in range(1, 4):
                full("w_in_a", 192 * c, n=192)
            for h in range(ML_H):
                full("w_in_a", 192 * (4 + h), n=192)
                full("w_in_a", 1536 + C * h if h < 3 else 2312)
        else:
            full("w_kv", 0)
            full("w_kv", 256)
            for c in range(3):
                out.append([("w_in_b", 0, KT, 64 * SWA_ORDER[4 * c + i], 64, 64 * i) for i in range(4)])
            full("w_in_b", 768)
        for c in range(2):
            full(f"w_mem_kv_{layer}", C * c)
        run(f"w_out_{layer}", 0, 1024)
        for c in range(FF // C):
            full(f"w_ffn_in_{layer}", C * c)
            full(f"w_ffn_in_{layer}", FF + C * c)
        for c in range(4):
            for r in range(0, FFT, KT):
                full(f"w_ffn_out_{layer}", C * c, r0=r, rt=min(KT, FFT - r))
    return out


NS = len(slots())


class Waits:

    def __init__(self, eng, chain):
        self.eng, self.chain, self.at, self.links = eng, chain, {}, 0

    def next(self, sem, by=1):
        self.at[sem.name] = self.at.get(sem.name, 0) + by
        self.eng.wait_ge(sem, self.at[sem.name])

    def link(self, instruction):
        self.links += 1
        instruction.then_inc(self.chain, 1)
        self.eng.wait_ge(self.chain, self.links)


def build(nc, stream, x_in, mem_in, mem2_in, consts, cols, gposts, wup, gmlb, pos_in, line, out):
    ctx = ExitStack()
    with ctx:
        def sb(name, shape, dt=F32):
            return ctx.enter_context(nc.sbuf_tensor(name, shape, dt))

        def region(name, kbytes):
            base = ctx.enter_context(ExitStack())

            def place(tensor, at, shape, dt=F32):
                with ExitStack() as inner:
                    if at:
                        inner.enter_context(nc.sbuf_tensor(f"before_{tensor}", [P, int(at * 256)], F32))
                    return inner.enter_context(nc.sbuf_tensor(tensor, shape, dt))

            def close():
                base.enter_context(nc.sbuf_tensor(name, [P, kbytes * 256], F32))
            return place, close

        raw = sb("raw", [P, 2, KT, C])
        whi = sb("whi", [P, 2, KT, C], F32R)
        wlo = sb("wlo", [P, 2, KT, C], F32R)
        K = sb("K", [P, K_ALL])
        V = sb("V", [P, V_COLS])
        gpost = sb("gpost", [P, D])
        small = sb("small", [P, 512])

        place, close = region("H", 32)
        hhi = place("hhi", 0, [P, KT, T], F32R)
        hlo = place("hlo", 16, [P, KT, T], F32R)
        o_ffn = place("o_ffn", 0, [P, NT, D])
        memxb = place("memxb", 0, [P, 2, D])
        memjb = place("memjb", 8, [P, 2, D])
        xp2 = place("xp2", 0, [P, 3, NT, M])
        xpt2 = place("xpt2", 12, [P, 2, 2, T])
        mo = place("mo", 28, [P, 2, T])
        close()

        place, close = region("XR", 16)
        X = place("X", 0, [P, NT, D])
        maskt = place("maskt", 0, [P, sum(MASK_COLS)])
        linet = place("linet", 5, [DSA_H, 384])
        tbias = place("tbias", 8, [P, DSA_H, C])
        close()

        place, close = region("R", 99)
        yhi = place("yhi", 0, [P, KT, T], F32R)
        ylo = place("ylo", 16, [P, KT, T], F32R)
        merged = place("merged", 32, [P, KT, T])
        dhi = place("dhi", 64, [P, KT, T], F32R)
        dlo = place("dlo", 80, [P, KT, T], F32R)
        xn = place("xn", 64, [P, NT, D])
        junk1 = place("junk1", 0, [P, NT, C])
        junk2 = place("junk2", 92, [P, NT, C])
        o_mix = place("o_mix", 48, [P, NT, D])
        ztmp = place("ztmp", 48, [P, 2, T])
        gsig = place("gsig", 52, [P, 2, T])
        gprod = place("gprod", 56, [P, 2, T])
        ikT = place("ikT", 96, [P, T])
        iq = place("iq", 32, [P, 4, T])
        relu = place("relu", 40, [P, 4, T])
        gq = place("gq", 48, [P, GLA_H, T])
        gk = place("gk", 56, [P, GLA_H, T])
        gv = place("gv", 64, [P, NT, D])
        go = place("go", 80, [P, KT, T])
        spT = place("spT", 80, [P, T])
        la = place("la", 0, [P, NT, 512])
        gkt = place("gkt", 8, [P, GLA_H, T])
        S_t = place("S_t", 0, [P, 4, GLA_H, GLA_DV])
        gktok = place("gktok", 16, [P, NT, 512])
        attm = place("attm", 24, [P, 2, GLA_H, P])
        lscr = place("lscr", 16, [P, NT, 512])
        zbuf = place("zbuf", 32, [P, KT, T])
        gsq = place("gsq", 28, [P, KT, P])
        ge = place("ge", 26, [P, 3, T])
        wup_s = place("wup_s", 26, [GLA_RANK, 512])
        ba_s = place("ba_s", 28, [1, 512])
        dq = place("dq", 48, [P, DSA_H, T])
        dk = place("dk", 64, [P, DSA_KV, T])
        dv = place("dv", 68, [P, NT, C])
        do = place("do", 80, [P, DSA_H, T])
        pt = place("pt", 0, [P, 2, 2, NT, P])
        lg = place("lg", 16, [P, 3, 2, T])
        xq = place("xq", 48, [P, 8, T])
        mk = place("mk", 64, [P, 8, M])
        mv = place("mv", 72, [P, 2, D])
        xo = place("xo", 80, [P, 8, T])
        memx = place("memx", 64, [P, 2, D])
        memxa = place("memxa", 0, [P, 2, D])
        memj = place("memj", 72, [P, 2, D])
        mhi = place("mhi", 0, [P, KT, M], F32R)
        mlo = place("mlo", 8, [P, KT, M], F32R)
        xp = place("xp", 16, [P, 3, NT, M])
        xpt = place("xpt", 0, [P, 2, 2, T])
        mk2 = place("mk2", 77, [P, 2, M])
        mv2 = place("mv2", 79, [P, 2, M])
        lq = place("lq", 32, [P, ML_H, T])
        lk = place("lk", 40, [P, ML_H, T])
        lv = place("lv", 48, [P, NT, ML_H, ML_DV + 1])
        lo = place("lo", 61, [P, NT, 768])
        mq = place("mq", 73, [P, 2, T])
        gT = place("gT", 81, [P, T])
        Lb = place("Lb", 83, [P, ML_H, T])
        at = place("at", 8, [P, NT, T])
        hm = place("hm", 16, [P, NT, ML_H, ML_DV])
        yahi = place("yahi", 32, [P, KT, T], F32R)
        yalo = place("yalo", 0, [P, KT, T], F32R)
        ljunk = place("ljunk", 94, [P, ML_DV])
        gmb = place("gmb", 91, [P, 768])
        bhi = place("bhi", 0, [P, KT, T], F32R)
        blo = place("blo", 16, [P, KT, T], F32R)
        sk = place("sk", 32, [P, NT, C])
        sv = place("sv", 36, [P, NT, C])
        sq = place("sq", 40, [P, 3, NT, C])
        qrT = place("qrT", 40, [P, 6, T])
        mqb = place("mqb", 52, [P, 2, T])
        ra = place("ra", 56, [P, NT, C])
        rb = place("rb", 92, [P, NT, C])
        sqr = place("sqr", 62, [P, 3, NT, C])
        so = place("so", 62, [P, 6, T])
        skr = place("skr", 81, [P, NT, C])
        krT = place("krT", 85, [P, 2, T])
        slg = place("slg", 16, [P, 3, NT, C])
        spt = place("spt", 0, [P, 2, 7, P])
        cs = place("cs", 97, [P, 2, NT, 32])
        ahi = place("ahi", 0, [P, FFT, T], F32R)
        alo = place("alo", 44, [P, FFT, T], F32R)
        fa = place("fa", 88, [P, 2, T])
        fs = place("fs", 92, [P, 2, T])
        close()

        PS = ctx.enter_context(nc.psum_tensor("PS", [P, 8, 512], F32))

        ident = K[:, K_ID:K_ID + P]
        u64 = K[:, K_U64:K_U64 + P]
        u128 = K[:, K_U128:K_U128 + P]
        ones = K[:, K_ONE:K_ONE + P]
        swa = K[:, K_SWA:K_SWA + C]
        dcm = K[:, K_DCM:K_DCM + P]
        lcm = K[:, K_LCM:K_LCM + P]
        hot = K[0:BUCKETS, K_HOT:K_HOT + 384]
        inv = K[:, K_INV:K_INV + 32]
        relb_v = V[0:BUCKETS, V_ALL:V_COLS]
        epsv = V[:, V_EPS:V_EPS + 1]

        ss = small[:, 0:16]
        root = small[:, 16:32]
        rstd = small[:, 32:48]
        iwt = small[:, 48:80].rearrange("p (t h) -> p t h", t=NT)
        nmax = small[:, 80:88].rearrange("p (b t) -> p b t", b=2)
        psum_ = small[:, 340:348].rearrange("p (b t) -> p b t", b=2)
        prec = small[:, 360:368].rearrange("p (b t) -> p b t", b=2)
        top8 = small[:, 96:104]
        dec = small[:, 104:136].rearrange("p (h c) -> p h c", h=GLA_H)
        lgt = small[:, 136:168].rearrange("p (t g) -> p t g", t=NT)
        lex = small[:, 184:200].rearrange("p (t h) -> p t h", t=NT)
        lgf = small[:, 200:216].rearrange("p (t h) -> p t h", t=NT)
        bi = small[:, 216:280].rearrange("p (s j h) -> p s j h", s=4, j=4)
        rstd16 = small[:, 280:296]
        nsink = small[:, 296:308]
        esink = small[:, 352:360].rearrange("p (b t) -> p b t", b=2)
        part = small[:, 368:384].rearrange("p (t c) -> p t c", t=NT)
        posf = small[:, 312:316]
        posi = small[:, 316:320].bitcast(I32)
        lden = small[:, 320:324]
        blast = small[:, 324:332]

        def seen(qt):
            return maskt[:, sum(MASK_COLS[:qt - 1]):sum(MASK_COLS[:qt])]

        def row_order(m):
            first = 2 * (m % 2)
            return [first, first + 1] + [b for b in range(KT) if b // 2 != m % 2]

        def logit_banks(u):
            return 2 * (u % 2) + (4 if u < 2 else 0)

        def score_bank(s):
            bank, at_ = ((4, 0), (5, 0), (6, 0), (5, 384))[s]
            return PS[:, bank, at_:at_ + T - s * P]

        S = {}

        def sem(name):
            S[name] = ctx.enter_context(nc.semaphore(name))
            return S[name]

        raw_ready = [sem(f"raw_ready{p}") for p in range(2)]
        hi_ready = [sem(f"hi_ready{p}") for p in range(2)]
        lo_ready = [sem(f"lo_ready{p}") for p in range(2)]
        slot_used = [sem(f"slot_used{p}") for p in range(2)]
        pair_free = [sem(f"pair_free{p}") for p in range(2)]
        for name in """x_loaded0 x_loaded1 x_loaded2 x_loaded3 vectors_loaded ident_loaded tables_loaded gate_w_loaded
                gpost_loaded gml_loaded out_stored norm_root xn_ready mem_root memn_ready norm_turned hhi_ready
                hlo_ready act_chain dve_chain pool_chain z_gain z_prod y_hi y_lo merged_ready special_ready
                iw_turned la_psum la_exp la_ready b_psum eb_ready ediff_ready ekt_ready gk_ready kt_turned
                kt_copied att_psum att_ready gla_upd S_ready go_psum go_copied sq_ready ssq_psum gla_root
                gla_rstd rs_psum mem_loaded line_ready line_stored tbias_loaded idx_psum relu_ready relu_used
                score_masked lg_psum lg_ready p_exp p_norm p_turned pt_ready pv_psum o_copied o_sq o_sum o_root
                x_new gt_turned gate_soft gate_abs gate_exp logf_ready cl_psum bi_ready lb_psum lb_ready
                lsc_psum lw_arg lw_exp at_ready num_psum hm_ready hm_root hm_done hm_turned rope_arg rope_sin
                rope_done rope_turned rot_copied ffn_a ffn_hi ffn_lo ffo_free ones_ready o_half pos_loaded x_again
                pe_chain""".split():
            sem(name)

        block = ctx.enter_context(nc.Block())

        @block.tensor
        def _(pe):
            w = Waits(pe, S["pe_chain"])
            n = m = 0

            def three(out, k, n_k, lhs, rhs):
                (lh, ll), (rh, rl) = lhs, rhs
                nc.tensor.matmul(out, lh, rh, start=(k == 0), stop=False)
                nc.tensor.matmul(out, lh, rl, start=False, stop=False)
                return nc.tensor.matmul(out, ll, rh, start=False, stop=(k == n_k - 1))

            def slot_begin():
                pe.wait_ge(lo_ready[n % 2], n // 2 + 1)
                if m >= 2:
                    pe.wait_ge(pair_free[m % 2], m // 2)

            def gemm_features(hi, lo, groups=(0, P), tokens=T, arrival=None):
                nonlocal n, m
                slot_begin()
                p = n % 2
                for g, c in enumerate(groups):
                    for i, k in enumerate(row_order(m) if arrival is normed else range(KT)):
                        if arrival and g == 0:
                            arrival(i)
                        last = three(PS[:, 2 * (m % 2) + g, 0:tokens], i, KT,
                                     (whi[:, p, k, c:c + P], wlo[:, p, k, c:c + P]), (hi[:, k, :], lo[:, k, :]))
                last.then_inc(slot_used[p], 1)
                n, m = n + 1, m + 1

            def gemm_tokens(hi, lo, width=C, tiles=NT, arrival=None):
                nonlocal n, m
                slot_begin()
                p = n % 2
                for t in range(tiles):
                    out_ = PS[:, 2 * (m % 2) + t // 2, (t % 2) * C:(t % 2) * C + width]
                    for i, k in enumerate(row_order(m) if arrival is normed else range(KT)):
                        if arrival and t == 0:
                            arrival(i)
                        last = three(out_, i, KT, (hi[:, k, t * P:t * P + P], lo[:, k, t * P:t * P + P]),
                                     (whi[:, p, k, 0:width], wlo[:, p, k, 0:width]))
                last.then_inc(slot_used[p], 1)
                n, m = n + 1, m + 1

            def stored():
                for b in range(2):
                    pe.wait_ge(pair_free[b], (m + 1 - b) // 2)

            def all_but_last_stored():
                pe.wait_ge(pair_free[m % 2], m // 2)

            def turn_normed(src, ready):
                stored()
                tiles = src.shape[1]
                for t in range(tiles):
                    w.next(ready)
                    for k in row_order(m):
                        last = nc.tensor.transpose(PS[:, k, t * P:t * P + P], src[:, t, k * P:k * P + P], ident)
                        if t == tiles - 1:
                            last.then_inc(S["norm_turned"], 1)
                w.next(S["hlo_ready"], 2)

            def normed(i):
                if i >= 2:
                    w.next(S["hlo_ready"])

            def attention(units, logits, turn, values, slot=None):
                for u in range(-2, units + 1):
                    if u + 2 < units:
                        if u >= 0:
                            w.next(S["p_exp"])
                        logits(u + 2, logit_banks(u + 2)).then_inc(S["lg_psum"], 1)
                    if slot and u == -1:
                        slot()
                        stored()
                    if 0 <= u < units:
                        w.next(S["p_norm"])
                        if u:
                            w.next(S["pt_ready"])
                        turn(u).then_inc(S["p_turned"], 1)
                    if u >= 1:
                        if u == units:
                            w.next(S["pt_ready"])
                        if u >= 2:
                            w.next(S["o_copied"])
                        values(u - 1).then_inc(S["pv_psum"], 1)
                w.next(S["p_exp"], 2)
                w.next(S["o_copied"])

            def memory_attention(heads, parts, values_, cross, slot=None):
                p_, pt_ = (xp, xpt) if cross else (xp2, xpt2)

                def logits(h, b):
                    ps_ = parts(h)
                    for t in range(NT):
                        for i, (q_, k_, (rows, kt)) in enumerate(ps_):
                            last = nc.tensor.matmul(PS[:, b + t // 2, (t % 2) * C:(t % 2) * C + M],
                                                    q_[rows, kt, t * P:t * P + P], k_[rows, kt, :],
                                                    start=(i == 0), stop=(i == len(ps_) - 1))
                    return last

                def turn(h):
                    for j in range(2):
                        for t in range(NT):
                            last = nc.tensor.transpose(PS[:, 4 + j, t * P:t * P + P], p_[:, h % 3, t, j * P:j * P + P], ident)
                    return last

                def values(h):
                    for v in range(2 if cross else 1):
                        for j in range(2):
                            if cross:
                                last = nc.tensor.matmul(PS[:, 6 + v, :], values_[:, j, h * X_HD + v * P:h * X_HD + v * P + P],
                                                        pt_[:, h % 2, j, :], start=(j == 0), stop=(j == 1))
                            else:
                                r = MEM_HD * (h % 2)
                                last = nc.tensor.matmul(PS[r:r + MEM_HD, 6, :], values_[:, j, h * MEM_HD:h * MEM_HD + MEM_HD],
                                                        pt_[:, h % 2, j, :], start=(j == 0), stop=(j == 1))
                    return last

                attention(heads, logits, turn, values, slot)

            def index_scores(qt, half):
                for h in range(4 * half, 4 * half + 4):
                    if qt > 1 or half:
                        w.next(S["relu_ready"])
                    r = slice(IDX_D * (h % 2), IDX_D * (h % 2) + IDX_D)
                    nc.tensor.matmul(PS[:, 4 + h % 4, 0:(qt + 1) * P], iq[r, h // 2, qt * P:qt * P + P], ikT[r, 0:(qt + 1) * P],
                                     start=True, stop=True).then_inc(S["idx_psum"], 1)

            def merge():
                for c in range(4):
                    gemm_features(hhi, hlo)
                    if c == 0:
                        w.next(S["y_lo"], 4)
                    gemm_features(yhi, ylo)

            pe.wait_ge(S["ident_loaded"], 16)
            turn_normed(xn, S["xn_ready"])
            gemm_features(hhi, hlo, arrival=normed)
            for c in range(2):
                gemm_features(hhi, hlo)
            pe.wait_ge(S["tables_loaded"], 16)
            for t in range(NT):
                nc.tensor.transpose(PS[:, 4, t * 32:t * 32 + 32], spT[0:32, t * P:t * P + P], ident[0:32, 0:32])
            nc.tensor.matmul(PS[0:DSA_H, 5, 0:384], relb_v, hot, start=True, stop=True).then_inc(S["iw_turned"], 1)
            for c in range(4):
                gemm_features(hhi, hlo)
                if c == 0:
                    stored()
                    w.next(S["special_ready"])
                    w.next(S["line_ready"])
                index_scores(1 + c // 2, c % 2)
            for c in range(4):
                gemm_tokens(hhi, hlo)
                if c < 2:
                    index_scores(3, c)
            w.next(S["relu_ready"], 4)

            stored()
            pe.wait_ge(S["gate_w_loaded"], 32)
            for t in range(NT):
                nc.tensor.matmul(PS[:, 4 + t, :], spT[0:GLA_RANK, t * P:t * P + P], wup_s[:, :], start=True, stop=False)
                last = nc.tensor.matmul(PS[:, 4 + t, :], ones[0:1, :], ba_s[:, :], start=False, stop=True)
            last.then_inc(S["la_psum"], 1)
            gemm_features(hhi, hlo)
            w.next(S["la_ready"])
            for h in range(GLA_H):
                for t in range(NT):
                    last = nc.tensor.matmul(PS[:, 4 + h, t * P:t * P + P], la[:, t, h * P:h * P + P], u64, start=True, stop=True)
                last.then_inc(S["b_psum"], 1)
            for c in range(2):
                gemm_features(hhi, hlo)
            for h in range(GLA_H):
                w.next(S["gk_ready"])
                for t in range(NT):
                    last = nc.tensor.transpose(PS[:, 4 + h, t * P:t * P + P], gkt[:, h, t * P:t * P + P], ident)
                last.then_inc(S["kt_turned"], 1)
            w.next(S["kt_copied"], GLA_H)

            def gla_products(t):
                tk = slice(t * P, t * P + P)
                for h in range(GLA_H):
                    last = nc.tensor.matmul(PS[:, 2, h * P:h * P + P], gk[:, h, tk], gq[:, h, tk], start=True, stop=True)
                last.then_inc(S["att_psum"], 1)

            def gla_update(c):
                if c == 2 * NT - 1:
                    return
                if c >= 2:
                    pe.wait_ge(S["S_ready"], c - 1)
                t, r = c // 2, slice(64 * (c % 2), 64 * (c % 2) + 64)
                for h in range(GLA_H):
                    last = nc.tensor.matmul(PS[:, (0 if c % 2 else 5) + h // 2, (h % 2) * C:(h % 2) * C + GLA_DV],
                                            gktok[r, t, h * P:h * P + P], gv[r, t, h * GLA_DV:(h + 1) * GLA_DV],
                                            start=True, stop=True)
                last.then_inc(S["gla_upd"], 1)

            def gla_square_sums(t):
                w.next(S["sq_ready"])
                for h in range(GLA_H):
                    for v in range(2):
                        last = nc.tensor.matmul(PS[:, 3, 4 * t + h:4 * t + h + 1], gsq[:, 2 * h + v, :],
                                                ones[:, 0:1], start=(v == 0), stop=(v == 1))
                last.then_inc(S["ssq_psum"], 1)

            gla_products(0)
            gla_update(0)
            gla_update(1)
            for t in range(NT):
                w.next(S["att_ready"])
                if t + 1 < NT:
                    gla_products(t + 1)
                    gla_update(2 * t + 2)
                pe.wait_ge(S["S_ready"], 2 * t + 1)
                if t:
                    w.next(S["go_copied"])
                for h in range(GLA_H):
                    for v in range(2):
                        i = (h % 2) * 2 + v
                        vc = slice(h * GLA_DV + v * P, h * GLA_DV + v * P + P)
                        bank = 4 if h < 2 else 7
                        nc.tensor.matmul(PS[:, bank, i * P:i * P + P], gv[:, t, vc], attm[:, t % 2, h, :], start=True, stop=False)
                        if t:
                            nc.tensor.matmul(PS[:, bank, i * P:i * P + 64], S_t[:, (2 * t) % 4, h, v * P:v * P + P],
                                             gq[:, h, t * P:t * P + 64], start=False, stop=False)
                        last = nc.tensor.matmul(PS[:, bank, i * P + 64:i * P + P], S_t[:, (2 * t + 1) % 4, h, v * P:v * P + P],
                                                gq[:, h, t * P + 64:t * P + P], start=False, stop=True)
                last.then_inc(S["go_psum"], 1)
                if t + 1 < NT:
                    gla_update(2 * t + 3)
                if t:
                    gla_square_sums(t - 1)
            gla_square_sums(NT - 1)
            w.next(S["go_copied"])
            gemm_features(hhi, hlo)
            w.next(S["gla_rstd"])
            for h in range(GLA_H):
                for t in range(NT):
                    last = nc.tensor.matmul(PS[:, 4 + h, t * P:t * P + P],
                                            rstd16[:, 4 * t + h:4 * t + h + 1].broadcast_to([P, P]), ident, start=True, stop=True)
            last.then_inc(S["rs_psum"], 1)
            merge()

            for c in range(5):
                gemm_features(hhi, hlo)
            all_but_last_stored()

            def logits(u, b):
                qt, heads = u // 4, 2 * (u % 4)
                for i in range(2):
                    last = nc.tensor.matmul(PS[:, b + i, 0:(qt + 1) * P], dq[:, heads + i, qt * P:qt * P + P],
                                            dk[:, heads // 4, 0:(qt + 1) * P], start=True, stop=True)
                return last

            def turn(u):
                for i in range(2):
                    for b in range(u // 4 + 1):
                        last = nc.tensor.transpose(PS[:, 4 + i, b * P:b * P + P], lg[:, u % 3, i, b * P:b * P + P], ident)
                return last

            def values(u):
                qt, kv = u // 4, u % 4 // 2
                for i in range(2):
                    for b in range(qt + 1):
                        last = nc.tensor.matmul(PS[:, 6, i * P:i * P + P], dv[:, b, kv * P:kv * P + P], pt[:, u % 2, i, b, :],
                                                start=(b == 0), stop=(b == qt))
                return last

            attention(4 * NT, logits, turn, values, lambda: gemm_tokens(hhi, hlo))
            for c in range(4):
                gemm_features(hhi, hlo)
            merge()

            turn_normed(memx, S["memn_ready"])
            for c in range(4):
                gemm_features(mhi, mlo, tokens=M, arrival=None if c else normed)
            for c in range(4):
                gemm_tokens(mhi, mlo, tiles=2)
            for c in range(3):
                gemm_features(hhi, hlo)
            all_but_last_stored()
            memory_attention(X_H, lambda h: [(xq, mk, (slice(0, P), 2 * h + i)) for i in range(2)], mv, True,
                             lambda: gemm_features(hhi, hlo))
            for c in range(4):
                gemm_features(hhi, hlo)
            merge()

            def pair_split(i):
                if i % 2 == 0:
                    w.next(S["y_lo"])

            for c in range(4):
                gemm_tokens(dhi, dlo, arrival=None if c else pair_split)

            def feed_forward():
                nonlocal n, m
                turn_normed(xn, S["xn_ready"])
                h0 = w.at[S["hlo_ready"].name]
                w.at[S["hlo_ready"].name] += 6
                order = row_order(m)
                a, b = n % 2, (n + 1) % 2
                ga, gb = m % 2, (m + 1) % 2
                ka, kb = n // 2, (n + 1) // 2
                ma, mb = m // 2, (m + 1) // 2
                with pe.Fori(0, FFT // 2) as i:
                    for p, g, kk, mm in ((a, ga, ka, ma), (b, gb, kb, mb)):
                        pe.wait_ge(lo_ready[p], i + (kk + 1))
                        pe.wait_ge(pair_free[g], i + mm)
                        for j in range(2):
                            for at_, k in enumerate(order):
                                if p == a and j == 0 and at_ >= 2:
                                    pe.wait_ge(S["hlo_ready"], h0 + at_ - 1)
                                last = three(PS[:, 2 * g + j, :], at_, KT,
                                             (whi[:, p, k, j * P:j * P + P], wlo[:, p, k, j * P:j * P + P]),
                                             (hhi[:, k, :], hlo[:, k, :]))
                        last.then_inc(slot_used[p], 1)
                n, m = n + FFT, m + FFT
                for c in range(4):
                    if c == 1:
                        stored()
                    if c >= 2:
                        w.next(S["ffo_free"])
                    for r in range(0, FFT, KT):
                        if c == 0:
                            w.next(S["ffn_lo"], min(KT, FFT - r) // 2)
                        pe.wait_ge(lo_ready[n % 2], n // 2 + 1)
                        p = n % 2
                        rows = min(KT, FFT - r)
                        for t in range(NT):
                            for k in range(rows):
                                last = three(PS[:, 4 * ((c + 1) % 2) + t, 0:C], r + k, FFT,
                                             (ahi[:, r + k, t * P:t * P + P], alo[:, r + k, t * P:t * P + P]),
                                             (whi[:, p, k, :], wlo[:, p, k, :]))
                        last.then_inc(slot_used[p], 1)
                        n += 1
                w.next(S["ffo_free"], 2)

            def memory_parts(q_):
                return lambda h: [(q_, mk2, (slice(MEM_HD * (h % 2), MEM_HD * (h % 2) + MEM_HD), h // 2))]

            turn_normed(xn, S["xn_ready"])
            gates = slice(ML_DK, ML_DK + 8)
            for c in range(4):
                gemm_features(hhi, hlo, groups=(0, ML_DK), arrival=None if c else normed)
                if c == 1:
                    all_but_last_stored()
                    for t in range(NT):
                        last = nc.tensor.transpose(PS[:, 4, t * 8:t * 8 + 8], gT[gates, t * P:t * P + P], ident[gates, gates])
                    last.then_inc(S["gt_turned"], 1)
                elif c == 2:
                    w.next(S["logf_ready"])
                    nc.tensor.matmul(PS[:, 4, 0:16], u128, small[:, 200:216], start=True, stop=True).then_inc(S["cl_psum"], 1)
            w.next(S["bi_ready"])
            for h in range(ML_H):
                for t in range(NT):
                    last = nc.tensor.matmul(PS[:, 4 + h, t * P:t * P + P], lgf[:, t, h:h + 1].broadcast_to([P, P]), u128,
                                            start=True, stop=True)
            last.then_inc(S["lb_psum"], 1)
            for h in range(ML_H):
                gemm_tokens(hhi, hlo, width=ML_DV)
                w.next(S["hm_ready"] if h else S["lb_ready"])
                all_but_last_stored()
                for s in range(NT):
                    last = nc.tensor.matmul(score_bank(s), lk[0:ML_DK, h, s * P:s * P + P], lq[0:ML_DK, h, s * P:T],
                                            start=True, stop=True)
                last.then_inc(S["lsc_psum"], 1)
                if h < 3:
                    gemm_tokens(hhi, hlo)
                else:
                    gemm_features(hhi, hlo)
                all_but_last_stored()
                w.next(S["at_ready"])
                for t in range(NT):
                    for s in range(t + 1):
                        last = nc.tensor.matmul(PS[:, 6 + t // 2, (t % 2) * C:(t % 2) * C + ML_DV + 1],
                                                at[:, s, t * P:t * P + P], lv[:, s, h, :], start=(s == 0), stop=(s == t))
                last.then_inc(S["num_psum"], 1)
            w.next(S["hm_ready"])
            turn_normed(memxa, S["memn_ready"])
            gemm_features(mhi, mlo, tokens=M, arrival=normed)
            stored()
            memory_attention(MEM_H, memory_parts(mq), mv2, False, lambda: gemm_tokens(mhi, mlo, tiles=2))
            for k in range(6):
                if k >= 4:
                    w.next(S["y_lo"])
                for t in range(NT):
                    if k == 0:
                        w.next(S["hm_done"])
                    last = nc.tensor.transpose(PS[:, 4 + k % 4, t * P:t * P + P],
                                               hm[:, t].rearrange("p h d -> p (h d)")[:, k * P:k * P + P], ident)
                last.then_inc(S["hm_turned"], 1)
            w.next(S["y_lo"], 5)
            for c in range(4):
                gemm_tokens(yahi, yalo)
            feed_forward()

            turn_normed(xn, S["xn_ready"])
            w.next(S["hlo_ready"], 2)
            gemm_tokens(hhi, hlo, arrival=normed)
            w.next(S["hlo_ready"], 2)
            gemm_tokens(hhi, hlo)

            def turn_rotated(i):
                w.next(S["rope_done"])
                for j in range(2):
                    b = 2 * i + j
                    if b >= 4:
                        w.next(S["rot_copied"])
                    for t in range(NT):
                        src = (sqr[:, i - 1] if i else skr)[:, t, j * P:j * P + P]
                        last = nc.tensor.transpose(PS[:, 4 + b % 4, t * P:t * P + P], src, ident)
                    last.then_inc(S["rope_turned"], 1)

            turn_rotated(0)
            w.next(S["hlo_ready"], 4)
            gemm_tokens(bhi, blo)
            for c in range(1, 3):
                gemm_tokens(bhi, blo)
                turn_rotated(c)
            gemm_features(bhi, blo)
            turn_rotated(3)
            w.next(S["rot_copied"], 4)
            turn_normed(memxb, S["memn_ready"])
            w.next(S["hlo_ready"], 6)

            def memory_slots():
                gemm_features(mhi, mlo, tokens=M)
                gemm_tokens(mhi, mlo, tiles=2)

            def logits(h, bank):
                place_, kv = SWA_ORDER.index(h), h // 3
                r = slice(SW_HD * (kv % 2), SW_HD * (kv % 2) + SW_HD)
                for t in range(NT):
                    k0 = max(t - 1, 0) * P
                    o0 = 0 if t else P
                    last = nc.tensor.matmul(PS[:, bank + t // 2, (t % 2) * C + o0:(t % 2) * C + C],
                                            qrT[r, place_ // 2, t * P:t * P + P], krT[r, kv // 2, k0:t * P + P], start=True, stop=True)
                return last

            def turn(h):
                for j in range(7):
                    t, b = (j + 1) // 2, (j + 1) % 2
                    last = nc.tensor.transpose(PS[:, 4 + j // 4, (j % 4) * P:(j % 4) * P + P], slg[:, h % 3, t, b * P:b * P + P], ident)
                return last

            def values(h):
                kv = h // 3
                ro = slice(SW_HD * (h % 2), SW_HD * (h % 2) + SW_HD)
                for t in range(NT):
                    for b in range(0 if t else 1, 2):
                        last = nc.tensor.matmul(PS[ro, 6, t * P:t * P + P], sv[:, t + b - 1, kv * SW_HD:(kv + 1) * SW_HD],
                                                spt[:, h % 2, 2 * t + b - 1, :], start=(b == (0 if t else 1)), stop=(b == 1))
                return last

            attention(SW_H, logits, turn, values, memory_slots)
            memory_attention(MEM_H, memory_parts(mqb), mv2, False)
            for c in range(4):
                gemm_tokens(yhi, ylo, arrival=None if c else pair_split)
            feed_forward()
            assert n == NS

        @block.scalar
        def _(act):
            w = Waits(act, S["act_chain"])
            n = m = 0

            def copy(out_, in_, scale=1.0, func=ACT.Copy):
                return nc.scalar.activation(out_, in_, func, scale=scale)

            def split(s):
                if s < NS:
                    act.wait_ge(raw_ready[s % 2], 16 * (s // 2 + 1))
                    if s >= 2:
                        act.wait_ge(slot_used[s % 2], s // 2)
                    copy(whi[:, s % 2], raw[:, s % 2]).then_inc(hi_ready[s % 2], 1)

            def pair():
                return PS[:, 2 * (m % 2):2 * (m % 2) + 2, :]

            def pair_tokens():
                return pair().rearrange("p b (u c) -> p (b u) c", u=2)

            def taken(instruction):
                nonlocal n, m
                instruction.then_inc(pair_free[m % 2], 1)
                split(n + 2)
                n, m = n + 1, m + 1

            def computed():
                act.wait_ge(slot_used[n % 2], n // 2 + 1)

            def store_features(dst, c, scale=1.0, tokens=T):
                computed()
                taken(copy(dst[:, 2 * c:2 * c + 2, :], pair()[:, :, 0:tokens], scale))

            def store_tokens(dst, c, scale=1.0, tiles=NT, func=ACT.Copy):
                computed()
                taken(copy(dst[:, :, c * C:(c + 1) * C], pair_tokens()[:, 0:tiles, :], scale, func))

            def passed(splits=True):
                nonlocal n, m
                if splits:
                    split(n + 2)
                n, m = n + 1, m + 1

            def row_roots(src, junk, tiles, out_, arrival, signal):
                for t in range(tiles):
                    arrival(t)
                    w.link(nc.scalar.activation(junk[:, t], src[:, t], ACT.Square, accum_out=ss[:, out_ + t:out_ + t + 1]))
                    nc.scalar.activation(root[:, out_ + t:out_ + t + 1], ss[:, out_ + t:out_ + t + 1], ACT.Sqrt, bias=epsv,
                                         scale=1.0 / D).then_inc(S[signal], 1)

            def new_roots(o):
                row_roots(X, o, NT, 4, lambda t: w.next(S["x_new"]), "norm_root")

            def memory_roots(src, junk, loads):
                row_roots(src, junk, 2, 8, lambda t: act.wait_ge(S["mem_loaded"], 16 * loads), "mem_root")

            def upper(gain, hi, ks=None):
                for k in ks or row_order(m):
                    w.next(S["norm_turned"])
                    copy(hi[:, k, :], PS[:, k, 0:hi.shape[2]], V[:, gain + k:gain + k + 1]).then_inc(S["hhi_ready"], 1)

            def root_table():
                nc.scalar.activation(root[:, 12:13], epsv, ACT.Sqrt)

            def o_squares(c, banks, junk):
                if c:
                    w.next(S["o_sq"], 2)
                for half in (1, 0):
                    if half == 0:
                        w.next(S["o_half"])
                    for t in (2 * half, 2 * half + 1):
                        last = nc.scalar.activation(junk[:, t, :], banks[:, t, :], ACT.Square, accum_out=part[:, t, c:c + 1])
                    last.then_inc(S["o_sq"], 1)

            def o_roots():
                w.next(S["o_sq"], 2)
                w.next(S["o_sum"])
                nc.scalar.activation(root[:, 0:NT], ss[:, 0:NT], ACT.Sqrt, bias=epsv, scale=1.0 / D)\
                    .then_inc(S["o_root"], 1)

            def mixed(junk):
                root_table()
                for c in range(4):
                    computed()
                    o_squares(c, pair_tokens(), junk)
                    passed(splits=c < 3)
                o_roots()

            def output_part(src, c, dst):
                copy(dst, src[:, 2 * c:2 * c + 2, :]).then_inc(S["y_hi"], 1)

            def z_gate(c):
                computed()
                taken(copy(zbuf[:, 2 * c:2 * c + 2, :], pair(), func=ACT.Silu))

            def z_products(o):
                for c in range(4):
                    computed()
                    taken(copy(ztmp[:, :, :], pair(), func=ACT.Silu))
                    output_upper(o, c)

            def output_upper(o, c):
                w.next(S["z_prod"])
                copy(yhi[:, 2 * c:2 * c + 2, :], o[:, 2 * c:2 * c + 2, :]).then_inc(S["y_hi"], 1)

            def merge(last=False):
                for c in range(4):
                    computed()
                    if c:
                        act.wait_ge(pair_free[(m + 1) % 2], (m + 1) // 2)
                    taken(copy(gsig[:, :, :], pair(), func=ACT.Sigmoid))
                    passed()
                    if last:
                        w.next(S["merged_ready"])
                        copy(dhi[:, 2 * c:2 * c + 2, :], merged[:, 2 * c:2 * c + 2, :]).then_inc(S["y_hi"], 1)

            def attention(units, exps, turned, output, beside=None, slot=None):
                for u in range(-2, units + 1):
                    if 0 <= u < units:
                        w.next(S["p_turned"])
                        turned(u).then_inc(S["pt_ready"], 1)
                        if beside and u < 3:
                            beside(u)
                    if u + 2 < units:
                        w.next(S["lg_ready"])
                        exps(u + 2).then_inc(S["p_exp"], 1)
                    if slot and u == -1:
                        slot()
                    if u >= 1:
                        w.next(S["pv_psum"])
                        output(u - 1).then_inc(S["o_copied"], 1)
                w.next(S["o_copied"], units)

            def memory_attention(heads, cross, dst, beside=None, slot=None):
                p_, pt_ = (xp, xpt) if cross else (xp2, xpt2)

                def exps(h):
                    for t in range(NT):
                        last = nc.scalar.activation(p_[:, h % 3, t, :],
                                                    PS[:, logit_banks(h) + t // 2, (t % 2) * C:(t % 2) * C + C], ACT.Exp,
                                                    bias=nmax[:, h % 2, t:t + 1], accum_out=psum_[:, h % 2, t:t + 1])
                    return last

                def output(h):
                    if cross:
                        return copy(dst[:, 2 * h:2 * h + 2, :], PS[:, 6:8, :])
                    r = slice(MEM_HD * (h % 2), MEM_HD * (h % 2) + MEM_HD)
                    return copy(dst[r, h // 2, :], PS[r, 6, :])

                attention(heads, exps, lambda h: copy(pt_[:, h % 2], PS[:, 4:6, :]), output, beside, slot)

            def index_relu(qt, half):
                for h in range(4 * half, 4 * half + 4):
                    if qt > 1 or half:
                        w.next(S["relu_used"])
                    w.next(S["idx_psum"])
                    copy(relu[:, h % 4, 0:(qt + 1) * P], PS[:, 4 + h % 4, 0:(qt + 1) * P], func=ACT.Relu)\
                        .then_inc(S["relu_ready"], 1)

            act.wait_ge(S["vectors_loaded"], 16)
            row_roots(X, o_mix, NT, 4, lambda t: act.wait_ge(S[f"x_loaded{t}"], 16), "norm_root")
            split(0)
            upper(V_PRE, hhi)
            split(1)
            computed()
            copy(ikT[:, :], PS[:, 0, :])
            taken(copy(spT[0:32, :], PS[0:32, 1, :]))
            for c in range(2):
                store_features(iq, c)
            w.next(S["iw_turned"])
            copy(linet[:, :], PS[0:DSA_H, 5, 0:384]).then_inc(S["line_ready"], 1)
            for c in range(2):
                store_features(gq, c, GLA_DK ** -0.5)
                index_relu(1, c)
            for c in range(2):
                store_features(gk, c)
                index_relu(2, c)
            for c in range(4):
                store_tokens(gv, c)
                if c < 2:
                    index_relu(3, c)

            w.next(S["la_psum"])
            w.link(copy(lscr[:, :, :], PS[:, 4:8, :], func=ACT.Abs))
            w.link(copy(lscr[:, :, :], lscr[:, :, :], -1.0, ACT.Exp))
            nc.scalar.activation(lscr[:, :, :], lscr[:, :, :], ACT.Ln, bias=1.0).then_inc(S["la_exp"], 1)
            z_gate(0)
            for h in range(GLA_H):
                w.next(S["b_psum"])
                if h:
                    w.next(S["gk_ready"])
                copy(ge[:, 0, :], PS[:, 4 + h, :], 1.0 / GLA_NORM, ACT.Exp)
                copy(ge[:, 1, :], PS[:, 4 + h, :], -1.0 / GLA_NORM, ACT.Exp).then_inc(S["eb_ready"], 1)
                w.next(S["ediff_ready"])
                copy(ge[:, 2, :], ge[:, 2, :], 1.0 / GLA_NORM, ACT.Exp).then_inc(S["ekt_ready"], 1)
            z_gate(1)
            z_gate(2)
            for h in range(GLA_H):
                w.next(S["kt_turned"])
                copy(gktok[:, :, h * P:h * P + P], PS[:, 4 + h, :].rearrange("p (t d) -> p t d", t=NT))\
                    .then_inc(S["kt_copied"], 1)
            for t in range(NT):
                w.next(S["go_psum"])
                copy(go[:, 0:4, t * P:t * P + P], PS[:, 4, :].rearrange("p (v t) -> p v t", v=4))
                copy(go[:, 4:8, t * P:t * P + P], PS[:, 7, :].rearrange("p (v t) -> p v t", v=4)).then_inc(S["go_copied"], 1)
                w.next(S["go_copied"])
                if t:
                    w.next(S["ssq_psum"])
                copy(gsq[:, :, :], go[:, :, t * P:t * P + P], func=ACT.Square).then_inc(S["sq_ready"], 1)
            w.next(S["ssq_psum"])
            nc.scalar.activation(root[:, 0:16], PS[:, 3, 0:16], ACT.Sqrt, bias=epsv, scale=1.0 / GLA_DV)\
                .then_inc(S["gla_root"], 1)
            z_gate(3)
            for c in range(4):
                output_upper(go, c)
            merge()

            store_features(dk, 0)
            for c in range(4):
                store_features(dq, c, DSA_HD ** -0.5)
            def exps(u):
                L = (u // 4 + 1) * P
                for i in range(2):
                    last = nc.scalar.activation(lg[:, u % 3, i, 0:L], lg[:, u % 3, i, 0:L], ACT.Exp,
                                                bias=nmax[:, u % 2, i:i + 1], accum_out=psum_[:, u % 2, i:i + 1])
                return last

            def turned(u):
                blocks = u // 4 + 1
                return copy(pt[:, u % 2, :, 0:blocks, :], PS[:, 4:6, 0:blocks * P].rearrange("p i (b q) -> p i b q", q=P))

            def output(u):
                qt, heads = u // 4, 2 * (u % 4)
                return copy(do[:, heads:heads + 2, qt * P:(qt + 1) * P], PS[:, 6, 0:2 * P].rearrange("p (i q) -> p i q", i=2))

            attention(4 * NT, exps, turned, output, slot=lambda: store_tokens(dv, 0))
            z_products(do)
            memory_roots(memx, memj, 1)
            merge()

            upper(V_MEM, mhi)
            for c in range(4):
                store_features(mk, c, tokens=M)
            for c in range(4):
                store_tokens(mv, c, tiles=2)
            for c in range(3):
                store_features(xq, c, X_HD ** -0.5)
            memory_attention(X_H, True, xo, slot=lambda: store_features(xq, 3, X_HD ** -0.5))
            z_products(xo)
            merge(last=True)
            mixed(junk1)

            def feed_forward(gain):
                nonlocal n, m
                new_roots(o_mix)
                upper(gain, hhi)
                split(n + 1)
                sg, su = n % 2, (n + 1) % 2
                kg, ku = n // 2, (n + 1) // 2
                pg = m % 2
                r0 = w.at.get(S["ffn_a"].name, 0)
                with act.Fori(0, FFT // 2) as i:
                    act.wait_ge(slot_used[sg], i + (kg + 1))
                    copy(fs[:, :, :], PS[:, 2 * pg:2 * pg + 2, :], func=ACT.Silu).then_inc(pair_free[pg], 1)
                    act.wait_ge(raw_ready[sg], i * 16 + 16 * (kg + 2))
                    copy(whi[:, sg], raw[:, sg]).then_inc(hi_ready[sg], 1)
                    act.wait_ge(S["ffn_a"], i + (r0 + 1))
                    copy(ahi[:, bass.ds(i * 2, 2), :], fa[:, :, :]).then_inc(S["ffn_hi"], 1)
                    act.wait_ge(slot_used[su], i + (ku + 1))
                    act.wait_ge(raw_ready[su], i * 16 + 16 * (ku + 2))
                    copy(whi[:, su], raw[:, su]).then_inc(hi_ready[su], 1)
                w.at[S["ffn_a"].name] = r0 + FFT // 2
                n, m = n + FFT, m + FFT
                root_table()
                for c in range(4):
                    for r in range(0, FFT, KT):
                        act.wait_ge(slot_used[n % 2], n // 2 + 1)
                        if r + KT >= FFT:
                            o_squares(c, PS[:, 4 * ((c + 1) % 2):4 * ((c + 1) % 2) + 4, 0:C], junk2)
                        if r + KT < FFT or c < 3:
                            split(n + 2)
                        n += 1
                o_roots()

            new_roots(o_mix)
            upper(V_MIX0, hhi)
            split(n + 1)
            memory_roots(memxa, memj, 2)
            for c in range(4):
                computed()
                if c == 0:
                    copy(gT[ML_DK:ML_DK + 8, :], pair()[ML_DK:ML_DK + 8, 1, :])
                dst = (lq if c < 2 else lk)[0:ML_DK, 2 * (c % 2):2 * (c % 2) + 2, :]
                taken(copy(dst, pair()[0:ML_DK], 1.0 if c < 2 else ML_DK ** -0.5))
                if c == 1:
                    w.next(S["gate_soft"])
                    copy(lgt[:, :, :], lgt[:, :, :], 1.0 / SOFTCAP, ACT.Tanh).then_inc(S["gate_abs"], 1)
                    w.next(S["gate_exp"])
                    w.link(copy(lex[:, :, :], lgt[:, :, 4:8], func=ACT.Abs))
                    w.link(copy(lex[:, :, :], lex[:, :, :], -1.0, ACT.Exp))
                    nc.scalar.activation(lex[:, :, :], lex[:, :, :], ACT.Ln, bias=1.0).then_inc(S["la_exp"], 1)
            w.next(S["lb_psum"])
            copy(Lb[:, :, :], PS[:, 4:8, :]).then_inc(S["lb_ready"], 1)
            for h in range(ML_H):
                computed()
                taken(copy(lv[:, :, h, 0:ML_DV], pair_tokens()[:, :, 0:ML_DV]))
                w.next(S["lw_arg"])
                for s in range(NT):
                    for j in range(s, NT):
                        js = slice(j * P, j * P + P)
                        src, bias = (at[:, s, js], 0.0) if j == s else (Lb[:, h, js], bi[:, s, j, h:h + 1])
                        last = nc.scalar.activation(at[:, s, js], src, ACT.Exp, bias=bias)
                last.then_inc(S["lw_exp"], 1)
                if h < 3:
                    store_tokens(lo, h, func=ACT.Sigmoid)
                else:
                    store_features(mq, 0, MEM_HD ** -0.5)
                w.next(S["hm_ready"])
                for t in range(NT):
                    w.link(nc.scalar.activation(ljunk[:, :], hm[:, t, h, :], ACT.Square,
                                                accum_out=ss[:, 4 * t + h:4 * t + h + 1]))
            nc.scalar.activation(root[:, 0:16], ss[:, 0:16], ACT.Sqrt, bias=epsv, scale=1.0 / ML_DV).then_inc(S["hm_root"], 1)
            upper(V_MEM0, mhi)
            store_features(mk2, 0, tokens=M)
            memory_attention(MEM_H, False, mo, slot=lambda: store_tokens(mv2, 0, tiles=2))
            for k in range(6):
                w.next(S["hm_turned"])
                copy(yahi[:, k, :], PS[:, 4 + k % 4, :]).then_inc(S["y_hi"], 1)
            output_part(mo, 0, yahi[:, 6:8, :])
            mixed(junk2)
            feed_forward(V_FFN0)

            new_roots(o_ffn)
            for before, ks in ((0, row_order(m)[:2]), (2, row_order(m)[2:])):
                split_before = w.at[S["norm_turned"].name] + before
                upper(V_KV, hhi, ks)
                for i, k in enumerate(ks):
                    act.wait_ge(S["hlo_ready"], split_before + i + 1)
                    copy(bhi[:, k, :], PS[:, k, :], V[:, V_MIX1 + k:V_MIX1 + k + 1]).then_inc(S["hhi_ready"], 1)
            split(n + 1)
            for j in range(2):
                w.next(S["rope_arg"])
                copy(cs[:, j], cs[:, j], func=ACT.Sin).then_inc(S["rope_sin"], 1)

            def store_rotated(i):
                for j in range(2):
                    w.next(S["rope_turned"])
                    b = 2 * i + j
                    copy(qrT[:, b - 2, :] if i else krT[:, b, :], PS[:, 4 + b % 4, :]).then_inc(S["rot_copied"], 1)

            store_tokens(sk, 0)
            store_tokens(sv, 0)
            store_rotated(0)
            store_tokens(sq[:, 0], 0, SW_HD ** -0.5)
            memory_roots(memxb, memjb, 3)
            for c in range(1, 3):
                store_tokens(sq[:, c], 0, SW_HD ** -0.5)
                store_rotated(c)
            store_features(mqb, 0, MEM_HD ** -0.5)
            store_rotated(3)
            upper(V_MEM1, mhi)

            def memory_slots():
                store_features(mk2, 0, tokens=M)
                store_tokens(mv2, 0, tiles=2)

            def exps(h):
                for t in range(NT):
                    nc.scalar.activation(slg[:, h % 3, t, :], slg[:, h % 3, t, :], ACT.Exp, bias=nmax[:, h % 2, t:t + 1],
                                         accum_out=psum_[:, h % 2, t:t + 1])
                return nc.scalar.activation(esink[:, h % 2, :], nmax[:, h % 2, :], ACT.Exp, bias=V[:, V_SINK + h:V_SINK + h + 1])

            def output(h):
                r = slice(SW_HD * (h % 2), SW_HD * (h % 2) + SW_HD)
                return copy(so[r, h // 2, :], PS[r, 6, :])

            attention(SW_H, exps, lambda h: copy(spt[:, h % 2], PS[:, 4:6, :].rearrange("p b (j q) -> p (b j) q", q=P)[:, 0:7, :]),
                      output, slot=memory_slots)
            memory_attention(MEM_H, False, mo, lambda c: output_part(so, c, yhi[:, 2 * c:2 * c + 2, :]))
            output_part(mo, 0, yhi[:, 6:8, :])
            mixed(junk2)
            feed_forward(V_FFN1)

        @block.vector
        def _(dve):
            w = Waits(dve, S["dve_chain"])
            V_ = nc.vector
            n = m = 0

            def split(s):
                if s < NS:
                    dve.wait_ge(hi_ready[s % 2], s // 2 + 1)
                    V_.tensor_tensor(wlo[:, s % 2], raw[:, s % 2], whi[:, s % 2], ALU.subtract).then_inc(lo_ready[s % 2], 1)

            def pair():
                return PS[:, 2 * (m % 2):2 * (m % 2) + 2, :]

            def passed(count=1):
                nonlocal n, m
                for _ in range(count):
                    split(n + 2)
                    n, m = n + 1, m + 1

            def stored():
                for b in range(2):
                    dve.wait_ge(pair_free[b], (m + 1 - b) // 2)

            def norm_rows(t, src, dst, at_, roots, signal):
                w.next(roots)
                w.link(V_.reciprocal(rstd[:, at_ + t:at_ + t + 1], root[:, at_ + t:at_ + t + 1]))
                V_.tensor_scalar(dst[:, t], src[:, t], rstd[:, at_ + t:at_ + t + 1], None, ALU.mult).then_inc(signal, 1)

            def norm_memory(memory):
                for t in range(2):
                    norm_rows(t, memory, memory, 8, S["mem_root"], S["memn_ready"])

            def lower(gain, hi, lo, ks=None):
                for k in ks or row_order(m):
                    w.next(S["hhi_ready"])
                    V_.scalar_tensor_tensor(lo[:, k, :], PS[:, k, 0:hi.shape[2]], V[:, gain + k:gain + k + 1],
                                            hi[:, k, :], ALU.mult, ALU.subtract).then_inc(S["hlo_ready"], 1)

            def take_output(o, c, banks, free):
                dve.wait_ge(slot_used[n % 2], n // 2 + 1)

                def take(tiles):
                    return V_.tensor_tensor(o[:, tiles, c * C:(c + 1) * C], banks[:, tiles],
                                            gpost[:, c * C:(c + 1) * C].unsqueeze(1).broadcast_to([P, 2, C]), ALU.mult)

                take(slice(0, 2)).then_inc(S["o_half"], 1)
                w.next(S["o_sq"], 2)
                if c == 3:
                    V_.tensor_reduce(ss[:, 0:NT], part[:, :, :], AX.X, ALU.add).then_inc(S["o_sum"], 1)
                take(slice(2, 4)).then_inc(free, 1)

            def mixed(loads):
                nonlocal n, m
                dve.wait_ge(S["gpost_loaded"], 16 * loads)
                for c in range(4):
                    take_output(o_mix, c, pair().rearrange("p b (u c) -> p (b u) c", u=2), pair_free[m % 2])
                    if c < 3:
                        passed()
                n, m = n + 1, m + 1
                stored()

            def residual(o, more=True):
                w.next(S["o_root"])
                w.link(V_.reciprocal(rstd[:, 0:NT], root[:, 0:NT]))
                for t in range(NT):
                    V_.scalar_tensor_tensor(X[:, t], o[:, t], rstd[:, t:t + 1], X[:, t], ALU.mult, ALU.add).then_inc(S["x_new"], 1)
                    if more and t:
                        norm_rows(t - 1, X, xn, 4, S["norm_root"], S["xn_ready"])
                if more:
                    norm_rows(NT - 1, X, xn, 4, S["norm_root"], S["xn_ready"])

            def output_part(src, c, hi, lo_):
                w.next(S["y_hi"])
                V_.tensor_tensor(lo_, src[:, 2 * c:2 * c + 2, :], hi, ALU.subtract).then_inc(S["y_lo"], 1)

            def output_lower(o, c):
                output_part(o, c, yhi[:, 2 * c:2 * c + 2, :], ylo[:, 2 * c:2 * c + 2, :])

            def z_products(o):
                for c in range(4):
                    oc = o[:, 2 * c:2 * c + 2, :]
                    dve.wait_ge(pair_free[m % 2], m // 2 + 1)
                    V_.tensor_tensor(oc, oc, ztmp[:, :, :], ALU.mult).then_inc(S["z_prod"], 1)
                    passed()
                    output_lower(o, c)

            def merge(branch):
                nonlocal n, m
                for c in range(4):
                    mc = merged[:, 2 * c:2 * c + 2, :]
                    dve.wait_ge(pair_free[m % 2], m // 2 + 1)
                    passed()
                    dve.wait_ge(slot_used[n % 2], n // 2 + 1)
                    if branch == 0:
                        last = V_.tensor_tensor(mc, pair(), gsig[:, :, :], ALU.mult)
                        last.then_inc(pair_free[m % 2], 1)
                    else:
                        V_.tensor_tensor(gprod[:, :, :], pair(), gsig[:, :, :], ALU.mult).then_inc(pair_free[m % 2], 1)
                        dve.wait_ge(pair_free[m % 2], m // 2 + 1)
                        last = V_.tensor_tensor(mc, mc, gprod[:, :, :], ALU.add)
                        if branch == 2:
                            last.then_inc(S["merged_ready"], 1)
                        else:
                            w.link(last)
                    passed()
                    if branch == 2:
                        w.next(S["y_hi"])
                        V_.tensor_tensor(dlo[:, 2 * c:2 * c + 2, :], mc, dhi[:, 2 * c:2 * c + 2, :], ALU.subtract)\
                            .then_inc(S["y_lo"], 1)
                    if not branch:
                        take(3, 4, last=(c == 3))

            def attention(units, p, count, peaks, sink=False, beside=None, slot=0):
                def scale(u):
                    w.next(S["p_exp"])
                    sums, r = psum_[:, u % 2, 0:count], prec[:, u % 2, 0:count]
                    if sink:
                        w.link(V_.tensor_tensor(r, sums, esink[:, u % 2, :], ALU.add))
                        sums = r
                    w.link(V_.reciprocal(r, sums))
                    V_.tensor_tensor(p(u), p(u), r.unsqueeze(2).broadcast_to([P, count, p(u).shape[2]]), ALU.mult)\
                        .then_inc(S["p_norm"], 1)

                for u in range(units + 1):
                    if u >= 3:
                        w.next(S["p_turned"])
                    if u < units:
                        w.next(S["lg_psum"])
                        peaks(u).then_inc(S["lg_ready"], 1)
                    if u and not (slot and u == 2):
                        scale(u - 1)
                        if beside and u <= 3:
                            beside(u - 1)
                    if slot and u == 1:
                        scale(1)
                        passed(slot)
                w.next(S["p_turned"], 2)

            def memory_attention(heads, p_, beside=None, slot=0):
                attention(heads, lambda h: p_[:, h % 3], NT,
                          lambda h: V_.tensor_reduce(nmax[:, h % 2, :], PS[:, logit_banks(h):logit_banks(h) + 2, :]
                                                     .rearrange("p b (u c) -> p (b u) c", u=2), AX.X, ALU.max, negate=True), beside=beside, slot=slot)

            def index_sum(qt, half):
                score = seen(qt)
                for h in range(4 * half, 4 * half + 4):
                    w.next(S["relu_ready"])
                    r_, iw = relu[:, h % 4, 0:(qt + 1) * P], iwt[:, qt, h:h + 1]
                    if h == 0:
                        last = V_.tensor_scalar(score, r_, iw, None, ALU.mult)
                    else:
                        last = V_.scalar_tensor_tensor(score, r_, iw, score, ALU.mult, ALU.add)
                    last.then_inc(S["relu_used"], 1)
                    w.next(S["relu_used"])

            def take(qt, rounds, first=False, last=False):
                if first:
                    w.next(S["score_masked"])
                for r in range(rounds):
                    w.link(V_.max(top8, seen(qt)))
                    w.link(V_.match_replace(seen(qt), top8, seen(qt), TAKEN))
                if last:
                    w.link(V_.tensor_scalar(seen(qt), seen(qt), TAKEN, NEG, ALU.not_equal, ALU.mult))

            for t in range(NT):
                norm_rows(t, X, xn, 4, S["norm_root"], S["xn_ready"])
            split(0)
            lower(V_PRE, hhi, hlo)
            split(1)
            passed(3)
            w.next(S["iw_turned"])
            V_.tensor_scalar(iwt, PS[:, 4, 0:128].rearrange("p (t c) -> p t c", t=NT)[:, :, 16:24],
                             IDX_H ** -0.5, IDX_D ** -0.5, ALU.mult, ALU.mult).then_inc(S["special_ready"], 1)
            w.next(S["special_ready"])
            V_.tensor_scalar(nsink, V[:, V_SINK:V_SINK + SW_H], -1.0, None, ALU.mult)
            for c in range(2):
                passed()
                index_sum(1, c)
            for c in range(2):
                passed()
                index_sum(2, c)
                take(1, 4, first=(c == 0))
            for c in range(4):
                passed()
                if c < 2:
                    index_sum(3, c)
                    take(1, 4, last=(c == 1))
                else:
                    take(2, 4, first=(c == 2))

            w.next(S["la_exp"])
            V_.scalar_tensor_tensor(la[:, :, :], PS[:, 4:8, :], 0.0, lscr[:, :, :], ALU.min, ALU.subtract)\
                .then_inc(S["la_ready"], 1)
            passed()
            for h in range(GLA_H):
                w.next(S["eb_ready"])
                b_ = PS[:, 4 + h, :].rearrange("p (c t) -> p c t", t=64)
                w.link(V_.tensor_copy(blast, b_[:, :, 63]))
                V_.tensor_tensor(ge[:, 2, :].rearrange("p (c t) -> p c t", t=64), blast.unsqueeze(2).broadcast_to([P, 8, 64]), b_,
                                 ALU.subtract).then_inc(S["ediff_ready"], 1)
                V_.tensor_copy(dec[:, h, :], ge[:, 0, :].rearrange("p (c t) -> p c t", t=64)[:, :, 63])
                V_.tensor_tensor(gq[:, h, :], gq[:, h, :], ge[:, 0, :], ALU.mult)
                w.next(S["ekt_ready"])
                w.link(V_.tensor_tensor(gkt[:, h, :], gk[:, h, :], ge[:, 2, :], ALU.mult))
                V_.tensor_tensor(gk[:, h, :], gk[:, h, :], ge[:, 1, :], ALU.mult).then_inc(S["gk_ready"], 1)
            passed(2)
            w.next(S["kt_copied"], GLA_H)
            w.link(V_.memset(attm[:, :, :, :], 0.0))
            for t in range(NT):
                w.next(S["att_psum"])
                V_.copy_predicated(attm[:, t % 2], u64.bitcast(U32).unsqueeze(1).broadcast_to([P, GLA_H, P]),
                                   PS[:, 2, :].rearrange("p (h t) -> p h t", h=GLA_H)).then_inc(S["att_ready"], 1)
                for c in (2 * t, 2 * t + 1):
                    if c == 2 * NT - 1:
                        break
                    w.next(S["gla_upd"])
                    for h in range(GLA_H):
                        new, upd = S_t[:, (c + 1) % 4, h, :], PS[:, (0 if c % 2 else 5) + h // 2, (h % 2) * C:(h % 2) * C + C]
                        if c:
                            last = V_.scalar_tensor_tensor(new, S_t[:, c % 4, h, :], dec[:, h, c:c + 1], upd, ALU.mult, ALU.add)
                        else:
                            last = V_.tensor_copy(new, upd)
                    last.then_inc(S["S_ready"], 1)
                    w.next(S["S_ready"])
            w.next(S["gla_root"])
            V_.reciprocal(rstd16, root[:, 0:16]).then_inc(S["gla_rstd"], 1)

            def z_gain(c):
                for v in range(2):
                    V_.scalar_tensor_tensor(go[:, 2 * c + v, :], go[:, 2 * c + v, :], V[:, V_GLA + v:V_GLA + v + 1],
                                            zbuf[:, 2 * c + v, :], ALU.mult, ALU.mult).then_inc(S["z_gain"], 1)

            stored()
            for c in range(3):
                z_gain(c)
            take(2, 8, last=True)
            passed()
            stored()
            z_gain(3)
            w.next(S["rs_psum"])
            for h in range(GLA_H):
                w.next(S["z_gain"], 2)
                gh = go[:, 2 * h:2 * h + 2, :]
                V_.tensor_tensor(gh, gh, PS[:, 4 + h, :].unsqueeze(1).broadcast_to([P, 2, T]), ALU.mult).then_inc(S["z_prod"], 1)
            for c in range(4):
                output_lower(go, c)
            take(3, 0, first=True)
            merge(0)

            passed(5)
            dve.wait_ge(S["tbias_loaded"], 16)

            def peaks(u):
                qt, heads = u // 4, 2 * (u % 4)
                L = (qt + 1) * P
                near = min(L, C)
                l_ = lg[:, u % 3, :, 0:L]
                mask = seen(qt) if qt else dcm
                w.link(V_.tensor_tensor(l_, PS[:, logit_banks(u):logit_banks(u) + 2, 0:L], mask.unsqueeze(1).broadcast_to([P, 2, L]), ALU.add))
                w.link(V_.tensor_tensor(l_[:, :, L - near:L], l_[:, :, L - near:L], tbias[:, heads:heads + 2, C - near:C], ALU.add))
                return V_.tensor_reduce(nmax[:, u % 2, 0:2], l_, AX.X, ALU.max, negate=True)

            attention(4 * NT, lambda u: lg[:, u % 3, :, 0:(u // 4 + 1) * P], 2, peaks, slot=1)
            w.next(S["o_copied"], 4 * NT)
            z_products(do)
            norm_memory(memx)
            merge(1)

            lower(V_MEM, mhi, mlo)
            passed(11)
            memory_attention(X_H, xp, slot=1)
            w.next(S["o_copied"], X_H)
            z_products(xo)
            merge(2)
            mixed(1)

            def feed_forward(gain, loads, more=True):
                nonlocal n, m
                lower(gain, hhi, hlo)
                split(n + 1)
                sg, su = n % 2, (n + 1) % 2
                kg, ku = n // 2, (n + 1) // 2
                pg, pu, mg = m % 2, (m + 1) % 2, m // 2
                r0 = w.at.get(S["ffn_hi"].name, 0)
                with dve.Fori(0, FFT // 2) as i:
                    dve.wait_ge(hi_ready[sg], i + (kg + 2))
                    V_.tensor_tensor(wlo[:, sg], raw[:, sg], whi[:, sg], ALU.subtract).then_inc(lo_ready[sg], 1)
                    dve.wait_ge(pair_free[pg], i + (mg + 1))
                    dve.wait_ge(slot_used[su], i + (ku + 1))
                    V_.tensor_tensor(fa[:, :, :], PS[:, 2 * pu:2 * pu + 2, :], fs[:, :, :], ALU.mult).then_inc(pair_free[pu], 1)
                    dve.wait_ge(pair_free[pu], i + ((m + 1) // 2 + 1))
                    V_.tensor_copy(small[:, 336:337], fa[:, 0, 0:1]).then_inc(S["ffn_a"], 1)
                    dve.wait_ge(S["ffn_hi"], i + (r0 + 1))
                    V_.tensor_tensor(alo[:, bass.ds(i * 2, 2), :], fa[:, :, :], ahi[:, bass.ds(i * 2, 2), :], ALU.subtract)\
                        .then_inc(S["ffn_lo"], 1)
                    dve.wait_ge(hi_ready[su], i + (ku + 2))
                    V_.tensor_tensor(wlo[:, su], raw[:, su], whi[:, su], ALU.subtract).then_inc(lo_ready[su], 1)
                w.at[S["ffn_hi"].name] = r0 + FFT // 2
                n, m = n + FFT, m + FFT
                dve.wait_ge(S["gpost_loaded"], 16 * loads)
                for c in range(4):
                    for r in range(0, FFT, KT):
                        if r + KT >= FFT:
                            take_output(o_ffn, c, PS[:, 4 * ((c + 1) % 2):4 * ((c + 1) % 2) + 4, 0:C], S["ffo_free"])
                        if r + KT < FFT or c < 3:
                            split(n + 2)
                        n += 1
                w.next(S["ffo_free"], 4)
                residual(o_ffn, more)

            dve.wait_ge(S["x_again"], 16)
            residual(o_mix)

            lower(V_MIX0, hhi, hlo)
            split(n + 1)
            norm_memory(memxa)
            V_.memset(lv[:, :, :, ML_DV:ML_DV + 1], 1.0).then_inc(S["ones_ready"], 1)
            passed(2)
            w.next(S["gt_turned"])
            V_.tensor_tensor(lgt, PS[:, 4, 0:32].rearrange("p (t g) -> p t g", t=NT),
                             V[:, V_BG:V_BG + 8].unsqueeze(1).broadcast_to([P, NT, 8]), ALU.add).then_inc(S["gate_soft"], 1)
            w.next(S["gate_abs"])
            V_.tensor_scalar(lgt, lgt, SOFTCAP, None, ALU.mult).then_inc(S["gate_exp"], 1)
            w.next(S["la_exp"])
            V_.scalar_tensor_tensor(lgf, lgt[:, :, 4:8], 0.0, lex, ALU.min, ALU.subtract).then_inc(S["logf_ready"], 1)
            passed()
            w.next(S["cl_psum"])
            for t in range(NT):
                last = V_.tensor_tensor(bi[:, t, t, :], lgt[:, t, 0:4], PS[:, 4, 4 * t:4 * t + 4], ALU.subtract)
            last.then_inc(S["bi_ready"], 1)
            w.next(S["bi_ready"])
            passed()
            w.next(S["lb_ready"])
            for s in range(NT):
                for j in range(s + 1, NT):
                    w.link(V_.tensor_tensor(bi[:, s, j, :], bi[:, s, j - 1, :], Lb[:, :, j * P - 1], ALU.add))
            for h in range(ML_H):
                for s in range(NT):
                    ssl = slice(s * P, s * P + P)
                    last = V_.scalar_tensor_tensor(at[:, s, ssl], Lb[:, h, ssl], bi[:, s, s, h:h + 1], lcm, ALU.add, ALU.add)
                last.then_inc(S["lw_arg"], 1)
                passed()
                w.next(S["lw_exp"])
                w.next(S["lsc_psum"])
                for s in range(NT):
                    last = V_.tensor_tensor(at[:, s, s * P:T], at[:, s, s * P:T], score_bank(s), ALU.mult)
                last.then_inc(S["at_ready"], 1)
                if h == 3:
                    dve.wait_ge(S["gml_loaded"], 16)
                    stored()
                    for t in range(NT):
                        w.link(V_.tensor_tensor(lo[:, t, :], lo[:, t, :], gmb[:, :], ALU.mult))
                passed()
                w.next(S["num_psum"])
                num = PS[:, 6:8, :].rearrange("p b (u c) -> p (b u) c", u=2)
                w.link(V_.tensor_copy(lden.unsqueeze(2), num[:, :, ML_DV:ML_DV + 1]))
                w.link(V_.scalar_tensor_tensor(lden, lden, -1.0, lden, ALU.mult, ALU.max))
                w.link(V_.tensor_scalar(lden, lden, 1.0, None, ALU.max))
                w.link(V_.reciprocal(lden, lden))
                V_.tensor_tensor(hm[:, :, h, :], num[:, :, 0:ML_DV], lden.unsqueeze(2).broadcast_to([P, NT, ML_DV]), ALU.mult)\
                    .then_inc(S["hm_ready"], 1)
            lower(V_MEM0, mhi, mlo)
            w.next(S["hm_root"])
            w.link(V_.reciprocal(rstd16, root[:, 0:16]))
            for t in range(NT):
                for h in range(ML_H):
                    last = V_.scalar_tensor_tensor(hm[:, t, h, :], hm[:, t, h, :], rstd16[:, 4 * t + h:4 * t + h + 1],
                                                   lo[:, t, h * ML_DV:(h + 1) * ML_DV], ALU.mult, ALU.mult)
                last.then_inc(S["hm_done"], 1)
            passed()
            memory_attention(MEM_H, xp2, slot=1)
            for k in range(6):
                w.next(S["y_hi"])
                V_.tensor_tensor(yalo[:, k, :], PS[:, 4 + k % 4, :], yahi[:, k, :], ALU.subtract).then_inc(S["y_lo"], 1)
            output_part(mo, 0, yahi[:, 6:8, :], yalo[:, 6:8, :])
            mixed(2)
            residual(o_mix)
            feed_forward(V_FFN0, 3)

            for ks in (row_order(m)[:2], row_order(m)[2:]):
                lower(V_KV, hhi, hlo, ks)
                lower(V_MIX1, bhi, blo, ks)
            split(n + 1)
            ang, arg, ki, kf = (b_[:, 0, i:i + 128].rearrange("p (t d) -> p t d", t=NT)
                                for b_, i in ((ra, 0), (ra, 128), (rb.bitcast(I32), 0), (rb, 128)))
            dve.wait_ge(S["pos_loaded"], 16)
            w.link(V_.tensor_copy(posf, posi))
            w.link(V_.tensor_tensor(ang, posf.unsqueeze(2).broadcast_to([P, NT, 32]),
                                    inv.unsqueeze(1).broadcast_to([P, NT, 32]), ALU.mult))
            for j in range(2):
                w.link(V_.tensor_scalar(ki, ang, 1.0 / (2 * math.pi), 0.25 * (1 - j), ALU.mult, ALU.add))
                w.link(V_.tensor_copy(kf, ki))
                w.link(V_.scalar_tensor_tensor(arg, kf, -TURN[0], ang, ALU.mult, ALU.add))
                w.link(V_.scalar_tensor_tensor(arg, kf, -TURN[1], arg, ALU.mult, ALU.add))
                w.link(V_.scalar_tensor_tensor(arg, kf, -TURN[2], arg, ALU.mult, ALU.add))
                if j == 0:
                    w.link(V_.tensor_scalar(arg, arg, math.pi / 2, None, ALU.add))
                V_.tensor_scalar(cs[:, j], arg, PI_IN, -PI_IN, ALU.min, ALU.max).then_inc(S["rope_arg"], 1)
                w.next(S["rope_sin"])

            def rotate(src, dst):
                stored()
                w4 = "p t (h a d) -> p t h a d"
                x, y, xc, xs = (b_.rearrange(w4, a=2, d=32) for b_ in (src, dst, ra, rb))
                cos = cs[:, 0].unsqueeze(2).broadcast_to([P, NT, 8, 32])
                sin = cs[:, 1].unsqueeze(2).broadcast_to([P, NT, 4, 32])
                V_.tensor_tensor(ra[:, :, :].rearrange("p t (h d) -> p t h d", d=32), src.rearrange("p t (h d) -> p t h d", d=32),
                                 cos, ALU.mult)
                V_.tensor_tensor(xs[:, :, :, 0, :], x[:, :, :, 1, :], sin, ALU.mult)
                w.link(V_.tensor_tensor(xs[:, :, :, 1, :], x[:, :, :, 0, :], sin, ALU.mult))
                V_.tensor_tensor(y[:, :, :, 0, :], xc[:, :, :, 0, :], xs[:, :, :, 0, :], ALU.subtract)
                V_.tensor_tensor(y[:, :, :, 1, :], xc[:, :, :, 1, :], xs[:, :, :, 1, :], ALU.add).then_inc(S["rope_done"], 1)
                w.next(S["rope_done"])

            passed()
            rotate(sk[:, :, :], skr[:, :, :])
            passed()
            for c in range(3):
                passed()
                rotate(sq[:, c], sqr[:, c])
            norm_memory(memxb)
            passed()
            lower(V_MEM1, mhi, mlo)

            def peaks(h):
                b, ps_ = h % 2, PS[:, logit_banks(h):logit_banks(h) + 2, :].rearrange("p b (u c) -> p (b u) c", u=2)
                V_.memset(slg[:, h % 3, 0, 0:P], NEG)
                V_.tensor_tensor(slg[:, h % 3, 0, P:C], ps_[:, 0, P:C], swa[:, P:C], ALU.add)
                w.link(V_.tensor_tensor(slg[:, h % 3, 1:NT], ps_[:, 1:NT, :], swa.unsqueeze(1).broadcast_to([P, NT - 1, C]), ALU.add))
                w.link(V_.tensor_reduce(nmax[:, b, :], slg[:, h % 3], AX.X, ALU.max, negate=True))
                return V_.tensor_scalar(nmax[:, b, :], nmax[:, b, :], nsink[:, h:h + 1], None, ALU.min)

            attention(SW_H, lambda h: slg[:, h % 3], NT, peaks, sink=True, slot=2)
            memory_attention(MEM_H, xp2, lambda c: output_lower(so, c))
            output_part(mo, 0, yhi[:, 6:8, :], ylo[:, 6:8, :])
            mixed(4)
            residual(o_mix)
            feed_forward(V_FFN1, 5, more=False)

        @block.gpsimd
        def _(pool):
            w = Waits(pool, S["pool_chain"])

            def gain(i):
                if i:
                    pool.wait_ge(S["x_new"], NT * i)
                pool.dma_start(gpost[:, :], gposts[i:i + 1, :].broadcast_to([P, D])).then_inc(S["gpost_loaded"], 16)

            gain(0)
            w.next(S["line_ready"])
            pool.dma_start(bass.AP(line.tensor, 0, [[LINE_HEAD, DSA_H], [LINE + 1, P], [1, 384]]),
                           linet[:, :].unsqueeze(1).broadcast_to([DSA_H, P, 384])).then_inc(S["line_stored"], 16)
            pool.wait_ge(S["line_stored"], 16)
            pool.dma_start(tbias[:, :, :], bass.AP(line.tensor, P - 1, [[LINE, P], [LINE_HEAD, DSA_H], [1, C]]))\
                .then_inc(S["tbias_loaded"], 16)
            for qt in range(1, NT):
                w.next(S["relu_used"], IDX_H)
                diagonal = seen(qt)[:, qt * P:qt * P + P]
                pool.affine_select(out=diagonal, in_=diagonal, pattern=[[-1, P]], compare_op=ALU.is_ge, fill=HIDDEN,
                                   base=0, channel_multiplier=1).then_inc(S["score_masked"], 1)
            w.next(S["o_copied"], 4 * NT)
            pool.dma_start(X[:, :, :], x_in.rearrange("(t p) d -> p t d", p=P)).then_inc(S["x_again"], 16)
            pool.dma_start(memx[:, :, :], mem_in.rearrange("(t p) d -> p t d", p=P)).then_inc(S["mem_loaded"], 16)
            gain(1)
            pool.dma_start(memxa[:, :, :], mem2_in.rearrange("(t p) d -> p t d", p=P)).then_inc(S["mem_loaded"], 16)
            pool.dma_start(gmb[:, :], gmlb.broadcast_to([P, 768])).then_inc(S["gml_loaded"], 16)
            gain(2)
            gain(3)
            w.next(S["rope_turned"])
            pool.dma_start(memxb[:, :, :], mem2_in.rearrange("(t p) d -> p t d", p=P)).then_inc(S["mem_loaded"], 16)
            gain(4)

        @block.sync
        def _(sp):
            for t in range(NT):
                sp.dma_start(X[:, t, :], x_in[t * P:t * P + P, :]).then_inc(S[f"x_loaded{t}"], 16)
                if t == 0:
                    sp.dma_start(V[:, :], cols).then_inc(S["vectors_loaded"], 16)
                    sp.dma_start(K[:, 0:P], consts[:, 0:P]).then_inc(S["ident_loaded"], 16)
            for p in range(2):
                sp.dma_start(raw[:, p], stream[0, p]).then_inc(raw_ready[p], 16)
            sp.dma_start(K[:, P:K_ALL], consts[:, P:K_ALL]).then_inc(S["tables_loaded"], 16)
            sp.dma_start(wup_s[:, :], wup[0:GLA_RANK, :]).then_inc(S["gate_w_loaded"], 16)
            sp.dma_start(ba_s[:, :], wup[GLA_RANK:GLA_RANK + 1, :]).then_inc(S["gate_w_loaded"], 16)
            sp.dma_start(posi, pos_in).then_inc(S["pos_loaded"], 16)
            with sp.Fori(1, NS // 2) as i:
                for p in range(2):
                    sp.wait_ge(lo_ready[p], i)
                    sp.dma_start(raw[:, p], stream[bass.ds(i, 1), p]).then_inc(raw_ready[p], 16)
            if NS % 2:
                sp.wait_ge(lo_ready[0], NS // 2)
                sp.dma_start(raw[:, 0], stream[NS // 2, 0]).then_inc(raw_ready[0], 16)
            for t in range(NT):
                sp.wait_ge(S["x_new"], NT * 4 + t + 1)
                sp.dma_start(out[t * P:t * P + P, :], X[:, t, :]).then_inc(S["out_stored"], 16)
            sp.wait_ge(S["out_stored"], 16 * NT)



def t5_bucket(distance):
    exact = BUCKETS // 2
    if distance < exact:
        return max(distance, 0)
    return min(exact + int(math.log(distance / exact) / math.log(MAX_DIST / exact) * (BUCKETS - exact)), BUCKETS - 1)


def constants():
    a, b = np.arange(P)[:, None], np.arange(P)[None, :]
    k = np.zeros((P, K_ALL), np.float32)
    k[:, K_ID:K_ID + P] = a == b
    k[:, K_U64:K_U64 + P] = (a <= b) & (a // 64 == b // 64)
    k[:, K_U128:K_U128 + P] = a <= b
    k[:, K_ONE:K_ONE + P] = 1.0
    d = a + P - np.arange(C)[None, :]
    k[:, K_SWA:K_SWA + C] = np.where((d >= 0) & (d < P), 0.0, NEG)
    k[:, K_DCM:K_DCM + P] = np.where(b <= a, 0.0, NEG)
    k[:, K_LCM:K_LCM + P] = np.where(b >= a, 0.0, NEG)
    for i in range(384):
        k[t5_bucket(255 - i), K_HOT + i] += 1.0
        k[BUCKETS - 1, K_HOT + i] -= 1.0
    k[:, K_INV:K_INV + 32] = np.float32(1.0) / np.float32(10000.0) ** (np.arange(0, 64, 2, dtype=np.float32) / np.float32(64))
    return k


def kernel(**inputs):
    import concourse.bacc as bacc
    from concourse.bass_utils import run_bass_kernel_spmd

    a = {name: np.asarray(v) for name, v in inputs.items()}
    weights = {name: a[name][0] for name in
               ("w_in", "w_gla_out", "w_dsa_out", "w_x_out", "w_mem_kv", "w_o")}
    weights |= {"w_in_a": a["w_in_a_2"][0], "w_in_b": a["w_in_b_2"][0], "w_kv": a["w_kv_2"]}
    for layer in range(2):
        for name in ("w_mem_kv", "w_out", "w_ffn_in", "w_ffn_out"):
            weights[f"{name}_{layer}"] = a[f"{name}_2"][layer]
    stream = np.zeros((2 * -(-NS // 2), P, KT, C), np.float32)
    for s, pieces in enumerate(slots()):
        for name, row, tiles, column, width, place in pieces:
            w = weights[name][row * P:(row + tiles) * P, column:column + width]
            stream[s, :, 0:tiles, place:place + width] = w.reshape(tiles, P, width).transpose(1, 0, 2)

    cols = np.zeros((P, V_COLS), np.float32)
    for at, v in ((V_PRE, a["g_pre"][0]), (V_MEM, a["g_mem"][0]), (V_GLA, a["g_gla"][0]),
                  (V_MIX0, a["g_mix_pre_2"][0]), (V_FFN0, a["g_ffn_pre_2"][0]), (V_KV, a["g_kv_2"]),
                  (V_MIX1, a["g_mix_pre_2"][1]), (V_FFN1, a["g_ffn_pre_2"][1]),
                  (V_MEM0, a["g_mem_2"][0]), (V_MEM1, a["g_mem_2"][1])):
        cols[:, at:at + v.size // P] = v.reshape(-1, P).T
    cols[:, V_BG:V_BG + 8] = a["b_gates_a_2"][0]
    cols[:, V_SINK:V_SINK + SW_H] = a["sinks_b_2"][0]
    cols[0:BUCKETS, V_ALL:V_COLS] = a["rel_bias"]
    cols[:, V_EPS] = EPS

    arrays = {
        "stream": stream.reshape(-1, 2, P, KT * C),
        "x": a["x"][0], "mem": a["mem"][0], "mem2": a["mem_2"][0],
        "consts": constants(), "cols": cols,
        "gposts": np.stack([a["g_post"][0], a["g_mix_post_2"][0], a["g_ffn_post_2"][0],
                            a["g_mix_post_2"][1], a["g_ffn_post_2"][1]]),
        "wup": np.concatenate([a["w_gla_a_up"][0], a["b_gla_a"]]),
        "gml": a["g_mlstm_out_2"],
        "positions": np.ascontiguousarray(a["positions_2"].reshape(NT, P).T),
    }
    arrays = {name: np.ascontiguousarray(v) for name, v in arrays.items()}
    nc = bacc.Bacc("TRN2", target_bir_lowering=False, num_devices=1)
    t = {name: nc.dram_tensor(f"in_{name}", v.shape, mybir.dt.from_np(v.dtype), kind="ExternalInput").ap()
         for name, v in arrays.items()}
    line = nc.dram_tensor("bias_line", (DSA_H, LINE_HEAD), F32, kind="Internal").ap()
    out = nc.dram_tensor("out", (T, D), F32, kind="ExternalOutput").ap()
    build(nc, t["stream"], t["x"], t["mem"], t["mem2"], t["consts"], t["cols"], t["gposts"], t["wup"], t["gml"],
          t["positions"], line, out)
    r = run_bass_kernel_spmd(nc, [{f"in_{name}": v for name, v in arrays.items()}], core_ids=[0])
    return r.results[0]["out"].reshape(1, T, D)
```
